# Optimizing a Trainium2 kernel written in Bass

```python
import math
import jax
import jax.numpy as jnp
from jax import lax
import numpy as np

D_MODEL = 1024
BATCH = 1
SEQ = 256
DEPTH = 2

RMS_EPS = 1e-6
ROPE_THETA = 500000.0
Q_BLOCK = 128
A_HEADS = 8
A_KV_HEADS = 2
A_HEAD_DIM = 64
A_ROT = A_HEAD_DIM // 4
IDX_HEADS = 8
IDX_DIM = 32
IDX_ROT = IDX_DIM // 4
IDX_TOPK_MAX = 256
SC_W = 512
SC_KERNEL = 3
GM_W = 512
GM_GROUPS = 4
GM_GROUP_W = GM_W // GM_GROUPS
GM_CHUNK = 128
M_DINNER = 512
M_HEAD_DIM = 64
M_HEADS = M_DINNER // M_HEAD_DIM
M_GROUPS = 2
M_STATE = 64
M_CONV = 4
M_CHUNK = 128
M_BC = M_GROUPS * M_STATE
M_XBC = M_DINNER + 2 * M_BC
N_BRANCH = 4
BRANCH_W = 512
N_EXPERTS = 16
N_EXPERT_GROUPS = 4
EXPERTS_PER_GROUP = N_EXPERTS // N_EXPERT_GROUPS
TOP_K = 2
D_FF_EXPERT = 512

A_Q = A_HEADS * A_HEAD_DIM
A_KV = A_KV_HEADS * A_HEAD_DIM
IDX_Q = IDX_HEADS * IDX_DIM
IN_SPLITS = (A_Q, A_KV, A_KV, IDX_Q, IDX_DIM, IDX_HEADS,
             SC_W, SC_W, SC_W,
             2 * GM_W,
             M_DINNER, M_XBC, M_HEADS,
             N_BRANCH * D_MODEL)
IN_COLS = sum(IN_SPLITS)

kernel_name = "hybrid_dsa_conv_gmlp_ssd_moe"

def rms_norm(x, g):
    xf = x.astype(jnp.float32)
    y = xf * lax.rsqrt(jnp.mean(xf * xf, axis=-1, keepdims=True) + RMS_EPS)
    return y.astype(x.dtype) * g

def partial_rope(x, positions, rot_dim):
    half = rot_dim // 2
    inv_freq = jnp.exp(-math.log(ROPE_THETA) * jnp.arange(half, dtype=jnp.float32) * 2.0 / rot_dim)
    ang = positions.astype(jnp.float32)[..., None] * inv_freq
    cos = jnp.cos(ang)[:, :, None, :].astype(x.dtype)
    sin = jnp.sin(ang)[:, :, None, :].astype(x.dtype)
    x1 = x[..., :half]
    x2 = x[..., half:rot_dim]
    return jnp.concatenate([x1 * cos - x2 * sin, x2 * cos + x1 * sin, x[..., rot_dim:]], axis=-1)

def causal_depthwise_conv(u, w):
    k_w, ch = w.shape
    return lax.conv_general_dilated(
        u, w[:, None, :].astype(u.dtype), window_strides=(1,), padding=[(k_w - 1, 0)],
        dimension_numbers=('NWC', 'WIO', 'NWC'), feature_group_count=ch)

def dsa_attention(q, k, v, qi, ki, wi):
    bsz, seq = q.shape[0], q.shape[1]
    topk = min(IDX_TOPK_MAX, seq // 4)
    nb = seq // Q_BLOCK
    rep = A_HEADS // A_KV_HEADS
    key_pos = jnp.arange(seq, dtype=jnp.int32)

    def to_blocks(a):
        return jnp.moveaxis(a.reshape((bsz, nb, Q_BLOCK) + a.shape[2:]), 1, 0)

    def one_block(args):
        qb, qib, wib, start = args
        q_pos = start + jnp.arange(Q_BLOCK, dtype=jnp.int32)
        causal = key_pos[None, :] <= q_pos[:, None]
        dots = jnp.einsum('bthd,bsd->bths', qib, ki).astype(jnp.float32) * (IDX_DIM ** -0.5)
        idx_score = jnp.einsum('bths,bth->bts', jax.nn.relu(dots), wib.astype(jnp.float32))
        idx_score = jnp.where(causal[None], idx_score, -jnp.inf)
        _, sel = lax.top_k(idx_score, topk)
        kg = jax.vmap(lambda kk, ii: kk[ii])(k, sel)
        vg = jax.vmap(lambda vv, ii: vv[ii])(v, sel)
        valid = sel <= q_pos[None, :, None]
        qg = qb.reshape(bsz, Q_BLOCK, A_KV_HEADS, rep, A_HEAD_DIM)
        logits = jnp.einsum('btgrd,btkgd->btgrk', qg, kg).astype(jnp.float32) * (A_HEAD_DIM ** -0.5)
        logits = jnp.where(valid[:, :, None, None, :], logits, -jnp.inf)
        p = jax.nn.softmax(logits, axis=-1).astype(vg.dtype)
        o = jnp.einsum('btgrk,btkgd->btgrd', p, vg)
        return o.reshape(bsz, Q_BLOCK, A_Q)

    starts = jnp.arange(nb, dtype=jnp.int32) * Q_BLOCK
    out = lax.map(one_block, (to_blocks(q), to_blocks(qi), to_blocks(wi), starts))
    return jnp.moveaxis(out, 0, 1).reshape(bsz, seq, A_Q)

def ssd_scan(xs, dt, a_coef, bm, cm):
    bsz, seq, nh, hp = xs.shape
    nc = seq // M_CHUNK
    rep = nh // bm.shape[2]
    bh = jnp.repeat(bm, rep, axis=2).reshape(bsz, nc, M_CHUNK, nh, M_STATE)
    ch = jnp.repeat(cm, rep, axis=2).reshape(bsz, nc, M_CHUNK, nh, M_STATE)
    xdt = (xs * dt[..., None]).reshape(bsz, nc, M_CHUNK, nh, hp)
    acs = jnp.cumsum((dt * a_coef).reshape(bsz, nc, M_CHUNK, nh), axis=2)
    acs_h = jnp.swapaxes(acs, 2, 3)
    diff = acs_h[..., :, None] - acs_h[..., None, :]
    tri = jnp.tril(jnp.ones((M_CHUNK, M_CHUNK), dtype=bool))
    decay = jnp.exp(jnp.where(tri, diff, -jnp.inf))
    scores = jnp.einsum('bclhn,bcshn->bchls', ch, bh) * decay
    y_diag = jnp.einsum('bchls,bcshp->bclhp', scores, xdt)
    decay_states = jnp.exp(acs[:, :, -1:, :] - acs)
    states = jnp.einsum('bclhn,bclh,bclhp->bchpn', bh, decay_states, xdt)
    chunk_decay = jnp.exp(acs[:, :, -1, :])

    def step(carry, inp):
        st, dec = inp
        return carry * dec[..., None, None] + st, carry

    init = jnp.zeros((bsz, nh, hp, M_STATE), dtype=states.dtype)
    _, prev = lax.scan(step, init, (jnp.moveaxis(states, 1, 0), jnp.moveaxis(chunk_decay, 1, 0)))
    prev = jnp.moveaxis(prev, 0, 1)
    y_off = jnp.einsum('bclhn,bchpn,bclh->bclhp', ch, prev, jnp.exp(acs))
    return (y_diag + y_off).reshape(bsz, seq, nh, hp).astype(xs.dtype)

def hybrid_mixer(h, positions, w_in, q_norm_g, k_norm_g, sc_conv_w, g_v_norm_g, g_spatial_w,
                 g_spatial_b, m_conv_w, m_conv_b, m_dt_bias, m_a_log, m_d, m_norm_g, w_branch, w_out):
    bsz, seq, _ = h.shape
    points = [int(p) for p in np.cumsum(IN_SPLITS)[:-1]]
    proj = h @ w_in
    (q, k, v, qi, ki, wi, sc_b, sc_c, sc_x, g_uv, m_z, m_xbc, m_dt, gates) = jnp.split(proj, points, axis=-1)

    q = partial_rope(rms_norm(q.reshape(bsz, seq, A_HEADS, A_HEAD_DIM), q_norm_g), positions, A_ROT)
    k = partial_rope(rms_norm(k.reshape(bsz, seq, A_KV_HEADS, A_HEAD_DIM), k_norm_g), positions, A_ROT)
    v = v.reshape(bsz, seq, A_KV_HEADS, A_HEAD_DIM)
    qi = partial_rope(qi.reshape(bsz, seq, IDX_HEADS, IDX_DIM), positions, IDX_ROT)
    ki = partial_rope(ki.reshape(bsz, seq, 1, IDX_DIM), positions, IDX_ROT)[:, :, 0]
    wi = wi * (IDX_HEADS ** -0.5)
    o_a = dsa_attention(q, k, v, qi, ki, wi)

    o_b = sc_b * causal_depthwise_conv(sc_c * sc_x, sc_conv_w)

    g_uv = jax.nn.gelu(g_uv, approximate=False)
    u, gv = jnp.split(g_uv, 2, axis=-1)
    gv = rms_norm(gv, g_v_norm_g)
    vb = gv.reshape(bsz, seq // GM_CHUNK, GM_CHUNK, GM_GROUPS, GM_GROUP_W)
    tri = jnp.tril(jnp.ones((GM_CHUNK, GM_CHUNK), dtype=bool))
    ws = jnp.where(tri[None], g_spatial_w, 0.0).astype(vb.dtype)
    mixed = jnp.einsum('gts,bcsgd->bctgd', ws, vb) + g_spatial_b.T[None, None, :, :, None]
    o_c = u * mixed.reshape(bsz, seq, GM_W)

    xbc = jax.nn.silu(causal_depthwise_conv(m_xbc, m_conv_w) + m_conv_b)
    xs, bm, cm = jnp.split(xbc, [M_DINNER, M_DINNER + M_BC], axis=-1)
    xs = xs.reshape(bsz, seq, M_HEADS, M_HEAD_DIM)
    bm = bm.reshape(bsz, seq, M_GROUPS, M_STATE)
    cm = cm.reshape(bsz, seq, M_GROUPS, M_STATE)
    dt = jax.nn.softplus(m_dt.astype(jnp.float32) + m_dt_bias.astype(jnp.float32))
    a_coef = -jnp.exp(m_a_log.astype(jnp.float32))
    y = ssd_scan(xs, dt, a_coef, bm, cm) + m_d[:, None] * xs
    o_d = rms_norm(y.reshape(bsz, seq, M_DINNER) * jax.nn.silu(m_z), m_norm_g)

    gates = jax.nn.sigmoid(gates.reshape(bsz, seq, N_BRANCH, D_MODEL))
    branches = (o_a, o_b, o_c, o_d)
    merged = gates[:, :, 0] * (branches[0] @ w_branch[0])
    for i in range(1, N_BRANCH):
        merged = merged + gates[:, :, i] * (branches[i] @ w_branch[i])
    return merged @ w_out

def grouped_moe(h, router_w, router_bias, w_gate, w_up, w_down):
    bsz, seq, dm = h.shape
    t = h.reshape(-1, dm)
    ntok = t.shape[0]
    scores = jax.nn.sigmoid((t @ router_w).astype(jnp.float32))
    sel = scores + router_bias.astype(jnp.float32)
    grp_score = lax.top_k(sel.reshape(ntok, N_EXPERT_GROUPS, EXPERTS_PER_GROUP), 2)[0].sum(-1)
    best = jnp.argmax(grp_score, axis=-1)
    in_grp = (jnp.arange(N_EXPERTS) // EXPERTS_PER_GROUP)[None, :] == best[:, None]
    _, idx = lax.top_k(jnp.where(in_grp, sel, -jnp.inf), TOP_K)
    wts = jnp.take_along_axis(scores, idx, axis=-1)
    wts = wts / jnp.sum(wts, axis=-1, keepdims=True)
    combine = jnp.sum(jax.nn.one_hot(idx, N_EXPERTS, dtype=jnp.float32) * wts[..., None], axis=1).astype(t.dtype)
    out = jnp.zeros_like(t)
    for e in range(N_EXPERTS):
        hid = jax.nn.silu(t @ w_gate[e]) * (t @ w_up[e])
        out = out + combine[:, e:e + 1] * (hid @ w_down[e])
    return out.reshape(bsz, seq, dm)

def setup_inputs(seed: int = 0) -> dict:
    key = jax.random.key(seed)
    ks = iter(jax.random.split(key, 32))

    def nrm(shape, scale):
        return jax.random.normal(next(ks), shape, jnp.float32) * scale

    L, D = DEPTH, D_MODEL
    x = nrm((BATCH, SEQ, D), 1.0)
    c = nrm((BATCH, D), 1.0)
    positions = jnp.tile(jnp.arange(SEQ, dtype=jnp.int32)[None, :], (BATCH, 1))
    ada_w = nrm((L, D, 6 * D), 0.5 * D ** -0.5)
    ada_b = nrm((L, 6 * D), 0.01)
    norm1_g = 1.0 + nrm((L, D), 0.01)
    w_in = nrm((L, D, IN_COLS), D ** -0.5)
    q_norm_g = 1.0 + nrm((L, A_HEAD_DIM), 0.01)
    k_norm_g = 1.0 + nrm((L, A_HEAD_DIM), 0.01)
    sc_conv_w = nrm((L, SC_KERNEL, SC_W), SC_KERNEL ** -0.5)
    g_v_norm_g = 1.0 + nrm((L, GM_W), 0.01)
    g_spatial_w = nrm((L, GM_GROUPS, GM_CHUNK, GM_CHUNK), GM_CHUNK ** -0.5)
    g_spatial_b = 1.0 + nrm((L, GM_GROUPS, GM_CHUNK), 0.01)
    m_conv_w = nrm((L, M_CONV, M_XBC), M_CONV ** -0.5)
    m_conv_b = nrm((L, M_XBC), 0.01)
    dt0 = jnp.exp(jax.random.uniform(next(ks), (L, M_HEADS), jnp.float32, math.log(1e-3), math.log(1e-1)))
    m_dt_bias = dt0 + jnp.log(-jnp.expm1(-dt0))
    m_a_log = jnp.log(jax.random.uniform(next(ks), (L, M_HEADS), jnp.float32, 1.0, 16.0))
    m_d = 1.0 + nrm((L, M_HEADS), 0.01)
    m_norm_g = 1.0 + nrm((L, M_DINNER), 0.01)
    w_branch = nrm((L, N_BRANCH, BRANCH_W, D), BRANCH_W ** -0.5)
    w_out = nrm((L, D, D), D ** -0.5)
    norm2_g = 1.0 + nrm((L, D), 0.01)
    router_w = nrm((D, N_EXPERTS), D ** -0.5)
    router_bias = nrm((N_EXPERTS,), 0.01)
    exp_w_gate = nrm((L, N_EXPERTS, D, D_FF_EXPERT), D ** -0.5)
    exp_w_up = nrm((L, N_EXPERTS, D, D_FF_EXPERT), D ** -0.5)
    exp_w_down = nrm((L, N_EXPERTS, D_FF_EXPERT, D), D_FF_EXPERT ** -0.5)
    return {"x": x, "c": c, "positions": positions, "ada_w": ada_w, "ada_b": ada_b,
            "norm1_g": norm1_g, "w_in": w_in, "q_norm_g": q_norm_g, "k_norm_g": k_norm_g,
            "sc_conv_w": sc_conv_w, "g_v_norm_g": g_v_norm_g, "g_spatial_w": g_spatial_w,
            "g_spatial_b": g_spatial_b, "m_conv_w": m_conv_w, "m_conv_b": m_conv_b,
            "m_dt_bias": m_dt_bias, "m_a_log": m_a_log, "m_d": m_d, "m_norm_g": m_norm_g,
            "w_branch": w_branch, "w_out": w_out, "norm2_g": norm2_g, "router_w": router_w,
            "router_bias": router_bias, "exp_w_gate": exp_w_gate, "exp_w_up": exp_w_up,
            "exp_w_down": exp_w_down}

def reference(x, c, positions, ada_w, ada_b, norm1_g, w_in, q_norm_g, k_norm_g, sc_conv_w,
              g_v_norm_g, g_spatial_w, g_spatial_b, m_conv_w, m_conv_b, m_dt_bias, m_a_log, m_d,
              m_norm_g, w_branch, w_out, norm2_g, router_w, router_bias, exp_w_gate, exp_w_up,
              exp_w_down):
    c_act = jax.nn.silu(c)
    for l in range(DEPTH):
        mod = c_act @ ada_w[l] + ada_b[l]
        shift1, scale1, gate1, shift2, scale2, gate2 = jnp.split(mod, 6, axis=-1)
        h = rms_norm(x, norm1_g[l]) * (1.0 + scale1[:, None, :]) + shift1[:, None, :]
        mix = hybrid_mixer(h, positions, w_in[l], q_norm_g[l], k_norm_g[l], sc_conv_w[l],
                           g_v_norm_g[l], g_spatial_w[l], g_spatial_b[l], m_conv_w[l], m_conv_b[l],
                           m_dt_bias[l], m_a_log[l], m_d[l], m_norm_g[l], w_branch[l], w_out[l])
        x = x + gate1[:, None, :] * mix
        h = rms_norm(x, norm2_g[l]) * (1.0 + scale2[:, None, :]) + shift2[:, None, :]
        x = x + gate2[:, None, :] * grouped_moe(h, router_w, router_bias, exp_w_gate[l],
                                                exp_w_up[l], exp_w_down[l])
    return x


_drawn_inputs = setup_inputs


def setup_inputs(seed=0):
    import zlib

    import numpy as np

    out = dict(_drawn_inputs(seed))
    spreads = {}
    factors = {'q_norm_g': 15.886,
     'k_norm_g': 14.658,
     'g_v_norm_g': 24.114,
     'g_spatial_b': 16.145,
     'm_conv_b': 3.471,
     'm_d': 28.703,
     'm_norm_g': 10.587,
     'norm2_g': 2.782}
    for name, (base, spread) in spreads.items():
        noise = np.random.default_rng([zlib.crc32(name.encode()), seed]).standard_normal(out[name].shape)
        drawn = base * np.exp(spread * noise) if base else spread * noise
        out[name] = jnp.asarray(drawn.astype(out[name].dtype))
    for name, factor in factors.items():
        out[name] = (out[name] * factor).astype(out[name].dtype)
    return out
```

```python
import math
from contextlib import ExitStack

import numpy as np

import concourse.bass as bass
from concourse import mybir

F32 = mybir.dt.float32
I32 = mybir.dt.int32
ALU = mybir.AluOpType
ACT = mybir.ActivationFunctionType
AX_X = mybir.AxisListType.X

P = 128
D_MODEL, SEQ, DEPTH = 1024, 256, 2
TT = SEQ // P
KD = D_MODEL // P
W = 512
HK = KD // 2
EPS = 1e-6
ROPE_THETA = 500000.0
AH, AG, AD, AROT = 8, 2, 64, 16
IH, ID, IROT = 8, 32, 8
TOPK = 64
SC_K, M_K = 3, 4
GG, MH, MP, MG, MN = 4, 8, 64, 2, 64
NE, EG, EPG, FF = 16, 4, 4, 512
CT = W // P
NB = 4

CQ, CK, CV, CQI, CKI, CWI = 0, 512, 640, 768, 1024, 1056
CSB, CSC, CSX, CGU, CGV, CZ, CXBC, CDT, CG = 1064, 1576, 2088, 2600, 3112, 3624, 4136, 4904, 4912
SMALL = AG * AD * 2 + ID + IH + MH
BRANCH_ORDER = (1, 2, 0, 3)

PR = {}
PROWS = 0
for _name, _n in (("norm1", KD), ("norm2", KD), ("adab", 6 * KD), ("scw", SC_K * CT), ("gvg", CT),
                  ("mcw", M_K * 6), ("mcb", 6), ("mng", CT), ("c", KD)):
    PR[_name] = PROWS
    PROWS += _n

BIG = 1e30
FILLS = 5 + AROT // 2 + NE + 5
TAKEN = -3e38

RING = 6
UNITS = [(n, h) for n in ("C", "B", "A", "xbc", "gv", "z", "gu", "scc", "scx", "scb") for h in range(2)]
for _i in BRANCH_ORDER:
    for _j in range(2):
        UNITS += [(f"g{_i}{_j}", 0), (f"g{_i}{_j}", 1), (f"b{_i}{_j}", 0)]
UNITS += [("o0", 0), ("o0", 1), ("o1", 0), ("o1", 1)]
MOE0 = len(UNITS)
PER_E = 6
UNITS_L = MOE0 + NE * PER_E
assert MOE0 % RING == 0 and PER_E == RING
PARTS = [3 if n == "B" else 2 if n == "C" or n[:2] == "b0" else 1 for n, _ in UNITS]
LANDED = [sum(PARTS[m] for m in range(n % RING, n + 1, RING)) for n in range(MOE0)]
SLOT_MIX = [sum(PARTS[m] for m in range(s, MOE0, RING)) for s in range(RING)]
SLOT_L = [SLOT_MIX[s] + NE for s in range(RING)]

PROJ_JOBS = ["C", "B", "A", "xbc", "gv", "z", "gu", "scc", "scx", "scb"]
PROJ_JOBS += [f"g{i}{j}" for i in BRANCH_ORDER for j in range(2)]
S_JOBS = ["h1_0", "h1_1", "qiT", "kiT"]
S_JOBS += [f"dot{t}{g}{u}" for t in range(TT) for g in range(2) for u in range(2)]
S_JOBS += ["qT0", "qT1", "kT", "xs0", "xs1", "Bt"]
S_JOBS += [x for i in range(4) for x in (f"PT{i}a", f"PT{i}b", f"PV{i}")]
S_JOBS += ["scT", "states", "odT0", "odT1", "mT0", "mT1", "mT2", "mT3", "h2_0", "h2_1"]
V_JOBS = ["modA", "h1_2", "h1_3", "wsT"]
V_JOBS += [f"lg{t}{i}" for t in range(TT) for i in range(4)]
V_JOBS += ["acs", "ab00", "ab01", "y0", "ab10", "ab11", "yoff", "y1", "mix0", "mix1"]
V_JOBS += [f"b{i}{j}{t}" for i in BRANCH_ORDER for j in range(2) for t in range(TT)]
V_JOBS += ["gate10", "gate11", "modB", "gate20", "gate21"]
V_JOBS += [f"o{j}{t}" for j in range(2) for t in range(TT)]
V_JOBS += ["h2_2", "h2_3", "router", "pad"]
PCOL = "pcol"
V_JOBS = [PCOL] + V_JOBS
if len(V_JOBS) % 2:
    V_JOBS.remove("pad")
assert len(PROJ_JOBS) % 2 == 0 and len(S_JOBS) % 2 == 0 and len(V_JOBS) % 2 == 0
BY_UNIT = {f"b{i}{j}1": UNITS.index((f"b{i}{j}", 0)) for i in BRANCH_ORDER for j in range(2)}
BY_UNIT |= {f"o{j}{t}": UNITS.index((f"o{j}", 1)) for j in range(2) for t in range(TT)}
BY_CHUNK = {"modA": 3, "gate10": 4, "gate11": 5, "modB": 9, "gate20": 10, "gate21": 11}
V_PLAIN = [n for n in V_JOBS if n not in BY_UNIT and n not in BY_CHUNK and n != "pad"]
NVR = len(V_PLAIN)
NPJ, NSJ, NVJ = len(PROJ_JOBS), len(S_JOBS), len(V_JOBS)
MOD_CHUNKS = 6 * D_MODEL // W
ADA_U = MOD_CHUNKS * 4


def bcast(ap, axis, n):
    a = ap.unsqueeze(axis)
    shape = list(a.shape)
    shape[axis] = n
    return a.to_broadcast(shape)


def hybrid_trunk(nc, x, c, positions, ada_w, ada_b, norm1_g, w_in, q_norm_g, k_norm_g, sc_conv_w,
                 g_v_norm_g, g_spatial_w, g_spatial_b, m_conv_w, m_conv_b, m_dt_bias, m_a_log, m_d,
                 m_norm_g, w_branch, w_out, norm2_g, router_w, router_bias, exp_w_gate, exp_w_up,
                 exp_w_down, out):
    ctx = ExitStack()
    with ctx:
        def sb(name, shape, dt=F32):
            return ctx.enter_context(nc.sbuf_tensor(name, [P] + shape, dt))

        def sem(name):
            return ctx.enter_context(nc.semaphore(name))

        bank = ctx.enter_context(nc.psum_tensor("bank", [P, 8, W], F32))

        ring = sb("ring", [RING, HK, W])
        ada_buf = sb("ada_buf", [2, 2, W])
        x_sb = sb("x_sb", [TT, D_MODEL])
        hT = sb("hT", [KD, SEQ])
        scratch = sb("scratch", [TT * D_MODEL])
        merged = scratch[:, :].rearrange("p (t d) -> p t d", t=TT)
        gate_bc = sb("gate_bc", [2, D_MODEL])
        ada_acc = sb("ada_acc", [2, W])
        ident = sb("ident", [P])
        tri = sb("tri", [P])
        late = sb("late", [P])
        future = sb("future", [SEQ])
        ones = sb("ones", [P])
        invf = sb("invf", [AROT // 2])
        prow = sb("prow", [P])
        pcol = sb("pcol", [P])
        cact = sb("cact", [KD])
        gain = sb("gain", [2, AD])
        mrow = sb("mrow", [3, MH])
        gsb = sb("gsb", [GG, P])
        rbias = sb("rbias", [NE])
        rw = sb("rw", [KD, NE])
        wsraw = sb("wsraw", [GG, P])
        wsT = sb("wsT", [GG, P])
        pos_i = sb("pos_i", [TT], I32)
        pos_f = sb("pos_f", [TT])
        rope = sb("rope", [2, TT, AROT // 2])
        ang = sb("ang", [2, TT, AROT // 2])
        turns = sb("turns", [2, TT, AROT // 2])
        st = sb("st", [21, 32])
        modc = sb("modc", [2, 2, KD])
        qk = sb("qk", [TT, AH + AG, AD])
        xs_tok = qk[:, :, :, :].rearrange("p t h d -> p (t h d)")[:, 0:TT * W].rearrange(
            "p (t d) -> p t d", t=TT)
        qik = sb("qik", [TT, IH + 1, ID])
        kirep = sb("kirep", [TT, 4, ID])
        wdt = sb("wdt", [TT, IH + MH])
        v_sb = sb("v_sb", [TT, AG * AD])
        qiT = sb("qiT", [2, SEQ])
        bd_qt = sb("bd_qt", [2, 4, SEQ])
        kiTd = bd_qt[:, 0, :, :]
        qT = bd_qt[:, 1, :, :]
        kTd = sb("kTd", [AG, SEQ])
        score = sb("score", [3 * P])
        top8 = sb("top8", [TT, 8])
        mask = sb("mask", [3 * P])
        P_sb = sb("P_sb", [AH, 3 * P])
        p_flat = P_sb[:, :, :].rearrange("p h s -> p (h s)")
        M_sb = p_flat[:, 0:1024].rearrange("p (h l) -> p h l", h=MH)
        y_sb = p_flat[:, 1024:2048].rearrange("p (t d) -> p t d", t=TT)
        xdt = p_flat[:, 2048:3072].rearrange("p (t d) -> p t d", t=TT)
        PT = sb("PT", [AH * 3 * P + 8])
        scc = PT[:, 0:CT * SEQ].rearrange("p (m s) -> p m s", m=CT)
        cx = PT[:, CT * SEQ:CT * SEQ + CT * (SEQ + 2)].rearrange("p (m s) -> p m s", m=CT)
        scb = PT[:, CT * (2 * SEQ + 2):CT * (3 * SEQ + 2)].rearrange("p (m s) -> p m s", m=CT)
        oT = sb("oT", [NB, CT, SEQ])
        xbc = sb("xbc", [6, SEQ + M_K - 1])
        xbcT = sb("xbcT", [6, SEQ])
        Btok = sb("Btok", [P])
        CTd = sb("CTd", [MG, SEQ])
        dtA = sb("dtA", [4, TT, MH])
        acs = sb("acs", [2, TT, MH])
        xdtd = sb("xdtd", [W])
        z_sb = sb("z_sb", [TT, W])
        rt = z_sb[:, :, :].rearrange("p t d -> p (t d)")[:, 0:4 * TT * (AH + AG) * AROT // 2].rearrange(
            "p (i h f) -> p i h f", i=4, f=AROT // 2)
        prevd = sb("prevd", [W])
        scT = sb("scT", [TT, MG, P])
        uT = sb("uT", [CT, SEQ])
        gv = sb("gv", [TT, W])
        gsig = [qT.rearrange("p i s -> p (i s)").rearrange("p (t n) -> p t n", t=TT), gv[:, :, :]]
        rt1 = sb("rt1", [7, TT, NE])
        comb = sb("comb", [TT, NE])
        cw = sb("cw", [TT])
        rank = sb("rank", [NE])
        sg = p_flat[:, 0:1024].rearrange("p (m s) -> p m s", m=CT)
        hid = p_flat[:, 1024:2048].rearrange("p (m s) -> p m s", m=CT)

        slot_loaded = [sem(f"slot_loaded{s}") for s in range(RING)]
        units_read = sem("units_read")
        unit_turn = sem("unit_turn")
        ada_loaded = [sem(f"ada_loaded{s}") for s in range(2)]
        ada_freed = sem("ada_freed")
        acc_ready, acc_used = sem("acc_ready"), sem("acc_used")
        proj_evac = sem("proj_evac")
        s_ready, s_evac = sem("s_ready"), sem("s_evac")
        v_ready, v_evac = sem("v_ready"), sem("v_evac")
        consts, x_in, pos_in, rw_in = sem("consts"), sem("x_in"), sem("pos_in"), sem("rw_in")
        prow_in, wsraw_in, rows_in, gateb_in = sem("prow_in"), sem("wsraw_in"), sem("rows_in"), sem("gateb_in")
        dve_step, moe_step, CTd_ready = sem("dve_step"), sem("moe_step"), sem("CTd_ready")
        angles_ready, rope_ready = sem("angles_ready"), sem("rope_ready")
        pcol_ready, cact_ready = sem("pcol_ready"), sem("cact_ready")
        ss_ready, mean_ready, rs_ready = sem("ss_ready"), sem("mean_ready"), sem("rs_ready")
        xn_ready, modc_ready = sem("xn_ready"), sem("modc_ready")
        idx_rope, qk_ss, qk_rs, qk_roped = sem("idx_rope"), sem("qk_ss"), sem("qk_rs"), sem("qk_roped")
        dt_abs, dt_exp, dt_log, dt_ready = sem("dt_abs"), sem("dt_exp"), sem("dt_log"), sem("dt_ready")
        relu_used, mask_ready = sem("relu_used"), sem("mask_ready")
        max_ready, exp_ready, p_ready = sem("max_ready"), sem("exp_ready"), sem("p_ready")
        conv_ready, silu_ready = sem("conv_ready"), sem("silu_ready")
        ssd_in, acs_ready, R_ready, dec_exp, diff_ready = (
            sem("ssd_in"), sem("acs_ready"), sem("R_ready"), sem("dec_exp"), sem("diff_ready"))
        decay_in, decay_out, M_ready = sem("decay_in"), sem("decay_out"), sem("M_ready")
        y_ready, y_ss, y_rs, od_ready = sem("y_ready"), sem("y_ss"), sem("y_rs"), sem("od_ready")
        gv_ss, gv_mean, gv_rs, gv_ready = sem("gv_ss"), sem("gv_mean"), sem("gv_rs"), sem("gv_ready")
        oc_ready, ob_ready, gsig_used, merged_ready = (
            sem("oc_ready"), sem("ob_ready"), sem("gsig_used"), sem("merged_ready"))
        x_mid, logit_ready, sig_ready, comb_ready = sem("x_mid"), sem("logit_ready"), sem("sig_ready"), sem("comb_ready")
        silu_done, hid_ready, down_used = sem("silu_done"), sem("hid_ready"), sem("down_used")
        layer_done, stored = sem("layer_done"), sem("stored")

        def ps(name):
            if name in S_JOBS:
                return bank[:, 6 + S_JOBS.index(name) % 2, :]
            return bank[:, 4 + V_JOBS.index(name) % 2, :]

        def pj(name):
            b = 2 * (PROJ_JOBS.index(name) % 2)
            return bank[:, b:b + 2, :]

        block = ctx.enter_context(nc.Block())

        @block.sync
        def _(sp):
            w_in_v = w_in.rearrange("l (k p) n -> l p k n", p=P)
            w_br_v = w_branch.rearrange("l b (k p) n -> l b p k n", p=P)
            w_a_v = w_branch.rearrange("l b (g k p) n -> l b g p k n", g=AG, p=AD)
            w_out_v = w_out.rearrange("l (k p) n -> l p k n", p=P)
            wg_v = exp_w_gate.rearrange("l e (k p) n -> (l e) p k n", p=P)
            wu_v = exp_w_up.rearrange("l e (k p) n -> (l e) p k n", p=P)
            wd_v = exp_w_down.rearrange("l e (k p) n -> (l e) p k n", p=P)
            start = {"A": CQ, "xbc": CXBC, "gv": CGV, "z": CZ, "gu": CGU, "scc": CSC, "scx": CSX, "scb": CSB}

            sp.sem_inc(units_read, RING)
            sp.dma_start(x_sb[:, :, :], x[0].rearrange("(t p) d -> p t d", p=P)).then_inc(x_in, 16)
            with sp.Fori(0, DEPTH) as l:
                def load(n, src, dst=None):
                    s = n % RING
                    dst = ring[:, s, :, :] if dst is None else dst
                    sp.dma_start(dst, src).then_inc(slot_loaded[s], 16)

                for n, (name, h) in enumerate(UNITS):
                    s = n % RING
                    ks = slice(HK * h, HK * h + HK)
                    sp.wait_ge(units_read, l * UNITS_L + n + 1)
                    sp.sem_inc(unit_turn, 1)
                    if name == "C":
                        load(n, w_in_v[l, :, ks, CQI:CQI + 256], ring[:, s, :, 0:256])
                        load(n, w_in_v[l, :, ks, CXBC + W:CXBC + W + 256], ring[:, s, :, 256:512])
                    elif name == "B":
                        load(n, w_in_v[l, :, ks, CK:CK + 256], ring[:, s, :, 0:256])
                        load(n, w_in_v[l, :, ks, CKI:CKI + ID + IH], ring[:, s, :, 256:256 + ID + IH])
                        load(n, w_in_v[l, :, ks, CDT:CDT + MH], ring[:, s, :, 256 + ID + IH:SMALL])
                    elif name in start:
                        load(n, w_in_v[l, :, ks, start[name]:start[name] + W])
                    elif name[0] == "g":
                        c0 = CG + int(name[1]) * D_MODEL + int(name[2]) * W
                        load(n, w_in_v[l, :, ks, c0:c0 + W])
                    elif name[0:2] == "b0":
                        for g in range(AG):
                            load(n, w_a_v[l, 0, g, :, :, int(name[2]) * W:int(name[2]) * W + W],
                                 ring[AD * g:AD * g + AD, s, :, :])
                    elif name[0] == "b":
                        load(n, w_br_v[l, int(name[1]), :, :, int(name[2]) * W:int(name[2]) * W + W])
                    else:
                        load(n, w_out_v[l, :, ks, int(name[1]) * W:int(name[1]) * W + W])

                def gate_up(n, slot, view, e):
                    for h in range(2):
                        sp.wait_ge(units_read, l * UNITS_L + n + h + 1)
                        load(slot + h, view[e, :, HK * h:HK * h + HK, :])

                def down(n, slot, e):
                    for j in range(2):
                        sp.wait_ge(units_read, l * UNITS_L + n + j + 1)
                        load(slot + j, wd_v[e, :, :, j * W:j * W + W])

                first = sp.snap(l * NE)
                gate_up(MOE0, 0, wg_v, first)
                gate_up(MOE0 + 2, 2, wu_v, first)
                with sp.Fori(1, NE) as e:
                    n = MOE0 + 4 + (e - 1) * PER_E
                    this = sp.snap(l * NE + e)
                    last = sp.snap(l * NE + e - 1)
                    gate_up(n, 4, wg_v, this)
                    down(n + 2, 0, last)
                    gate_up(n + 4, 2, wu_v, this)
                down(UNITS_L - 2, 4, sp.snap(l * NE + NE - 1))
            sp.wait_ge(layer_done, DEPTH + 1)
            sp.dma_start(out[0].rearrange("(t p) d -> p t d", p=P), x_sb[:, :, :]).then_inc(stored, 16)
            sp.wait_ge(stored, 16)

        @block.gpsimd
        def _(pool):
            pool.dma_start(pos_i[:, :], positions[0].rearrange("(t p) -> p t", p=P),
                           allow_slow_non_contiguous=True).then_inc(pos_in, 16)
            pool.dma_start(rw[:, :, :], router_w.rearrange("(k p) e -> p k e", p=P)).then_inc(rw_in, 16)
            pool.dma_start(rbias[:, :], router_bias.partition_broadcast(P)).then_inc(rw_in, 16)
            for tile, val in ((ident, 0.0), (tri, 1.0), (late, 0.0), (future, 0.0), (ones, 1.0)):
                pool.memset(tile[:, :], val).then_inc(consts, 1)
            for f in range(AROT // 2):
                val = float(np.exp(np.float32(-math.log(ROPE_THETA)) * np.float32(f) * np.float32(2.0)
                                   / np.float32(AROT)))
                pool.memset(invf[:, f:f + 1], val).then_inc(consts, 1)
            for f in range(NE):
                pool.memset(rank[:, f:f + 1], float(NE - f)).then_inc(consts, 1)
            for tile in (bd_qt[:, 0, :, :], kTd[:, :, :], CTd[:, :, :], prevd[:, :], xbc[:, :, 0:M_K - 1]):
                pool.memset(tile, 0.0).then_inc(consts, 1)
            assert 5 + AROT // 2 + NE + 5 == FILLS
            pool.wait_ge(consts, FILLS)
            pool.affine_select(out=ident[:, :], in_=ident[:, :], compare_op=ALU.not_equal, fill=1.0,
                               base=0, pattern=[[-1, P]], channel_multiplier=1).then_inc(consts, 1)
            pool.affine_select(out=tri[:, :], in_=tri[:, :], compare_op=ALU.is_ge, fill=0.0,
                               base=0, pattern=[[1, P]], channel_multiplier=-1).then_inc(consts, 1)
            pool.affine_select(out=late[:, :], in_=late[:, :], compare_op=ALU.is_ge, fill=-BIG,
                               base=0, pattern=[[1, P]], channel_multiplier=-1).then_inc(consts, 1)
            pool.affine_select(out=future[:, :], in_=future[:, :], compare_op=ALU.is_ge, fill=-BIG,
                               base=P, pattern=[[-1, SEQ]], channel_multiplier=1).then_inc(consts, 1)

            pool.sem_inc(ada_freed, 2)
            ada_v = ada_w.rearrange("l (k p) n -> l p k n", p=P)
            with pool.Fori(0, DEPTH) as l:
                pool.wait_ge(pcol_ready, l + 1)
                rows = (("norm1", norm1_g[l]), ("norm2", norm2_g[l]), ("adab", ada_b[l]),
                        ("scw", sc_conv_w[l].rearrange("k n -> (k n)")), ("gvg", g_v_norm_g[l]),
                        ("mcw", m_conv_w[l].rearrange("k n -> (k n)")), ("mcb", m_conv_b[l]),
                        ("mng", m_norm_g[l]), ("c", c[0]))
                for name, src in rows:
                    v = src.rearrange("(r j) -> r j", j=P)
                    pool.dma_start(prow[PR[name]:PR[name] + v.shape[0], :], v).then_inc(prow_in, 16)

                def ada(u):
                    chunk, q = u // 4, u % 4
                    pool.wait_ge(ada_freed, l * ADA_U + u + 1)
                    pool.dma_start(ada_buf[:, u % 2, :, :],
                                   ada_v[l, :, 2 * q:2 * q + 2, chunk * W:chunk * W + W]
                                   ).then_inc(ada_loaded[u % 2], 16)

                for u in range(4):
                    ada(u)
                pool.wait_ge(layer_done, l + 1)
                pool.dma_start(gain[:, 0, :], q_norm_g[l].partition_broadcast(P)).then_inc(rows_in, 16)
                pool.dma_start(gain[:, 1, :], k_norm_g[l].partition_broadcast(P)).then_inc(rows_in, 16)
                for i, src in enumerate((m_dt_bias, m_a_log, m_d)):
                    pool.dma_start(mrow[:, i, :], src[l].partition_broadcast(P)).then_inc(rows_in, 16)
                pool.dma_start(gsb[:, :, :], g_spatial_b[l].partition_broadcast(P)).then_inc(rows_in, 16)
                for i in range(2):
                    c0 = (2 + 3 * i) * D_MODEL
                    pool.dma_start(gate_bc[:, i, :], ada_b[l, c0:c0 + D_MODEL].partition_broadcast(P)
                                   ).then_inc(gateb_in, 16)
                pool.dma_start(wsraw[:, :, :], g_spatial_w[l].rearrange("g t s -> t g s")).then_inc(wsraw_in, 16)
                for u in range(4, ADA_U):
                    ada(u)

        @block.tensor
        def _(pe):
            mm, tr = nc.tensor.matmul, nc.tensor.transpose
            pe.sem_inc(proj_evac, 2)
            pe.sem_inc(s_evac, 2)
            pe.sem_inc(v_evac, 2)
            pe.sem_inc(acc_used, 2)
            pe.wait_ge(consts, FILLS + 4)
            with pe.Fori(0, DEPTH) as l:
                done = {"proj": 0, "s": 0, "v": 0, "unit": 0}
                NJ = {"proj": NPJ, "s": NSJ, "v": NVJ}
                JOBS = {"proj": PROJ_JOBS, "s": S_JOBS, "v": V_JOBS}
                EVAC = {"proj": proj_evac, "s": s_evac, "v": v_evac}
                

                def begin(kind, name):
                    assert JOBS[kind][done[kind]] == name, (name, JOBS[kind][done[kind]])
                    pe.wait_ge(EVAC[kind], l * NJ[kind] + done[kind] + 1)
                    done[kind] += 1
                    return pj(name) if kind == "proj" else ps(name)

                def loaded():
                    n = done["unit"]
                    done["unit"] += 1
                    pe.wait_ge(slot_loaded[n % RING], l * (16 * SLOT_L[n % RING]) + 16 * LANDED[n])
                    return ring[:, n % RING, :, :]

                def tok_project(out2, w, h, n, c0=0, lhs=hT):
                    for t in range(TT):
                        for k in range(HK):
                            last = mm(out2[t], lhs[:, HK * h + k, t * P:t * P + P], w[:, k, c0:c0 + n],
                                      start=(h == 0 and k == 0), stop=(h == 1 and k == HK - 1))
                    return last

                def chan_project(out_of, w, h, c0, tiles):
                    for m in range(tiles):
                        for k in range(HK):
                            last = mm(out_of(m), w[:, k, c0 + m * P:c0 + m * P + P], hT[:, HK * h + k, :],
                                      start=(h == 0 and k == 0 and m % 2 == 0),
                                      stop=(h == 1 and k == HK - 1), skip_group_check=True)
                    return last

                def tok_job(name, n=W):
                    b = begin("proj", name)
                    for h in range(2):
                        w = loaded()
                        tok_project([b[:, t, 0:n] for t in range(TT)], w, h, n).then_inc(units_read, 1)

                def chan_job(name):
                    b = begin("proj", name)
                    for h in range(2):
                        w = loaded()
                        chan_project(lambda m: b[:, m // 2, (m % 2) * SEQ:(m % 2) * SEQ + SEQ], w, h, 0,
                                     CT).then_inc(units_read, 1)

                def modulate_transposes(norm):
                    for q in range(4):
                        b = begin("s" if q < 2 else "v", f"h{norm}_{q}")
                        for k in range(2):
                            for t in range(TT):
                                last = tr(b[:, (k * TT + t) * P:(k * TT + t + 1) * P],
                                          merged[:, t, (2 * q + k) * P:(2 * q + k + 1) * P], ident[:, :])
                        last.then_inc(s_ready if q < 2 else v_ready, 1)

                def mod_columns(name, chunks, l_chunk0):
                    b = begin("v", name)
                    for i in range(chunks):
                        n = l_chunk0 + i
                        pe.wait_ge(acc_ready, l * MOD_CHUNKS + n + 2)
                        for q in range(4):
                            last = mm(b[:, 4 * i + q:4 * i + q + 1], ada_acc[:, n % 2, q * P:q * P + P],
                                      ones[:, 0:1], start=True, stop=True)
                        last.then_inc(acc_used, 1)

                def mod_row(name, n):
                    b = begin("v", name)
                    pe.wait_ge(acc_ready, l * MOD_CHUNKS + n + 2)
                    mm(b[:, :], ones[:, :], ada_acc[:, n % 2, :], start=True, stop=True).then_inc(acc_used, 1)

                pe.wait_ge(down_used, l * NE + 1)
                b = begin("v", PCOL)
                pe.wait_ge(prow_in, (l + 1) * (9 * 16))
                tr(b[:, 0:PROWS], prow[0:PROWS, :], ident[0:PROWS, 0:PROWS]).then_inc(v_ready, 1)
                mod_columns("modA", 4, 0)
                pe.wait_ge(xn_ready, l * 2 + 1)
                modulate_transposes(1)

                pe.wait_ge(s_evac, l * NSJ + S_JOBS.index("h1_1") + 1 + 2)
                pe.wait_ge(v_evac, l * NVJ + V_JOBS.index("h1_3") + 1 + 2)
                b = begin("proj", "C")
                for h in range(2):
                    w = loaded()
                    for t in range(TT):
                        for k in range(HK):
                            mm(b[:, 0, t * 256:t * 256 + 256], hT[:, HK * h + k, t * P:t * P + P], w[:, k, 0:256],
                               start=(h == 0 and k == 0 and t == 0), stop=(h == 1 and k == HK - 1),
                               skip_group_check=True)
                    chan_project(lambda m: b[:, 1, m * SEQ:m * SEQ + SEQ], w, h, 256, 2).then_inc(units_read, 1)
                tok_job("B", SMALL)
                tok_job("A")

                pe.wait_ge(idx_rope, l + 1)
                b = begin("s", "qiT")
                for g in range(2):
                    for t in range(TT):
                        last = tr(b[:, (g * TT + t) * P:(g * TT + t + 1) * P],
                                  qik[:, t, 4 * g:4 * g + 4, :].rearrange("p h d -> p (h d)"), ident[:, :])
                last.then_inc(s_ready, 1)
                b = begin("s", "kiT")
                for t in range(TT):
                    last = tr(b[:, t * P:t * P + P], kirep[:, t, :, :].rearrange("p r d -> p (r d)"), ident[:, :])
                last.then_inc(s_ready, 1)
                chan_job("xbc")
                pe.wait_ge(s_evac, l * NSJ + S_JOBS.index("kiT") + 1 + 2)
                for t in range(TT):
                    ns = (t + 1) * P
                    for g in range(2):
                        for u in range(2):
                            b = begin("s", f"dot{t}{g}{u}")
                            mm(b[:, 0:2 * ns].rearrange("p (h s) -> p h s", h=2), qiT[:, g, t * P:t * P + P],
                               kiTd[:, 2 * u:2 * u + 2, 0:ns], start=True, stop=True).then_inc(s_ready, 1)
                pe.wait_ge(qk_roped, l + 1)
                for half in range(2):
                    b = begin("s", f"qT{half}")
                    for i in range(2):
                        for t in range(TT):
                            o = (2 * half + i) * 2
                            last = tr(b[:, (i * TT + t) * P:(i * TT + t + 1) * P],
                                      qk[:, t, o:o + 2, :].rearrange("p h d -> p (h d)"), ident[:, :])
                    last.then_inc(s_ready, 1)
                b = begin("s", "kT")
                for t in range(TT):
                    last = tr(b[:, t * P:t * P + P], qk[:, t, AH:AH + 2, :].rearrange("p h d -> p (h d)"),
                              ident[:, :])
                last.then_inc(s_ready, 1)
                tok_job("gv")
                pe.wait_ge(wsraw_in, (l + 1) * 16)
                b = begin("v", "wsT")
                for g in range(GG):
                    last = tr(b[:, g * P:g * P + P], wsraw[:, g, :], ident[:, :])
                last.then_inc(v_ready, 1)
                tok_job("z")
                pe.wait_ge(silu_ready, l + 1)
                for t in range(TT):
                    b = begin("s", f"xs{t}")
                    for m in range(CT):
                        last = tr(b[:, m * P:m * P + P], xbcT[:, m, t * P:t * P + P], ident[:, :])
                    last.then_inc(s_ready, 1)
                b = begin("s", "Bt")
                tr(b[:, 0:P], xbcT[:, 4, 0:P], ident[:, :]).then_inc(s_ready, 1)
                chan_job("gu")
                pe.wait_ge(s_evac, l * NSJ + S_JOBS.index("kT") + 1 + 2)
                for t in range(TT):
                    ns = (t + 1) * P
                    for i in range(4):
                        b = begin("v", f"lg{t}{i}")
                        mm(b[:, 0:2 * ns].rearrange("p (h s) -> p h s", h=2), qT[:, i, t * P:t * P + P],
                           kTd[:, :, 0:ns], start=True, stop=True).then_inc(v_ready, 1)
                pe.wait_ge(p_ready, l + 1)
                for i in range(4):
                    for u in range(2):
                        hd = i + 4 * u
                        b = begin("s", f"PT{i}{'ab'[u]}")
                        tr(b[:, 0:P], P_sb[:, hd, 0:P], ident[:, :])
                        tr(b[:, P:2 * P], P_sb[:, hd, P:2 * P], ident[:, :])
                        tr(b[:, 2 * P:3 * P], P_sb[:, hd, 2 * P:3 * P], ident[:, :]).then_inc(s_ready, 1)
                    b = begin("s", f"PV{i}")
                    pe.wait_ge(s_evac, l * NSJ + S_JOBS.index(f"PT{i}b") + 1 + 2)
                    for u in range(2):
                        pt = PT[:, (i + 4 * u) * 3 * P:(i + 4 * u + 1) * 3 * P]
                        mm(b[:, u * SEQ:u * SEQ + SEQ], v_sb[:, 0, :], pt[:, 0:SEQ], start=(u == 0), stop=False,
                           skip_group_check=True)
                        last = mm(b[:, u * SEQ + P:u * SEQ + SEQ], v_sb[:, 1, :], pt[:, SEQ:3 * P], start=False,
                                  stop=True, skip_group_check=True)
                    last.then_inc(s_ready, 1)
                pe.wait_ge(dt_ready, l + 1)
                b = begin("v", "acs")
                da = dtA[:, 1, :, :].rearrange("p c h -> p (c h)")
                mm(b[:, 0:16], tri[:, :], da, start=True, stop=True)
                mm(b[:, 16:32], ones[:, :], da, start=True, stop=True).then_inc(v_ready, 1)
                chan_job("scc")
                def cumulative(ch):
                    pe.wait_ge(R_ready, l * 2 + ch + 1)
                    for hh in range(2):
                        b = begin("v", f"ab{ch}{hh}")
                        mm(b[:, :], ones[:, :], scratch[:, ch * 1024 + hh * W:ch * 1024 + hh * W + W],
                           start=True, stop=True).then_inc(v_ready, 1)

                def chunk_output(ch):
                    b = begin("v", f"y{ch}")
                    pe.wait_ge(M_ready, l * 2 + ch + 1)
                    for hd in range(MH):
                        last = mm(b[:, hd * MP:hd * MP + MP], M_sb[:, hd, :], xdt[:, ch, hd * MP:hd * MP + MP],
                                  start=True, stop=True)
                    last.then_inc(v_ready, 1)

                cumulative(0)
                b = begin("s", "scT")
                pe.wait_ge(CTd_ready, l + 1)
                for c2 in range(TT):
                    last = mm(b[:, c2 * 256:c2 * 256 + 256].rearrange("p (g s) -> p g s", g=2),
                              xbcT[:, 4, c2 * P:c2 * P + P], CTd[:, :, c2 * P:c2 * P + P], start=True, stop=True)
                last.then_inc(s_ready, 1)
                chan_job("scx")
                chunk_output(0)
                b = begin("s", "states")
                pe.wait_ge(ssd_in, l + 1)
                mm(b[:, :], Btok[:, :], xdtd[:, :], start=True, stop=True).then_inc(s_ready, 1)
                cumulative(1)
                chan_job("scb")
                b = begin("v", "yoff")
                pe.wait_ge(s_evac, l * NSJ + S_JOBS.index("states") + 1 + 2)
                mm(b[:, :], xbcT[:, 5, P:2 * P], prevd[:, :], start=True, stop=True).then_inc(v_ready, 1)
                chunk_output(1)
                pe.wait_ge(gv_ready, l + 1)
                for q in range(2):
                    b = begin("v", f"mix{q}")
                    for g in range(2):
                        for ch in range(TT):
                            last = mm(b[:, (g * TT + ch) * P:(g * TT + ch + 1) * P],
                                      gv[:, ch, (2 * q + g) * P:(2 * q + g + 1) * P], wsT[:, 2 * q + g, :],
                                      start=True, stop=True)
                    last.then_inc(v_ready, 1)

                for i in BRANCH_ORDER:
                    if i == 1:
                        pe.wait_ge(ob_ready, l + 1)
                    elif i == 2:
                        pe.wait_ge(oc_ready, l + 1)
                    elif i == 3:
                        pe.wait_ge(od_ready, l + 1)
                        for q in range(2):
                            b = begin("s", f"odT{q}")
                            for m in range(2):
                                for t in range(TT):
                                    last = tr(b[:, (m * TT + t) * P:(m * TT + t + 1) * P],
                                              y_sb[:, t, (2 * q + m) * P:(2 * q + m + 1) * P], ident[:, :])
                            last.then_inc(s_ready, 1)
                    for j in range(2):
                        tok_job(f"g{i}{j}")
                        w = loaded()
                        if i == 3 and j == 0:
                            pe.wait_ge(s_evac, l * NSJ + S_JOBS.index("odT1") + 1 + 2)
                        for t in range(TT):
                            b = begin("v", f"b{i}{j}{t}")
                            for k in range(CT):
                                last = mm(b[:, :], oT[:, i, k, t * P:t * P + P], w[:, k, :],
                                          start=(k == 0), stop=(k == CT - 1))
                            last.then_inc(units_read if t else v_ready, 1)
                mod_row("gate10", 4)
                mod_row("gate11", 5)
                mod_columns("modB", 4, 6)
                mod_row("gate20", 10)
                mod_row("gate21", 11)
                pe.wait_ge(merged_ready, l + 1)
                for q in range(4):
                    b = begin("s", f"mT{q}")
                    for k in range(2):
                        for t in range(TT):
                            last = tr(b[:, (k * TT + t) * P:(k * TT + t + 1) * P],
                                      merged[:, t, (2 * q + k) * P:(2 * q + k + 1) * P], ident[:, :])
                    last.then_inc(s_ready, 1)
                pe.wait_ge(s_evac, l * NSJ + S_JOBS.index("mT3") + 1 + 2)
                for j in range(2):
                    b2 = [begin("v", f"o{j}{t}") for t in range(TT)]
                    for h in range(2):
                        w = loaded()
                        tok_project([b[:, :] for b in b2], w, h, W).then_inc(units_read, 1)

                pe.wait_ge(xn_ready, l * 2 + 2)
                modulate_transposes(2)
                pe.wait_ge(s_evac, l * NSJ + S_JOBS.index("h2_1") + 1 + 2)
                pe.wait_ge(v_evac, l * NVJ + V_JOBS.index("h2_3") + 1 + 2)
                b = begin("v", "router")
                pe.wait_ge(rw_in, 32)
                for t in range(TT):
                    for k in range(KD):
                        last = mm(b[:, t * NE:t * NE + NE], hT[:, k, t * P:t * P + P], rw[:, k, :],
                                  start=(k == 0), stop=(k == KD - 1))
                last.then_inc(v_ready, 1)
                if "pad" in V_JOBS:
                    begin("v", "pad")

                pe.wait_ge(proj_evac, (l + 1) * NPJ + 2)
                pe.wait_ge(s_evac, (l + 1) * NSJ + 2)
                pe.wait_ge(v_evac, (l + 1) * NVJ + 2)

                def gate_up(b0, slot, uses):
                    for h in range(2):
                        pe.wait_ge(slot_loaded[slot + h], l * (16 * SLOT_L[slot + h])
                                   + 16 * (SLOT_MIX[slot + h] + uses))
                        w = ring[:, slot + h, :, :]
                        last = chan_project(lambda m: bank[:, b0 + m // 2, (m % 2) * SEQ:(m % 2) * SEQ + SEQ],
                                            w, h, 0, CT)
                        last.then_inc(units_read, 1)

                def down(slot, uses, e1):
                    pe.wait_ge(hid_ready, l * NE + e1 + 1)
                    for j in range(2):
                        pe.wait_ge(slot_loaded[slot + j], l * (16 * SLOT_L[slot + j])
                                   + 16 * (SLOT_MIX[slot + j] + uses))
                        for t in range(TT):
                            for k in range(CT):
                                last = mm(bank[:, 4 + 2 * t + j, :], hid[:, k, t * P:t * P + P],
                                          ring[:, slot + j, k, :], start=(k == 0), stop=(k == CT - 1))
                        last.then_inc(units_read, 1)

                gate_up(0, 0, 1)
                gate_up(2, 2, 1)
                with pe.Fori(1, NE) as e:
                    pe.wait_ge(silu_done, l * NE + e)
                    gate_up(0, 4, e)
                    pe.wait_ge(down_used, l * NE + (e - 1) + 1)
                    down(0, e + 1, e)
                    gate_up(2, 2, e + 1)
                pe.wait_ge(down_used, l * NE + NE - 1 + 1)
                down(4, NE, NE)

        @block.scalar
        def _(act):
            A = nc.scalar.activation
            act.wait_ge(angles_ready, 1)
            A(rope[:, :, :, :], ang[:, :, :, :], ACT.Sin).then_inc(rope_ready, 1)
            act.wait_ge(x_in, 16)
            with act.Fori(0, DEPTH) as l:
                seen = {"s": 0, "proj": 0}

                def job(kind, name):
                    jobs = S_JOBS if kind == "s" else PROJ_JOBS
                    assert jobs[seen[kind]] == name, (name, jobs[seen[kind]])
                    seen[kind] += 1
                    if kind == "s":
                        act.wait_ge(s_ready, l * NSJ + seen[kind])
                    else:
                        act.wait_ge(units_read, l * UNITS_L + UNITS.index((name, 1)) + 1 + RING)
                    return ps(name) if kind == "s" else pj(name)

                def copy(dst, src):
                    return A(dst, src, ACT.Copy)

                act.wait_ge(pcol_ready, l + 2)
                act.wait_ge(acc_ready, l * MOD_CHUNKS + 1)
                A(cact[:, :], pcol[:, PR["c"]:PR["c"] + KD], ACT.Silu).then_inc(cact_ready, 1)

                def sum_squares(norm):
                    act.wait_ge(layer_done if norm == 1 else x_mid, l + 1)
                    for t in range(TT):
                        last = A(merged[:, t, :], x_sb[:, t, :], ACT.Square, accum_out=st[:, 0, t:t + 1])
                    last.then_inc(ss_ready, 1)

                def modulate(norm):
                    act.wait_ge(modc_ready, l * 2 + norm)
                    for q in range(2):
                        b = job("s", f"h{norm}_{q}")
                        for k in range(2):
                            kk = 2 * q + k
                            last = A(hT[:, kk, :], b[:, k * SEQ:k * SEQ + SEQ], ACT.Identity,
                                     scale=modc[:, norm - 1, 0, kk:kk + 1], bias=modc[:, norm - 1, 1, kk:kk + 1])
                        last.then_inc(s_evac, 1)

                sum_squares(1)
                act.wait_ge(mean_ready, l * 2 + 1)
                A(st[:, 2, 0:TT], st[:, 1, 0:TT], ACT.Sqrt).then_inc(rs_ready, 1)
                modulate(1)
                b = job("proj", "C")
                copy(qik[:, :, 0:IH, :], b[:, 0, :].rearrange("p (t h d) -> p t h d", t=TT, d=ID))
                copy(xbc[:, 4:6, M_K - 1:], b[:, 1, :].rearrange("p (m s) -> p m s", m=2)).then_inc(proj_evac, 1)
                b = job("proj", "B")
                o = 2 * AG * AD
                copy(qik[:, :, IH, :], b[:, :, o:o + ID])
                copy(wdt[:, :, :], b[:, :, o + ID:o + ID + IH + MH])
                copy(v_sb[:, :, :], b[:, :, AG * AD:o])
                copy(qk[:, :, AH:AH + 2, :], b[:, :, 0:AG * AD].rearrange("p t (g d) -> p t g d", g=AG)
                     ).then_inc(proj_evac, 1)
                b = job("proj", "A")
                for t in range(TT):
                    last = copy(qk[:, t, 0:AH, :].rearrange("p (i g) d -> p i g d", g=AG),
                                b[:, t, :].rearrange("p (g i d) -> p i g d", g=AG, i=4))
                last.then_inc(proj_evac, 1)
                act.wait_ge(dt_abs, l + 1)
                A(st[:, 4, 0:16], st[:, 3, 0:16], ACT.Exp, scale=-1.0).then_inc(dt_exp, 1)
                act.wait_ge(dt_exp, l + 1)
                A(st[:, 5, 0:16], st[:, 4, 0:16], ACT.Ln, bias=1.0)
                A(st[:, 7, 0:MH], mrow[:, 1, :], ACT.Exp).then_inc(dt_log, 1)
                act.wait_ge(qk_ss, l + 1)
                A(st[:, 9, 0:20], st[:, 8, 0:20], ACT.Sqrt).then_inc(qk_rs, 1)
                b = job("s", "qiT")
                copy(qiT[:, :, :], b[:, :].rearrange("p (g s) -> p g s", g=2)).then_inc(s_evac, 1)
                b = job("s", "kiT")
                for j in range(4):
                    last = copy(kiTd[32 * j:32 * j + 32, j, :], b[32 * j:32 * j + 32, 0:SEQ])
                last.then_inc(s_evac, 1)
                b = job("proj", "xbc")
                copy(xbc[:, 0:4, M_K - 1:], b[:, :, :].rearrange("p b (m s) -> p (b m) s", m=2)
                     ).then_inc(proj_evac, 1)
                act.wait_ge(qk_roped, l + 1)
                n = 0
                for t in range(TT):
                    ns = (t + 1) * P
                    for g in range(2):
                        for u in range(2):
                            b = job("s", f"dot{t}{g}{u}")
                            if n >= 2:
                                act.wait_ge(relu_used, l * 8 + n - 1)
                            A(scratch[:, (n % 2) * W:(n % 2) * W + 2 * ns], b[:, 0:2 * ns], ACT.Relu
                              ).then_inc(s_evac, 1)
                            n += 1
                for half in range(2):
                    b = job("s", f"qT{half}")
                    copy(qT[:, 2 * half:2 * half + 2, :], b[:, :].rearrange("p (i s) -> p i s", i=2)
                         ).then_inc(s_evac, 1)
                b = job("s", "kT")
                for g in range(AG):
                    last = copy(kTd[64 * g:64 * g + 64, g, :], b[64 * g:64 * g + 64, 0:SEQ])
                last.then_inc(s_evac, 1)
                b = job("proj", "gv")
                A(gv[:, :, :], b[:, :, :], ACT.Gelu).then_inc(proj_evac, 1)
                act.wait_ge(proj_evac, l * NPJ + PROJ_JOBS.index("gv") + 1 + 2)
                act.wait_ge(relu_used, l * 8 + 8)
                for t in range(TT):
                    last = A(scratch[:, t * W:t * W + W], gv[:, t, :], ACT.Square, accum_out=st[:, 10, t:t + 1])
                last.then_inc(gv_ss, 1)
                b = job("proj", "z")
                A(z_sb[:, :, :], b[:, :, :], ACT.Silu).then_inc(proj_evac, 1)
                act.wait_ge(conv_ready, l + 1)
                for m in range(6):
                    last = A(xbcT[:, m, :], xbcT[:, m, :], ACT.Silu, bias=pcol[:, PR["mcb"] + m:PR["mcb"] + m + 1])
                last.then_inc(silu_ready, 1)
                act.wait_ge(silu_ready, l + 1)
                for g in range(MG):
                    last = copy(CTd[64 * g:64 * g + 64, g, :], xbcT[64 * g:64 * g + 64, 5, :])
                last.then_inc(CTd_ready, 1)
                for t in range(TT):
                    b = job("s", f"xs{t}")
                    copy(xs_tok[:, t, :], b[:, :]).then_inc(s_evac, 1)
                b = job("s", "Bt")
                copy(Btok[:, :], b[:, 0:P]).then_inc(s_evac, 1)
                act.wait_ge(gv_mean, l + 1)
                A(st[:, 12, 0:TT], st[:, 11, 0:TT], ACT.Sqrt).then_inc(gv_rs, 1)
                b = job("proj", "gu")
                A(uT[:, :, :], b[:, :, :].rearrange("p b (m s) -> p (b m) s", m=2), ACT.Gelu).then_inc(proj_evac, 1)
                for t in range(TT):
                    act.wait_ge(max_ready, l * 2 + t + 1)
                    lo, hi = (0, P) if t == 0 else (P, 3 * P)
                    for hd in range(AH):
                        last = A(P_sb[:, hd, lo:hi], P_sb[:, hd, lo:hi], ACT.Exp, scale=AD ** -0.5,
                                 bias=st[:, 14 + t, hd:hd + 1], accum_out=st[:, 16 + t, hd:hd + 1])
                    last.then_inc(exp_ready, 1)
                for i in range(4):
                    for u in range(2):
                        hd = i + 4 * u
                        b = job("s", f"PT{i}{'ab'[u]}")
                        copy(PT[:, hd * 3 * P:(hd + 1) * 3 * P], b[:, 0:3 * P]).then_inc(s_evac, 1)
                    b = job("s", f"PV{i}")
                    for u in range(2):
                        last = copy(oT[64 * u:64 * u + 64, 0, i, :], b[64 * u:64 * u + 64, u * SEQ:u * SEQ + SEQ])
                    last.then_inc(s_evac, 1)
                b = job("proj", "scc")
                copy(scc, b[:, :, :].rearrange("p b (m s) -> p (b m) s", m=2)).then_inc(proj_evac, 1)
                act.wait_ge(acs_ready, l + 1)
                A(dtA[:, 2:4, :, :], dtA[:, 2:4, :, :], ACT.Exp).then_inc(decay_out, 1)
                b = job("s", "scT")
                copy(scT[:, :, :, :], b[:, :].rearrange("p (c g s) -> p c g s", c=2, g=2)).then_inc(s_evac, 1)
                act.wait_ge(diff_ready, l * 2 + 1)
                A(M_sb, M_sb, ACT.Exp).then_inc(dec_exp, 1)
                b = job("proj", "scx")
                copy(cx[:, :, 2:], b[:, :, :].rearrange("p b (m s) -> p (b m) s", m=2)).then_inc(proj_evac, 1)
                b = job("s", "states")
                copy(prevd[0:64, 0:256], b[0:64, 0:256])
                copy(prevd[64:128, 256:512], b[64:128, 256:512]).then_inc(s_evac, 1)
                b = job("proj", "scb")
                copy(scb, b[:, :, :].rearrange("p b (m s) -> p (b m) s", m=2)).then_inc(proj_evac, 1)
                act.wait_ge(diff_ready, l * 2 + 2)
                A(M_sb, M_sb, ACT.Exp).then_inc(dec_exp, 1)
                act.wait_ge(y_ss, l + 1)
                A(st[:, 20, 0:TT], st[:, 19, 0:TT], ACT.Sqrt).then_inc(y_rs, 1)
                for n, i in enumerate(BRANCH_ORDER):
                    if i == 3:
                        for q in range(2):
                            b = job("s", f"odT{q}")
                            for m in range(2):
                                mt = 2 * q + m
                                last = A(oT[:, 3, mt, :], b[:, m * SEQ:m * SEQ + SEQ], ACT.Copy,
                                         scale=pcol[:, PR["mng"] + mt:PR["mng"] + mt + 1])
                            last.then_inc(s_evac, 1)
                    for j in range(2):
                        b = job("proj", f"g{i}{j}")
                        if 2 * n + j >= 2:
                            act.wait_ge(gsig_used, l * 8 + 2 * n + j - 1)
                        A(gsig[j], b[:, :, :], ACT.Sigmoid).then_inc(proj_evac, 1)
                for q in range(4):
                    b = job("s", f"mT{q}")
                    copy(hT[:, 2 * q:2 * q + 2, :], b[:, :].rearrange("p (k s) -> p k s", k=2)).then_inc(s_evac, 1)
                sum_squares(2)
                act.wait_ge(mean_ready, l * 2 + 2)
                A(st[:, 2, 0:TT], st[:, 1, 0:TT], ACT.Sqrt).then_inc(rs_ready, 1)
                modulate(2)
                act.wait_ge(logit_ready, l + 1)
                A(rt1[:, 0, :, :], rt1[:, 0, :, :], ACT.Sigmoid).then_inc(sig_ready, 1)
                def silu_gate(read, e):
                    act.wait_ge(units_read, l * UNITS_L + MOE0 + read + RING)
                    act.wait_ge(hid_ready, l * NE + e + 1)
                    A(sg.rearrange("p (b m) s -> p b (m s)", b=2), bank[:, 0:2, :], ACT.Silu).then_inc(silu_done, 1)

                silu_gate(2, 0)
                with act.Fori(1, NE) as e:
                    silu_gate(PER_E * e, e)

        @block.vector
        def _(dve):
            V = nc.vector
            count = [0]

            def step(ins):
                count[0] += 1
                return ins.then_inc(dve_step, 1)

            def settle():
                dve.wait_ge(dve_step, count[0])

            def arrive():
                count[0] += 1
                dve.sem_inc(dve_step, 1)

            for started in (pcol_ready, layer_done, down_used, acc_ready, hid_ready):
                dve.sem_inc(started, 1)
            dve.wait_ge(pos_in, 16)
            dve.wait_ge(consts, FILLS + 4)
            step(V.tensor_copy(pos_f[:, :], pos_i[:, :]))
            settle()
            for i in range(2):
                step(V.tensor_tensor(ang[:, i, :, :], bcast(pos_f[:, :], 2, AROT // 2),
                                     bcast(invf[:, :], 1, TT), ALU.mult))
            settle()
            round_up = 1.5 * 2.0 ** 23
            for i in range(2):
                step(V.tensor_scalar(turns[:, i, :, :], ang[:, i, :, :], 1.0 / (2 * math.pi), 0.25 * i,
                                     ALU.mult, ALU.add))
            settle()
            step(V.tensor_scalar(turns[:, :, :, :], turns[:, :, :, :], round_up, None, ALU.add))
            settle()
            step(V.tensor_scalar(turns[:, :, :, :], turns[:, :, :, :], round_up, None, ALU.subtract))
            settle()
            c1 = 6.28125
            c2 = float(np.float32(round((2 * math.pi - c1) * 2 ** 20) / 2 ** 20))
            c3 = 2 * math.pi - c1 - c2
            for part in (c1, c2, c3):
                step(V.scalar_tensor_tensor(out=ang[:, :, :, :].rearrange("p a t f -> p (a t f)"),
                                            in0=turns[:, :, :, :].rearrange("p a t f -> p (a t f)"), scalar=-part,
                                            in1=ang[:, :, :, :].rearrange("p a t f -> p (a t f)"),
                                            op0=ALU.mult, op1=ALU.add))
                settle()
            step(V.tensor_scalar(ang[:, 1, :, :], ang[:, 1, :, :], math.pi / 2, None, ALU.add))
            settle()
            V.tensor_scalar(ang[:, :, :, :], ang[:, :, :, :], 3.1415925, -3.1415925, ALU.min, ALU.max
                            ).then_inc(angles_ready, 1)
            dve.wait_ge(rope_ready, 1)
            dve.sem_clear(dve_step)
            count[0] = 0

            with dve.Fori(0, DEPTH) as l:
                seen = [0]

                def job(name):
                    assert V_JOBS[seen[0]] == name, (name, V_JOBS[seen[0]])
                    seen[0] += 1
                    if name in BY_UNIT:
                        dve.wait_ge(units_read, l * UNITS_L + BY_UNIT[name] + 1 + RING)
                    elif name in BY_CHUNK:
                        dve.wait_ge(acc_used, l * MOD_CHUNKS + BY_CHUNK[name] + 1 + 2)
                    else:
                        dve.wait_ge(v_ready, l * NVR + V_PLAIN.index(name) + 1)
                    return ps(name)

                def evacuated():
                    dve.wait_ge(v_evac, l * NVJ + seen[0] + 2)

                def col(name, i=0, n=1):
                    return pcol[:, PR[name] + i:PR[name] + i + n]

                def ada_chunk(n):
                    dve.wait_ge(acc_used, l * MOD_CHUNKS + n + 1)
                    for q in range(4):
                        u = 4 * n + q
                        dve.wait_ge(ada_loaded[u % 2], l * (ADA_U // 2 * 16) + (u // 2 + 1) * 16)
                        for k in range(2):
                            w, ck = ada_buf[:, u % 2, k, :], cact[:, 2 * q + k:2 * q + k + 1]
                            acc = ada_acc[:, n % 2, :]
                            if q == 0 and k == 0:
                                ins = V.tensor_scalar(acc, w, ck, None, ALU.mult)
                            else:
                                ins = V.scalar_tensor_tensor(out=acc, in0=w, scalar=ck, in1=acc, op0=ALU.mult,
                                                             op1=ALU.add)
                            if k == 1:
                                ins.then_inc(ada_freed, 1)
                                dve.wait_ge(ada_freed, l * ADA_U + u + 1 + 2)
                            else:
                                step(ins)
                                settle()
                    dve.sem_inc(acc_ready, 1)

                def norm_scale(norm):
                    dve.wait_ge(ss_ready, l * 2 + norm)
                    V.tensor_scalar(st[:, 1, 0:TT], st[:, 0, 0:TT], 1.0 / D_MODEL, EPS, ALU.mult, ALU.add
                                    ).then_inc(mean_ready, 1)
                    dve.wait_ge(rs_ready, l * 2 + norm)
                    step(V.reciprocal(st[:, 2, 2:2 + TT], st[:, 2, 0:TT]))
                    settle()
                    for t in range(TT):
                        last = V.tensor_scalar(merged[:, t, :], x_sb[:, t, :], st[:, 2, 2 + t:3 + t], None, ALU.mult)
                    last.then_inc(xn_ready, 1)

                def mod_cols(norm, b):
                    a0 = (0 if norm == 1 else 3) * KD
                    step(V.tensor_tensor(modc[:, norm - 1, 1, :], b[:, 0:KD], col("adab", a0, KD), ALU.add))
                    V.tensor_tensor(modc[:, norm - 1, 0, :], b[:, KD:2 * KD], col("adab", a0 + KD, KD), ALU.add
                                    ).then_inc(v_evac, 1)
                    evacuated()
                    V.scalar_tensor_tensor(out=modc[:, norm - 1, 0, :], in0=modc[:, norm - 1, 0, :], scalar=1.0,
                                           in1=col(f"norm{norm}", 0, KD), op0=ALU.add, op1=ALU.mult
                                           ).then_inc(modc_ready, 1)
                    dve.wait_ge(modc_ready, l * 2 + norm)

                def modulate(norm):
                    for q in range(2, 4):
                        b = job(f"h{norm}_{q}")
                        for k in range(2):
                            kk = 2 * q + k
                            last = V.tensor_scalar(hT[:, kk, :], b[:, k * SEQ:k * SEQ + SEQ],
                                                   modc[:, norm - 1, 0, kk:kk + 1], modc[:, norm - 1, 1, kk:kk + 1],
                                                   ALU.mult, ALU.add)
                        last.then_inc(v_evac, 1)

                b = job(PCOL)
                V.tensor_copy(pcol[:, 0:PROWS], b[:, 0:PROWS]).then_inc(v_evac, 1)
                evacuated()
                dve.sem_inc(pcol_ready, 1)
                dve.wait_ge(cact_ready, l + 1)
                for n in range(4):
                    ada_chunk(n)
                mod_cols(1, job("modA"))
                norm_scale(1)
                modulate(1)

                def rotate(v, nh, half, freq_step, done):
                    x1, x2 = v[:, :, :, 0:half], v[:, :, :, half:2 * half]
                    sin = bcast(rope[:, 0, :, 0:AROT // 2:freq_step], 2, nh)
                    cos = bcast(rope[:, 1, :, 0:AROT // 2:freq_step], 2, nh)
                    tmp = [rt[:, i, 0:TT * nh, 0:half].rearrange("p (t h) f -> p t h f", t=TT) for i in range(4)]
                    step(V.tensor_tensor(tmp[0], x1, cos, ALU.mult))
                    step(V.tensor_tensor(tmp[1], x2, sin, ALU.mult))
                    step(V.tensor_tensor(tmp[2], x2, cos, ALU.mult))
                    step(V.tensor_tensor(tmp[3], x1, sin, ALU.mult))
                    settle()
                    step(V.tensor_tensor(x1, tmp[0], tmp[1], ALU.subtract))
                    last = V.tensor_tensor(x2, tmp[2], tmp[3], ALU.add)
                    if done is None:
                        step(last)
                        settle()
                    else:
                        last.then_inc(done, 1)

                dve.wait_ge(proj_evac, l * NPJ + 2 + 2)
                rotate(qik[:, :, :, :], IH + 1, IROT // 2, 2, None)
                V.tensor_copy(kirep[:, :, :, :], bcast(qik[:, :, IH, :], 2, 4)).then_inc(idx_rope, 1)
                dve.wait_ge(rows_in, (l + 1) * (6 * 16))
                r16 = lambda i: st[:, i, 0:16].rearrange("p (t h) -> p t h", t=TT)
                step(V.tensor_tensor(r16(6), wdt[:, :, IH:], bcast(mrow[:, 0, :], 1, TT), ALU.add))
                step(V.tensor_scalar(wdt[:, :, 0:IH], wdt[:, :, 0:IH], float(np.float32(IH ** -0.5 * ID ** -0.5)),
                                     None, ALU.mult))
                settle()
                step(V.tensor_scalar(st[:, 3, 0:16], st[:, 6, 0:16], -1.0, None, ALU.mult))
                settle()
                V.tensor_tensor(st[:, 3, 0:16], st[:, 3, 0:16], st[:, 6, 0:16], ALU.max).then_inc(dt_abs, 1)
                dve.wait_ge(dt_log, l + 1)
                step(V.tensor_scalar(st[:, 3, 0:16], st[:, 4, 0:16], 1.0, None, ALU.add))
                settle()
                step(V.tensor_scalar(st[:, 3, 0:16], st[:, 3, 0:16], 1.0, 1e-30, ALU.subtract, ALU.max))
                settle()
                step(V.reciprocal(st[:, 3, 0:16], st[:, 3, 0:16]))
                step(V.tensor_tensor(st[:, 5, 0:16], st[:, 5, 0:16], st[:, 4, 0:16], ALU.mult))
                settle()
                step(V.tensor_tensor(st[:, 5, 0:16], st[:, 5, 0:16], st[:, 3, 0:16], ALU.mult))
                settle()
                step(V.scalar_tensor_tensor(out=dtA[:, 0, :, :].rearrange("p t h -> p (t h)"), in0=st[:, 6, 0:16],
                                            scalar=0.0, in1=st[:, 5, 0:16], op0=ALU.max, op1=ALU.add))
                step(V.tensor_scalar(st[:, 7, 0:MH], st[:, 7, 0:MH], -1.0, None, ALU.mult))
                settle()
                V.tensor_tensor(dtA[:, 1, :, :], dtA[:, 0, :, :], bcast(st[:, 7, 0:MH], 1, TT), ALU.mult
                                ).then_inc(dt_ready, 1)

                dve.wait_ge(proj_evac, l * NPJ + 3 + 2)
                NQ = TT * (AH + AG)
                qk2 = qk[:, :, :, :].rearrange("p t h d -> p (t h) d")
                sq = scratch[:, 0:NQ * AD].rearrange("p (h d) -> p h d", d=AD)
                step(V.tensor_tensor(sq, qk2, qk2, ALU.mult))
                settle()
                step(V.tensor_reduce(st[:, 8, 0:NQ], sq, AX_X, ALU.add))
                settle()
                V.tensor_scalar(st[:, 8, 0:NQ], st[:, 8, 0:NQ], 1.0 / AD, EPS, ALU.mult, ALU.add).then_inc(qk_ss, 1)
                dve.wait_ge(qk_rs, l + 1)
                step(V.reciprocal(st[:, 9, 0:NQ], st[:, 9, 0:NQ]))
                settle()
                step(V.tensor_tensor(qk2, qk2, bcast(st[:, 9, 0:NQ], 2, AD), ALU.mult))
                settle()
                for t in range(TT):
                    step(V.tensor_tensor(qk[:, t, 0:AH, :], qk[:, t, 0:AH, :], bcast(gain[:, 0, :], 1, AH), ALU.mult))
                    step(V.tensor_tensor(qk[:, t, AH:, :], qk[:, t, AH:, :], bcast(gain[:, 1, :], 1, AG), ALU.mult))
                settle()
                rotate(qk[:, :, :, :], AH + AG, AROT // 2, 1, qk_roped)

                spans = [score[:, 0:P], score[:, P:3 * P]]
                masks = [mask[:, 0:P], mask[:, P:3 * P]]
                causal = [future[:, P:2 * P], future[:, :]]
                n = 0
                for t in range(TT):
                    ns = (t + 1) * P
                    for g in range(2):
                        for u in range(2):
                            dve.wait_ge(s_evac, l * NSJ + S_JOBS.index(f"dot{t}{g}{u}") + 1 + 2)
                            for q in range(2):
                                hd = 4 * g + 2 * u + q
                                prev = causal[t] if hd == 0 else spans[t]
                                ins = V.scalar_tensor_tensor(
                                    out=spans[t], in0=scratch[:, (n % 2) * W + q * ns:(n % 2) * W + (q + 1) * ns],
                                    scalar=wdt[:, t, hd:hd + 1], in1=prev, op0=ALU.mult, op1=ALU.add)
                                if q == 1:
                                    ins.then_inc(relu_used, 1)
                                    dve.wait_ge(relu_used, l * 8 + n + 1)
                                else:
                                    step(ins)
                                    settle()
                            n += 1
                arrive()
                for r in range(TOPK // 8):
                    for t in range(TT):
                        step(V.max(top8[:, t, :], spans[t]))
                    settle()
                    for t in range(TT):
                        step(V.match_replace(spans[t], top8[:, t, :], spans[t], TAKEN))
                    settle()
                for t in range(TT):
                    step(V.tensor_scalar(masks[t], spans[t], TAKEN / 2, -BIG, ALU.is_gt, ALU.mult))
                settle()
                for t in range(TT):
                    step(V.tensor_tensor(masks[t], masks[t], causal[t], ALU.add))
                dve.wait_ge(proj_evac, l * NPJ + PROJ_JOBS.index("xbc") + 1 + 2)
                for k in range(M_K):
                    for m in range(6):
                        tap, wk = xbc[:, m, k:k + SEQ], col("mcw", k * 6 + m)
                        if k == 0:
                            step(V.tensor_scalar(xbcT[:, m, :], tap, wk, None, ALU.mult))
                        else:
                            ins = V.scalar_tensor_tensor(out=xbcT[:, m, :], in0=tap, scalar=wk, in1=xbcT[:, m, :],
                                                         op0=ALU.mult, op1=ALU.add)
                            if k == M_K - 1 and m == 5:
                                ins.then_inc(conv_ready, 1)
                            else:
                                step(ins)
                    if k < M_K - 1:
                        settle()
                b = job("wsT")
                V.tensor_tensor(wsT[:, :, :], b[:, :].rearrange("p (g t) -> p g t", g=GG), bcast(tri[:, :], 1, GG),
                                ALU.mult).then_inc(v_evac, 1)
                dve.wait_ge(gv_ss, l + 1)
                V.tensor_scalar(st[:, 11, 0:TT], st[:, 10, 0:TT], 1.0 / W, EPS, ALU.mult, ALU.add).then_inc(gv_mean, 1)
                dve.wait_ge(gv_rs, l + 1)
                step(V.reciprocal(st[:, 12, 0:TT], st[:, 12, 0:TT]))
                settle()
                for t in range(TT):
                    last = V.tensor_scalar(gv[:, t, :], gv[:, t, :], st[:, 12, t:t + 1], None, ALU.mult)
                last.then_inc(gv_ready, 1)

                for t in range(TT):
                    lo, hi = (0, P) if t == 0 else (P, 3 * P)
                    for i in range(4):
                        b = job(f"lg{t}{i}")
                        settle()
                        arrive()
                        for u in range(2):
                            hd = i + 4 * u
                            ns = hi - lo
                            ins = V.tensor_tensor_reduce(P_sb[:, hd, lo:hi], b[:, u * ns:(u + 1) * ns], masks[t], 1.0,
                                                         -3e38, ALU.add, ALU.max, st[:, 13, t * 8 + hd:t * 8 + hd + 1])
                            if u == 1:
                                ins.then_inc(v_evac, 1)
                    evacuated()
                    V.tensor_scalar(st[:, 14 + t, 0:AH], st[:, 13, t * 8:t * 8 + 8], -AD ** -0.5, None, ALU.mult
                                    ).then_inc(max_ready, 1)
                for t in range(TT):
                    lo, hi = (0, P) if t == 0 else (P, 3 * P)
                    dve.wait_ge(exp_ready, l * 2 + t + 1)
                    step(V.reciprocal(st[:, 16 + t, 8:16], st[:, 16 + t, 0:8]))
                    settle()
                    for hd in range(AH):
                        last = V.tensor_scalar(P_sb[:, hd, lo:hi], P_sb[:, hd, lo:hi], st[:, 16 + t, 8 + hd:9 + hd],
                                               None, ALU.mult)
                        if t < TT - 1 or hd < AH - 1:
                            step(last)
                last.then_inc(p_ready, 1)

                b = job("acs")
                V.tensor_copy(acs[:, :, :, :].rearrange("p a c h -> p (a c h)"), b[:, 0:32]).then_inc(v_evac, 1)
                evacuated()
                step(V.tensor_tensor(dtA[:, 2, :, :], acs[:, 1, :, :], acs[:, 0, :, :], ALU.subtract))
                V.tensor_copy(dtA[:, 3, :, :], acs[:, 0, :, :]).then_inc(acs_ready, 1)
                for ch in range(TT):
                    V.tensor_tensor(scratch[:, ch * 1024:ch * 1024 + 1024].rearrange("p (h l) -> p h l", h=MH),
                                    bcast(dtA[:, 1, ch, :], 2, P), bcast(tri[:, :], 1, MH), ALU.mult
                                    ).then_inc(R_ready, 1)
                dve.wait_ge(s_evac, l * NSJ + S_JOBS.index("PV3") + 1 + 2)
                for ch in range(TT):
                    step(V.tensor_tensor(xdt[:, ch, :].rearrange("p (h q) -> p h q", h=MH),
                                         xs_tok[:, ch, :].rearrange("p (h q) -> p h q", h=MH),
                                         bcast(dtA[:, 0, ch, :], 2, MP), ALU.mult))
                settle()
                dve.wait_ge(decay_out, l + 1)
                V.tensor_tensor(xdtd[:, :].rearrange("p (h q) -> p h q", h=MH),
                                xdt[:, 0, :].rearrange("p (h q) -> p h q", h=MH),
                                bcast(dtA[:, 2, 0, :], 2, MP), ALU.mult).then_inc(ssd_in, 1)

                def decay(ch):
                    if ch:
                        dve.wait_ge(v_ready, l * NVR + V_PLAIN.index("y0") + 1)
                    for hh in range(2):
                        b = job(f"ab{ch}{hh}")
                        V.tensor_tensor(M_sb[:, 4 * hh:4 * hh + 4, :], b[:, :].rearrange("p (h l) -> p h l", h=4),
                                        bcast(acs[:, 0, ch, 4 * hh:4 * hh + 4], 2, P), ALU.subtract
                                        ).then_inc(v_evac, 1)
                    evacuated()
                    V.tensor_tensor(M_sb, M_sb, bcast(late[:, :], 1, MH), ALU.add).then_inc(diff_ready, 1)

                def weigh(ch):
                    dve.wait_ge(dec_exp, l * 2 + ch + 1)
                    dve.wait_ge(s_evac, l * NSJ + S_JOBS.index("scT") + 1 + 2)
                    for g in range(MG):
                        last = V.tensor_tensor(M_sb[:, 4 * g:4 * g + 4, :], M_sb[:, 4 * g:4 * g + 4, :],
                                               bcast(scT[:, ch, g, :], 1, 4), ALU.mult)
                        if g == 0:
                            step(last)
                    last.then_inc(M_ready, 1)

                def skip_y(ch):
                    b = job(f"y{ch}")
                    V.tensor_tensor(y_sb[:, ch, :], y_sb[:, ch, :], b[:, :], ALU.add).then_inc(v_evac, 1)
                    evacuated()

                decay(0)
                for ch in range(TT):
                    step(V.tensor_tensor(y_sb[:, ch, :].rearrange("p (h q) -> p h q", h=MH),
                                         xs_tok[:, ch, :].rearrange("p (h q) -> p h q", h=MH),
                                         bcast(mrow[:, 2, :], 2, MP), ALU.mult))
                weigh(0)
                settle()
                skip_y(0)
                decay(1)
                dve.wait_ge(proj_evac, l * NPJ + PROJ_JOBS.index("scx") + 1 + 2)
                step(V.memset(cx[:, :, 0:2], 0.0))
                step(V.tensor_tensor(cx[:, :, 2:], cx[:, :, 2:], scc, ALU.mult))
                settle()
                for k in range(SC_K):
                    for m in range(CT):
                        tap, wk = cx[:, m, k:k + SEQ], col("scw", k * CT + m)
                        if k == 0:
                            step(V.tensor_scalar(oT[:, 1, m, :], tap, wk, None, ALU.mult))
                        else:
                            step(V.scalar_tensor_tensor(out=oT[:, 1, m, :], in0=tap, scalar=wk, in1=oT[:, 1, m, :],
                                                        op0=ALU.mult, op1=ALU.add))
                    settle()
                weigh(1)
                b = job("yoff")
                yo = scratch[:, 0:W]
                V.tensor_tensor(yo.rearrange("p (h q) -> p h q", h=MH), b[:, :].rearrange("p (h q) -> p h q", h=MH),
                                bcast(dtA[:, 3, 1, :], 2, MP), ALU.mult).then_inc(v_evac, 1)
                evacuated()
                step(V.tensor_tensor(y_sb[:, 1, :], y_sb[:, 1, :], yo, ALU.add))
                settle()
                skip_y(1)
                dve.wait_ge(proj_evac, l * NPJ + PROJ_JOBS.index("z") + 1 + 2)
                step(V.tensor_tensor(y_sb, y_sb, z_sb[:, :, :], ALU.mult))
                settle()
                for t in range(TT):
                    step(V.tensor_tensor_reduce(scratch[:, t * W:t * W + W], y_sb[:, t, :], y_sb[:, t, :], 1.0, 0.0,
                                                ALU.mult, ALU.add, st[:, 19, 8 + t:9 + t]))
                settle()
                V.tensor_scalar(st[:, 19, 0:TT], st[:, 19, 8:8 + TT], 1.0 / W, EPS, ALU.mult, ALU.add
                                ).then_inc(y_ss, 1)
                dve.wait_ge(proj_evac, l * NPJ + PROJ_JOBS.index("scb") + 1 + 2)
                V.tensor_tensor(oT[:, 1, :, :], oT[:, 1, :, :], scb, ALU.mult).then_inc(ob_ready, 1)
                dve.wait_ge(y_rs, l + 1)
                step(V.reciprocal(st[:, 20, 0:TT], st[:, 20, 0:TT]))
                settle()
                for t in range(TT):
                    last = V.tensor_scalar(y_sb[:, t, :], y_sb[:, t, :], st[:, 20, t:t + 1], None, ALU.mult)
                last.then_inc(od_ready, 1)
                dve.wait_ge(proj_evac, l * NPJ + PROJ_JOBS.index("gu") + 1 + 2)
                for q in range(2):
                    b = job(f"mix{q}")
                    for g in range(2):
                        m = 2 * q + g
                        last = V.scalar_tensor_tensor(
                            out=oT[:, 2, m, :].rearrange("p (c t) -> p c t", c=TT),
                            in0=b[:, g * SEQ:g * SEQ + SEQ].rearrange("p (c t) -> p c t", c=TT),
                            scalar=col("gvg", m), in1=bcast(gsb[:, m, :], 1, TT), op0=ALU.mult, op1=ALU.add)
                    last.then_inc(v_evac, 1)
                evacuated()
                V.tensor_tensor(oT[:, 2, :, :], oT[:, 2, :, :], uT[:, :, :], ALU.mult).then_inc(oc_ready, 1)

                for n, i in enumerate(BRANCH_ORDER):
                    for j in range(2):
                        dve.wait_ge(proj_evac, l * NPJ + PROJ_JOBS.index(f"g{i}{j}") + 1 + 2)
                        for t in range(TT):
                            b = job(f"b{i}{j}{t}")
                            part = merged[:, t, j * W:j * W + W]
                            if n == 0:
                                V.tensor_tensor(part, gsig[j][:, t, :], b[:, :], ALU.mult).then_inc(v_evac, 1)
                            else:
                                V.tensor_tensor(gsig[j][:, t, :], gsig[j][:, t, :], b[:, :], ALU.mult
                                                ).then_inc(v_evac, 1)
                        evacuated()
                        if n == 0:
                            dve.sem_inc(gsig_used, 1)
                            continue
                        for t in range(TT):
                            part = merged[:, t, j * W:j * W + W]
                            last = V.tensor_tensor(part, part, gsig[j][:, t, :], ALU.add)
                            if t == 0:
                                step(last)
                        last.then_inc(gsig_used, 1)
                        dve.wait_ge(gsig_used, l * 8 + 2 * n + j + 1)
                dve.sem_inc(merged_ready, 1)
                dve.wait_ge(gateb_in, (l + 1) * 32)

                def gate_row(i, j):
                    b = job(f"gate{i + 1}{j}")
                    V.tensor_tensor(gate_bc[:, i, j * W:j * W + W], gate_bc[:, i, j * W:j * W + W], b[:, :], ALU.add
                                    ).then_inc(v_evac, 1)

                ada_chunk(4)
                ada_chunk(5)
                gate_row(0, 0)
                gate_row(0, 1)
                for n in range(6, 10):
                    ada_chunk(n)
                mod_cols(2, job("modB"))
                ada_chunk(10)
                ada_chunk(11)
                gate_row(1, 0)
                gate_row(1, 1)
                for j in range(2):
                    for t in range(TT):
                        b = job(f"o{j}{t}")
                        V.tensor_tensor(merged[:, t, j * W:j * W + W], b[:, :], gate_bc[:, 0, j * W:j * W + W],
                                        ALU.mult).then_inc(v_evac, 1)
                evacuated()
                V.tensor_tensor(x_sb[:, :, :], x_sb[:, :, :], merged, ALU.add).then_inc(x_mid, 1)
                norm_scale(2)
                modulate(2)

                R = lambda i: rt1[:, i, :, :]
                G = lambda i: rt1[:, i, :, :].rearrange("p t (g k) -> p t g k", g=EG)
                LG = lambda i: rt1[:, i, :, 0:EG]

                def op(out_, a, b_, o):
                    step(V.tensor_tensor(out_, a, b_, o))

                b = job("router")
                V.tensor_copy(R(0), b[:, 0:TT * NE].rearrange("p (t e) -> p t e", t=TT)).then_inc(v_evac, 1)
                if "pad" in V_JOBS:
                    seen[0] += 1
                    dve.wait_ge(v_evac, l * NVJ + NVJ - 1 + 2)
                    dve.sem_inc(v_evac, 1)
                evacuated()
                dve.sem_inc(logit_ready, 1)
                dve.wait_ge(sig_ready, l + 1)
                op(R(1), R(0), bcast(rbias[:, :], 1, TT), ALU.add)
                settle()
                op(rt1[:, 2, :, 0:2 * EG].rearrange("p t (g k) -> p t g k", g=EG), G(1)[:, :, :, 0:2], G(1)[:, :, :, 2:4],
                   ALU.max)
                op(rt1[:, 3, :, 0:2 * EG].rearrange("p t (g k) -> p t g k", g=EG), G(1)[:, :, :, 0:2], G(1)[:, :, :, 2:4],
                   ALU.min)
                settle()
                hi = rt1[:, 2, :, 0:2 * EG].rearrange("p t (g k) -> p t g k", g=EG)
                lo = rt1[:, 3, :, 0:2 * EG].rearrange("p t (g k) -> p t g k", g=EG)
                op(LG(4), hi[:, :, :, 0], hi[:, :, :, 1], ALU.max)
                op(LG(5), hi[:, :, :, 0], hi[:, :, :, 1], ALU.min)
                op(LG(6), lo[:, :, :, 0], lo[:, :, :, 1], ALU.max)
                settle()
                op(LG(5), LG(5), LG(6), ALU.max)
                settle()
                op(LG(4), LG(4), LG(5), ALU.add)
                settle()

                def first_of(val, n_, rank, tmp, dst):
                    step(V.tensor_reduce(rt1[:, tmp, :, 0], val, AX_X, ALU.max))
                    settle()
                    op(dst, val, bcast(rt1[:, tmp, :, 0], 2, n_), ALU.is_equal)
                    settle()
                    op(dst, dst, bcast(rank[:, 0:n_], 1, TT), ALU.mult)
                    settle()
                    step(V.tensor_reduce(rt1[:, tmp, :, 1], dst, AX_X, ALU.max))
                    settle()
                    op(dst, dst, bcast(rt1[:, tmp, :, 1], 2, n_), ALU.is_equal)
                    settle()

                first_of(LG(4), EG, rank, 6, LG(5))
                step(V.tensor_scalar(LG(5), LG(5), 1.0, BIG, ALU.subtract, ALU.mult))
                settle()
                op(G(2), G(1), bcast(LG(5), 3, EPG), ALU.add)
                settle()
                first_of(R(2), NE, rank, 6, R(3))
                step(V.scalar_tensor_tensor(out=R(4), in0=R(3), scalar=-2 * BIG, in1=R(2), op0=ALU.mult, op1=ALU.add))
                settle()
                first_of(R(4), NE, rank, 6, R(5))
                op(R(3), R(3), R(5), ALU.add)
                settle()
                op(R(3), R(3), R(0), ALU.mult)
                settle()
                step(V.tensor_reduce(rt1[:, 6, :, 0], R(3), AX_X, ALU.add))
                settle()
                step(V.reciprocal(rt1[:, 6, :, 1], rt1[:, 6, :, 0]))
                settle()
                op(comb[:, :, :], R(3), bcast(rt1[:, 6, :, 1], 2, NE), ALU.mult)
                settle()
                dve.sem_clear(dve_step)
                count[0] = 0

                def hidden(read, e):
                    dve.wait_ge(silu_done, l * NE + e + 1)
                    dve.wait_ge(units_read, l * UNITS_L + MOE0 + read + RING)
                    V.tensor_tensor(hid.rearrange("p (b m) s -> p b (m s)", b=2),
                                    sg.rearrange("p (b m) s -> p b (m s)", b=2), bank[:, 2:4, :], ALU.mult
                                    ).then_inc(hid_ready, 1)

                def add_expert(read, e):
                    V.tensor_copy(cw[:, :], comb[:, :, bass.ds(e, 1)].rearrange("p t o -> p (t o)")
                                  ).then_inc(moe_step, 1)
                    dve.wait_ge(moe_step, 1)
                    dve.wait_ge(units_read, l * UNITS_L + MOE0 + read + RING)
                    for t in range(TT):
                        o = merged[:, t, :].rearrange("p (b n) -> p b n", b=2)
                        last = V.scalar_tensor_tensor(out=o, in0=bank[:, 4 + 2 * t:6 + 2 * t, :],
                                                      scalar=cw[:, t:t + 1], in1=o, op0=ALU.mult, op1=ALU.add)
                    last.then_inc(down_used, 1)
                    dve.wait_ge(down_used, l * NE + e + 2)
                    dve.sem_inc(moe_step, 1)
                    dve.sem_clear(moe_step)

                V.memset(scratch[:, :], 0.0).then_inc(moe_step, 1)
                dve.wait_ge(moe_step, 1)
                dve.sem_clear(moe_step)
                hidden(4, 0)
                with dve.Fori(1, NE) as e:
                    add_expert(PER_E * e + 2, e - 1)
                    hidden(PER_E * e + 4, e)
                add_expert(PER_E * NE, NE - 1)
                for t in range(TT):
                    step(V.tensor_tensor(merged[:, t, :], merged[:, t, :], gate_bc[:, 1, :], ALU.mult))
                settle()
                V.tensor_tensor(x_sb[:, :, :], x_sb[:, :, :], merged, ALU.add).then_inc(layer_done, 1)
                dve.wait_ge(layer_done, l + 2)
                arrive()
                dve.sem_clear(dve_step)
                count[0] = 0


_INS = ["x", "c", "positions", "ada_w", "ada_b", "norm1_g", "w_in", "q_norm_g", "k_norm_g", "sc_conv_w",
        "g_v_norm_g", "g_spatial_w", "g_spatial_b", "m_conv_w", "m_conv_b", "m_dt_bias", "m_a_log", "m_d",
        "m_norm_g", "w_branch", "w_out", "norm2_g", "router_w", "router_bias", "exp_w_gate", "exp_w_up",
        "exp_w_down"]


def kernel(**inputs):
    import concourse.bacc as bacc
    from concourse.bass_utils import run_bass_kernel_spmd

    nc = bacc.Bacc("TRN2", target_bir_lowering=False, num_devices=1)
    arrays, args = {}, []
    for name in _INS:
        a = np.ascontiguousarray(inputs[name])
        arrays[f"in_{name}"] = a
        args.append(nc.dram_tensor(f"in_{name}", a.shape, mybir.dt.from_np(a.dtype), kind="ExternalInput").ap())
    out = nc.dram_tensor("out", (1, SEQ, D_MODEL), F32, kind="ExternalOutput").ap()
    hybrid_trunk(nc, *args, out)
    r = run_bass_kernel_spmd(nc, [arrays], core_ids=[0])
    return r.results[0]["out"]
```

```python
import math
from contextlib import ExitStack

import numpy as np

import concourse.bass as bass
from concourse import mybir

F32 = mybir.dt.float32
F32R = mybir.dt.float32r
I32 = mybir.dt.int32
ALU = mybir.AluOpType
ACT = mybir.ActivationFunctionType
AX_X = mybir.AxisListType.X

P = 128
D_MODEL, SEQ, DEPTH = 1024, 256, 2
TT = SEQ // P
KD = D_MODEL // P
W = 512
HK = KD // 2
EPS = 1e-6
ROPE_THETA = 500000.0
AH, AG, AD, AROT = 8, 2, 64, 16
IH, ID, IROT = 8, 32, 8
TOPK = 64
SC_K, M_K = 3, 4
GG, MH, MP, MG, MN = 4, 8, 64, 2, 64
NE, EG, EPG, FF = 16, 4, 4, 512
CT = W // P
NB = 4

CQ, CK, CV, CQI, CKI, CWI = 0, 512, 640, 768, 1024, 1056
CSB, CSC, CSX, CGU, CGV, CZ, CXBC, CDT, CG = 1064, 1576, 2088, 2600, 3112, 3624, 4136, 4904, 4912
SMALL = AG * AD * 2 + ID + IH + MH
BRANCH_ORDER = (1, 2, 0, 3)

PR = {}
PROWS = 0
for _name, _n in (("norm1", KD), ("norm2", KD), ("adab", 6 * KD), ("scw", SC_K * CT), ("gvg", CT),
                  ("mcw", M_K * 6), ("mcb", 6), ("mng", CT)):
    PR[_name] = PROWS
    PROWS += _n

BIG = 1e30
FILLS = 5 + AROT // 2 + NE + 5
TAKEN = -3e38

RING = 6
HIGHS = 3
UNITS = [(n, h) for n in ("C", "B", "A", "xbc", "gv", "z", "gu", "scc", "scx", "scb") for h in range(2)]
for _i in BRANCH_ORDER:
    for _j in range(2):
        UNITS += [(f"g{_i}{_j}", 0), (f"g{_i}{_j}", 1), (f"b{_i}{_j}", 0)]
UNITS += [("o0", 0), ("o0", 1), ("o1", 0), ("o1", 1)]
MOE0 = len(UNITS)
PER_E = 6
UNITS_L = MOE0 + NE * PER_E
assert MOE0 % RING == 0 and PER_E == RING
PARTS = [3 if n == "B" else 2 if n == "C" or n[:2] == "b0" else 1 for n, _ in UNITS]
LANDED = [sum(PARTS[m] for m in range(n % RING, n + 1, RING)) for n in range(MOE0)]
SLOT_MIX = [sum(PARTS[m] for m in range(s, MOE0, RING)) for s in range(RING)]
SLOT_L = [SLOT_MIX[s] + NE for s in range(RING)]

PROJ_JOBS = ["C", "B", "A", "xbc", "gv", "z", "gu", "scc", "scx", "scb"]
PROJ_JOBS += [f"g{i}{j}" for i in BRANCH_ORDER for j in range(2)]
S_JOBS = ["h1_0", "h1_1", "qiT", "kiT"]
S_JOBS += [f"dot{t}{g}{u}" for t in range(TT) for g in range(2) for u in range(2)]
S_JOBS += ["qT0", "qT1", "kT", "xs0", "xs1", "Bt"]
S_JOBS += [x for i in range(4) for x in (f"PT{i}a", f"PT{i}b", f"PV{i}")]
S_JOBS += ["scT", "states", "odT0", "odT1", "mT0", "mT1", "mT2", "mT3", "h2_0", "h2_1"]
V_JOBS = ["h1_2", "h1_3", "wsT"]
V_JOBS += [f"lg{t}{i}" for t in range(TT) for i in range(4)]
V_JOBS += ["acs", "ab00", "ab01", "y0", "ab10", "ab11", "yoff", "y1", "mix0", "mix1"]
CHUNKS = [4, 5, 6, 7, 8, 9, 10, 11, 0, 1, 2, 3]
GATE_STEPS = [(i, j) for i in BRANCH_ORDER for j in range(2)]
V_JOBS_OF_STEP = {1: ["gate10", "gate11"], 2: ["mod67"], 3: ["mod89"], 4: ["gate20", "gate21"], 5: ["mod01"],
                  6: ["mod23"]}
for _n, (_i, _j) in enumerate(GATE_STEPS):
    V_JOBS += [f"b{_i}{_j}{t}" for t in range(TT)] + V_JOBS_OF_STEP.get(_n, [])
V_JOBS += [f"o{j}{t}" for j in range(2) for t in range(TT)]
V_JOBS += ["h2_2", "h2_3", "router", "pad"]
PCOL = "pcol"
V_JOBS = [PCOL] + V_JOBS
if len(V_JOBS) % 2:
    V_JOBS.remove("pad")
assert len(PROJ_JOBS) % 2 == 0 and len(S_JOBS) % 2 == 0 and len(V_JOBS) % 2 == 0
BY_UNIT = {f"b{i}{j}1": UNITS.index((f"b{i}{j}", 0)) for i in BRANCH_ORDER for j in range(2)}
BY_UNIT |= {f"o{j}{t}": UNITS.index((f"o{j}", 1)) for j in range(2) for t in range(TT)}
BY_CHUNK = {"gate10": 0, "gate11": 1, "mod67": 3, "mod89": 5, "gate20": 6, "gate21": 7, "mod01": 9, "mod23": 11}
V_PLAIN = [n for n in V_JOBS if n not in BY_UNIT and n not in BY_CHUNK and n != "pad"]
NVR = len(V_PLAIN)
NPJ, NSJ, NVJ = len(PROJ_JOBS), len(S_JOBS), len(V_JOBS)
MOD_CHUNKS = 6 * D_MODEL // W
ADA_0 = 4


def bcast(ap, axis, n):
    a = ap.unsqueeze(axis)
    shape = list(a.shape)
    shape[axis] = n
    return a.to_broadcast(shape)


def hybrid_trunk(nc, x, c, positions, ada_w, ada_b, norm1_g, w_in, q_norm_g, k_norm_g, sc_conv_w,
                 g_v_norm_g, g_spatial_w, g_spatial_b, m_conv_w, m_conv_b, m_dt_bias, m_a_log, m_d,
                 m_norm_g, w_branch, w_out, norm2_g, router_w, router_bias, exp_w_gate, exp_w_up,
                 exp_w_down, out):
    ctx = ExitStack()
    with ctx:
        place = {}

        def sb(name, shape, dt=F32):
            place[name] = (nc.sbuf_base + 31) // 32 * 32
            return ctx.enter_context(nc.sbuf_tensor(name, [P] + shape, dt))

        def part_of(whole, name, word, shape):
            return nc.alloc_sbuf_tensor_at(name, [P] + shape, F32R, offset=place[whole] + 4 * word)

        def sem(name):
            return ctx.enter_context(nc.semaphore(name))

        bank = ctx.enter_context(nc.psum_tensor("bank", [P, 8, W], F32))

        ring = sb("ring", [RING, HK, W])
        ada_buf = sb("ada_buf", [2, 2, W])
        x_sb = sb("x_sb", [TT, D_MODEL])
        hT = sb("hT", [KD, SEQ])
        scratch = sb("scratch", [TT * D_MODEL])
        merged = scratch[:, :].rearrange("p (t d) -> p t d", t=TT)
        gate_bc = sb("gate_bc", [2, D_MODEL])
        ada_acc = sb("ada_acc", [2, W])
        ident = sb("ident", [P])
        tri = sb("tri", [P])
        late = sb("late", [P])
        future = sb("future", [SEQ])
        ones = sb("ones", [P])
        invf = sb("invf", [AROT // 2])
        prow = sb("prow", [P])
        c_raw = sb("c_raw", [KD])
        mod_sum = sb("mod_sum", [2, 2 * KD])
        pcol = sb("pcol", [P])
        cact = sb("cact", [KD])
        gain = sb("gain", [2, AD])
        mrow = sb("mrow", [3, MH])
        gsb = sb("gsb", [GG, P])
        rbias = sb("rbias", [NE])
        rw = sb("rw", [KD, NE])
        wsraw = sb("wsraw", [GG, P])
        wsT = sb("wsT", [GG, P])
        pos_i = sb("pos_i", [TT], I32)
        pos_f = sb("pos_f", [TT])
        rope = sb("rope", [2, TT, AROT // 2])
        ang = sb("ang", [2, TT, AROT // 2])
        turns = sb("turns", [2, TT, AROT // 2])
        st = sb("st", [21, 32])
        modc = sb("modc", [2, 2, KD])
        qk = sb("qk", [TT, AH + AG, AD])
        xs_tok = qk[:, :, :, :].rearrange("p t h d -> p (t h d)")[:, 0:TT * W].rearrange(
            "p (t d) -> p t d", t=TT)
        qik = sb("qik", [TT, IH + 1, ID])
        kirep = sb("kirep", [TT, 4, ID])
        wdt = sb("wdt", [TT, IH + MH])
        v_sb = sb("v_sb", [TT, AG * AD])
        qiT = sb("qiT", [2, SEQ])
        bd_qt = sb("bd_qt", [2, 4, SEQ])
        kiTd = bd_qt[:, 0, :, :]
        qT = bd_qt[:, 1, :, :]
        kTd = sb("kTd", [AG, SEQ])
        score = sb("score", [3 * P])
        top8 = sb("top8", [TT, 8])
        mask = sb("mask", [3 * P])
        P_sb = sb("P_sb", [AH, 3 * P])
        p_flat = P_sb[:, :, :].rearrange("p h s -> p (h s)")
        M_sb = p_flat[:, 0:1024].rearrange("p (h l) -> p h l", h=MH)
        y_sb = p_flat[:, 1024:2048].rearrange("p (t d) -> p t d", t=TT)
        xdt = p_flat[:, 2048:3072].rearrange("p (t d) -> p t d", t=TT)
        PT = sb("PT", [AH * 3 * P + 8])
        ada_place = [ada_buf[:, 0, :, :], ada_buf[:, 1, :, :]] + [
            PT[:, i * 2 * W:(i + 1) * 2 * W].rearrange("p (k n) -> p k n", k=2) for i in range(2)]
        scc = PT[:, 0:CT * SEQ].rearrange("p (m s) -> p m s", m=CT)
        cx = PT[:, CT * SEQ:CT * SEQ + CT * (SEQ + 2)].rearrange("p (m s) -> p m s", m=CT)
        scb = PT[:, CT * (2 * SEQ + 2):CT * (3 * SEQ + 2)].rearrange("p (m s) -> p m s", m=CT)
        oT = sb("oT", [NB, CT, SEQ])
        xbc = sb("xbc", [6, SEQ + M_K - 1])
        xbcT = sb("xbcT", [6, SEQ])
        Btok = sb("Btok", [P])
        CTd = sb("CTd", [MG, SEQ])
        dtA = sb("dtA", [4, TT, MH])
        acs = sb("acs", [2, TT, MH])
        xdtd = sb("xdtd", [W])
        zgv = sb("zgv", [2 * TT * W])
        z_sb = zgv[:, 0:TT * W].rearrange("p (t d) -> p t d", t=TT)
        gv = zgv[:, TT * W:].rearrange("p (t d) -> p t d", t=TT)
        rt = zgv[:, 0:4 * TT * (AH + AG) * AROT // 2].rearrange(
            "p (i h f) -> p i h f", i=4, f=AROT // 2)
        prevd = sb("prevd", [W])
        scT = sb("scT", [TT, MG, P])
        uT = sb("uT", [CT, SEQ])
        gsig = [qT.rearrange("p i s -> p (i s)").rearrange("p (t n) -> p t n", t=TT), gv]
        rt1 = sb("rt1", [7, TT, NE])
        comb = sb("comb", [TT, NE])
        cw = sb("cw", [TT])
        rank = sb("rank", [NE])
        sg = p_flat[:, 0:1024].rearrange("p (m s) -> p m s", m=CT)
        hid = p_flat[:, 1024:2048].rearrange("p (m s) -> p m s", m=CT)

        w_low = part_of("ring", "w_low", 0, [RING, HK, W])
        w_high = [part_of("oT", "w_high0", 0, [HK, W]), part_of("oT", "w_high1", HK * W, [HK, W]),
                  part_of("PT", "w_high2", 0, [HK, W])]
        h_low, h_high = part_of("hT", "h_low", 0, [KD, SEQ]), part_of("zgv", "h_high", 0, [KD, SEQ])
        hid_low = part_of("P_sb", "hid_low", 1024, [CT, SEQ])
        hid_high = part_of("P_sb", "hid_high", 2048, [CT, SEQ])

        slot_loaded = [sem(f"slot_loaded{s}") for s in range(RING)]
        units_read = sem("units_read")
        unit_turn = sem("unit_turn")
        ada_loaded = [sem(f"ada_loaded{s}") for s in range(4)]
        ada_freed = sem("ada_freed")
        c_in = sem("c_in")
        acc_ready, acc_used = sem("acc_ready"), sem("acc_used")
        proj_evac = sem("proj_evac")
        s_ready, s_evac = sem("s_ready"), sem("s_evac")
        v_ready, v_evac = sem("v_ready"), sem("v_evac")
        consts, x_in, pos_in, rw_in = sem("consts"), sem("x_in"), sem("pos_in"), sem("rw_in")
        prow_in, wsraw_in, rows_in, gateb_in = sem("prow_in"), sem("wsraw_in"), sem("rows_in"), sem("gateb_in")
        dve_step, moe_step, CTd_ready = sem("dve_step"), sem("moe_step"), sem("CTd_ready")
        angles_ready, rope_ready = sem("angles_ready"), sem("rope_ready")
        pcol_ready, cact_ready = sem("pcol_ready"), sem("cact_ready")
        ss_ready, mean_ready, rs_ready = sem("ss_ready"), sem("mean_ready"), sem("rs_ready")
        xn_ready, modc_ready = sem("xn_ready"), sem("modc_ready")
        idx_rope, qk_ss, qk_rs, qk_roped = sem("idx_rope"), sem("qk_ss"), sem("qk_rs"), sem("qk_roped")
        dt_abs, dt_exp, dt_log, dt_ready = sem("dt_abs"), sem("dt_exp"), sem("dt_log"), sem("dt_ready")
        relu_used, mask_ready = sem("relu_used"), sem("mask_ready")
        max_ready, exp_ready, p_ready = sem("max_ready"), sem("exp_ready"), sem("p_ready")
        conv_ready, silu_ready = sem("conv_ready"), sem("silu_ready")
        ssd_in, acs_ready, R_ready, dec_exp, diff_ready = (
            sem("ssd_in"), sem("acs_ready"), sem("R_ready"), sem("dec_exp"), sem("diff_ready"))
        decay_in, decay_out, M_ready = sem("decay_in"), sem("decay_out"), sem("M_ready")
        y_ready, y_ss, y_rs, od_ready = sem("y_ready"), sem("y_ss"), sem("y_rs"), sem("od_ready")
        gv_ss, gv_mean, gv_rs, gv_ready = sem("gv_ss"), sem("gv_mean"), sem("gv_rs"), sem("gv_ready")
        oc_ready, ob_ready, gsig_used, merged_ready = (
            sem("oc_ready"), sem("ob_ready"), sem("gsig_used"), sem("merged_ready"))
        mod0_read = sem("mod0_read")
        x_mid, logit_ready, sig_ready, comb_ready = sem("x_mid"), sem("logit_ready"), sem("sig_ready"), sem("comb_ready")
        silu_done, hid_ready, down_used = sem("silu_done"), sem("hid_ready"), sem("down_used")
        w_rounded, w_split = sem("w_rounded"), sem("w_split")
        h_rounded, h_split = sem("h_rounded"), sem("h_split")
        hid_made, hid_rounded = sem("hid_made"), sem("hid_rounded")
        layer_done, stored = sem("layer_done"), sem("stored")

        def ps(name):
            if name in S_JOBS:
                return bank[:, 6 + S_JOBS.index(name) % 2, :]
            return bank[:, 4 + V_JOBS.index(name) % 2, :]

        def pj(name):
            b = 2 * (PROJ_JOBS.index(name) % 2)
            return bank[:, b:b + 2, :]

        block = ctx.enter_context(nc.Block())

        @block.sync
        def _(sp):
            w_in_v = w_in.rearrange("l (k p) n -> l p k n", p=P)
            w_br_v = w_branch.rearrange("l b (k p) n -> l b p k n", p=P)
            w_a_v = w_branch.rearrange("l b (g k p) n -> l b g p k n", g=AG, p=AD)
            w_out_v = w_out.rearrange("l (k p) n -> l p k n", p=P)
            wg_v = exp_w_gate.rearrange("l e (k p) n -> (l e) p k n", p=P)
            wu_v = exp_w_up.rearrange("l e (k p) n -> (l e) p k n", p=P)
            wd_v = exp_w_down.rearrange("l e (k p) n -> (l e) p k n", p=P)
            start = {"A": CQ, "xbc": CXBC, "gv": CGV, "z": CZ, "gu": CGU, "scc": CSC, "scx": CSX, "scb": CSB}

            sp.sem_inc(units_read, RING)
            sp.dma_start(x_sb[:, :, :], x[0].rearrange("(t p) d -> p t d", p=P)).then_inc(x_in, 16)
            with sp.Fori(0, DEPTH) as l:
                def load(n, src, dst=None):
                    s = n % RING
                    dst = ring[:, s, :, :] if dst is None else dst
                    sp.dma_start(dst, src).then_inc(slot_loaded[s], 16)

                for n, (name, h) in enumerate(UNITS):
                    s = n % RING
                    ks = slice(HK * h, HK * h + HK)
                    sp.wait_ge(units_read, l * UNITS_L + n + 1)
                    sp.sem_inc(unit_turn, 1)
                    if name == "C":
                        load(n, w_in_v[l, :, ks, CQI:CQI + 256], ring[:, s, :, 0:256])
                        load(n, w_in_v[l, :, ks, CXBC + W:CXBC + W + 256], ring[:, s, :, 256:512])
                    elif name == "B":
                        load(n, w_in_v[l, :, ks, CK:CK + 256], ring[:, s, :, 0:256])
                        load(n, w_in_v[l, :, ks, CKI:CKI + ID + IH], ring[:, s, :, 256:256 + ID + IH])
                        load(n, w_in_v[l, :, ks, CDT:CDT + MH], ring[:, s, :, 256 + ID + IH:SMALL])
                    elif name in start:
                        load(n, w_in_v[l, :, ks, start[name]:start[name] + W])
                    elif name[0] == "g":
                        c0 = CG + int(name[1]) * D_MODEL + int(name[2]) * W
                        load(n, w_in_v[l, :, ks, c0:c0 + W])
                    elif name[0:2] == "b0":
                        for g in range(AG):
                            load(n, w_a_v[l, 0, g, :, :, int(name[2]) * W:int(name[2]) * W + W],
                                 ring[AD * g:AD * g + AD, s, :, :])
                    elif name[0] == "b":
                        load(n, w_br_v[l, int(name[1]), :, :, int(name[2]) * W:int(name[2]) * W + W])
                    else:
                        load(n, w_out_v[l, :, ks, int(name[1]) * W:int(name[1]) * W + W])

                def gate_up(n, slot, view, e):
                    for h in range(2):
                        sp.wait_ge(units_read, l * UNITS_L + n + h + 1)
                        load(slot + h, view[e, :, HK * h:HK * h + HK, :])

                def down(n, slot, e):
                    for j in range(2):
                        sp.wait_ge(units_read, l * UNITS_L + n + j + 1)
                        load(slot + j, wd_v[e, :, :, j * W:j * W + W])

                first = sp.snap(l * NE)
                gate_up(MOE0, 0, wg_v, first)
                gate_up(MOE0 + 2, 2, wu_v, first)
                with sp.Fori(1, NE) as e:
                    n = MOE0 + 4 + (e - 1) * PER_E
                    this = sp.snap(l * NE + e)
                    last = sp.snap(l * NE + e - 1)
                    gate_up(n, 4, wg_v, this)
                    down(n + 2, 0, last)
                    gate_up(n + 4, 2, wu_v, this)
                down(UNITS_L - 2, 4, sp.snap(l * NE + NE - 1))
            sp.wait_ge(layer_done, DEPTH + 1)
            sp.dma_start(out[0].rearrange("(t p) d -> p t d", p=P), x_sb[:, :, :]).then_inc(stored, 16)
            sp.wait_ge(stored, 16)

        @block.gpsimd
        def _(pool):
            pool.dma_start(c_raw[:, :], c[0].rearrange("(k p) -> p k", p=P),
                           allow_slow_non_contiguous=True).then_inc(c_in, 16)
            ada_v = ada_w.rearrange("l (k p) n -> l p k n", p=P)
            pool.sem_inc(ada_freed, 4)

            def ada(layer, chunk, at):
                for q in range(4):
                    pool.wait_ge(ada_freed, 4 * at + q + 1)
                    pool.dma_start(ada_place[q], ada_v[layer, :, 2 * q:2 * q + 2, chunk * W:chunk * W + W]
                                   ).then_inc(ada_loaded[q], 16)

            ada(0, 0, 0)
            pool.dma_start(pos_i[:, :], positions[0].rearrange("(t p) -> p t", p=P),
                           allow_slow_non_contiguous=True).then_inc(pos_in, 16)
            pool.dma_start(rw[:, :, :], router_w.rearrange("(k p) e -> p k e", p=P)).then_inc(rw_in, 16)
            pool.dma_start(rbias[:, :], router_bias.partition_broadcast(P)).then_inc(rw_in, 16)
            for tile, val in ((ident, 0.0), (tri, 1.0), (late, 0.0), (future, 0.0), (ones, 1.0)):
                pool.memset(tile[:, :], val).then_inc(consts, 1)
            for f in range(AROT // 2):
                val = float(np.exp(np.float32(-math.log(ROPE_THETA)) * np.float32(f) * np.float32(2.0)
                                   / np.float32(AROT)))
                pool.memset(invf[:, f:f + 1], val).then_inc(consts, 1)
            for f in range(NE):
                pool.memset(rank[:, f:f + 1], float(NE - f)).then_inc(consts, 1)
            for tile in (bd_qt[:, 0, :, :], kTd[:, :, :], CTd[:, :, :], prevd[:, :], xbc[:, :, 0:M_K - 1]):
                pool.memset(tile, 0.0).then_inc(consts, 1)
            assert 5 + AROT // 2 + NE + 5 == FILLS
            pool.wait_ge(consts, FILLS)
            pool.affine_select(out=ident[:, :], in_=ident[:, :], compare_op=ALU.not_equal, fill=1.0,
                               base=0, pattern=[[-1, P]], channel_multiplier=1).then_inc(consts, 1)
            pool.affine_select(out=tri[:, :], in_=tri[:, :], compare_op=ALU.is_ge, fill=0.0,
                               base=0, pattern=[[1, P]], channel_multiplier=-1).then_inc(consts, 1)
            pool.affine_select(out=late[:, :], in_=late[:, :], compare_op=ALU.is_ge, fill=-BIG,
                               base=0, pattern=[[1, P]], channel_multiplier=-1).then_inc(consts, 1)
            pool.affine_select(out=future[:, :], in_=future[:, :], compare_op=ALU.is_ge, fill=-BIG,
                               base=P, pattern=[[-1, SEQ]], channel_multiplier=1).then_inc(consts, 1)

            for n in range(1, ADA_0):
                ada(0, n, n)
            with pool.Fori(0, DEPTH) as l:
                pool.wait_ge(pcol_ready, l + 1)
                rows = (("norm1", norm1_g[l]), ("norm2", norm2_g[l]), ("adab", ada_b[l]),
                        ("scw", sc_conv_w[l].rearrange("k n -> (k n)")), ("gvg", g_v_norm_g[l]),
                        ("mcw", m_conv_w[l].rearrange("k n -> (k n)")), ("mcb", m_conv_b[l]),
                        ("mng", m_norm_g[l]))
                for name, src in rows:
                    v = src.rearrange("(r j) -> r j", j=P)
                    pool.dma_start(prow[PR[name]:PR[name] + v.shape[0], :], v).then_inc(prow_in, 16)

                pool.wait_ge(layer_done, l + 1)
                pool.dma_start(gain[:, 0, :], q_norm_g[l].partition_broadcast(P)).then_inc(rows_in, 16)
                pool.dma_start(gain[:, 1, :], k_norm_g[l].partition_broadcast(P)).then_inc(rows_in, 16)
                for i, src in enumerate((m_dt_bias, m_a_log, m_d)):
                    pool.dma_start(mrow[:, i, :], src[l].partition_broadcast(P)).then_inc(rows_in, 16)
                pool.dma_start(gsb[:, :, :], g_spatial_b[l].partition_broadcast(P)).then_inc(rows_in, 16)
                for i in range(2):
                    c0 = (2 + 3 * i) * D_MODEL
                    pool.dma_start(gate_bc[:, i, :], ada_b[l, c0:c0 + D_MODEL].partition_broadcast(P)
                                   ).then_inc(gateb_in, 16)
                pool.dma_start(wsraw[:, :, :], g_spatial_w[l].rearrange("g t s -> t g s")).then_inc(wsraw_in, 16)
                next_l = pool.snap((l + 1) % DEPTH)
                pool.wait_ge(ob_ready, l + 1)
                for n, chunk in enumerate(CHUNKS):
                    ada(l if n < 8 else next_l, chunk, ADA_0 + l * MOD_CHUNKS + n)

        @block.tensor
        def _(pe):
            mm, tr = nc.tensor.matmul, nc.tensor.transpose
            pe.sem_inc(proj_evac, 2)
            pe.sem_inc(s_evac, 2)
            pe.sem_inc(v_evac, 2)
            pe.sem_inc(acc_used, 2)
            pe.wait_ge(consts, FILLS + 4)

            def chunk_columns(b, i, at):
                for q in range(4):
                    last = mm(b[:, 4 * i + q:4 * i + q + 1], ada_acc[:, at, q * P:q * P + P], ones[:, 0:1],
                              start=True, stop=True)
                last.then_inc(acc_used, 1)

            for n in range(ADA_0):
                pe.wait_ge(acc_ready, n + 2)
                chunk_columns(bank[:, 4, :], n, n % 2)
            pe.wait_ge(mod0_read, 1)
            with pe.Fori(0, DEPTH) as l:
                done = {"proj": 0, "s": 0, "v": 0, "unit": 0}
                NJ = {"proj": NPJ, "s": NSJ, "v": NVJ}
                JOBS = {"proj": PROJ_JOBS, "s": S_JOBS, "v": V_JOBS}
                EVAC = {"proj": proj_evac, "s": s_evac, "v": v_evac}
                

                def begin(kind, name):
                    assert JOBS[kind][done[kind]] == name, (name, JOBS[kind][done[kind]])
                    pe.wait_ge(EVAC[kind], l * NJ[kind] + done[kind] + 1)
                    done[kind] += 1
                    return pj(name) if kind == "proj" else ps(name)

                def loaded():
                    n = done["unit"]
                    done["unit"] += 1
                    pe.wait_ge(slot_loaded[n % RING], l * (16 * SLOT_L[n % RING]) + 16 * LANDED[n])
                    return ring[:, n % RING, :, :]

                def tok_project(out2, w, h, n, c0=0, lhs=hT):
                    for t in range(TT):
                        for k in range(HK):
                            last = mm(out2[t], lhs[:, HK * h + k, t * P:t * P + P], w[:, k, c0:c0 + n],
                                      start=(h == 0 and k == 0), stop=(h == 1 and k == HK - 1))
                    return last

                def chan_project(out_of, w, h, c0, tiles):
                    for m in range(tiles):
                        for k in range(HK):
                            last = mm(out_of(m), w[:, k, c0 + m * P:c0 + m * P + P], hT[:, HK * h + k, :],
                                      start=(h == 0 and k == 0 and m % 2 == 0),
                                      stop=(h == 1 and k == HK - 1), skip_group_check=True)
                    return last

                def tok_job(name, n=W):
                    b = begin("proj", name)
                    for h in range(2):
                        w = loaded()
                        tok_project([b[:, t, 0:n] for t in range(TT)], w, h, n).then_inc(units_read, 1)

                def chan_job(name):
                    b = begin("proj", name)
                    for h in range(2):
                        w = loaded()
                        chan_project(lambda m: b[:, m // 2, (m % 2) * SEQ:(m % 2) * SEQ + SEQ], w, h, 0,
                                     CT).then_inc(units_read, 1)

                def modulate_transposes(norm):
                    for q in range(4):
                        b = begin("s" if q < 2 else "v", f"h{norm}_{q}")
                        for k in range(2):
                            for t in range(TT):
                                last = tr(b[:, (k * TT + t) * P:(k * TT + t + 1) * P],
                                          merged[:, t, (2 * q + k) * P:(2 * q + k + 1) * P], ident[:, :])
                        last.then_inc(s_ready if q < 2 else v_ready, 1)

                def mod_columns(name, n):
                    b = begin("v", name)
                    for i in range(2):
                        pe.wait_ge(acc_ready, ADA_0 + l * MOD_CHUNKS + n + i + 2)
                        chunk_columns(b, i, (n + i) % 2)

                def mod_row(name, n):
                    b = begin("v", name)
                    pe.wait_ge(acc_ready, ADA_0 + l * MOD_CHUNKS + n + 2)
                    mm(b[:, :], ones[:, :], ada_acc[:, n % 2, :], start=True, stop=True).then_inc(acc_used, 1)

                pe.wait_ge(down_used, l * NE + 1)
                b = begin("v", PCOL)
                pe.wait_ge(prow_in, (l + 1) * (8 * 16))
                tr(b[:, 0:PROWS], prow[0:PROWS, :], ident[0:PROWS, 0:PROWS]).then_inc(v_ready, 1)
                pe.wait_ge(xn_ready, l * 2 + 1)
                modulate_transposes(1)

                pe.wait_ge(s_evac, l * NSJ + S_JOBS.index("h1_1") + 1 + 2)
                pe.wait_ge(v_evac, l * NVJ + V_JOBS.index("h1_3") + 1 + 2)
                b = begin("proj", "C")
                for h in range(2):
                    w = loaded()
                    for t in range(TT):
                        for k in range(HK):
                            mm(b[:, 0, t * 256:t * 256 + 256], hT[:, HK * h + k, t * P:t * P + P], w[:, k, 0:256],
                               start=(h == 0 and k == 0 and t == 0), stop=(h == 1 and k == HK - 1),
                               skip_group_check=True)
                    chan_project(lambda m: b[:, 1, m * SEQ:m * SEQ + SEQ], w, h, 256, 2).then_inc(units_read, 1)
                tok_job("B", SMALL)
                tok_job("A")

                pe.wait_ge(idx_rope, l + 1)
                b = begin("s", "qiT")
                for g in range(2):
                    for t in range(TT):
                        last = tr(b[:, (g * TT + t) * P:(g * TT + t + 1) * P],
                                  qik[:, t, 4 * g:4 * g + 4, :].rearrange("p h d -> p (h d)"), ident[:, :])
                last.then_inc(s_ready, 1)
                b = begin("s", "kiT")
                for t in range(TT):
                    last = tr(b[:, t * P:t * P + P], kirep[:, t, :, :].rearrange("p r d -> p (r d)"), ident[:, :])
                last.then_inc(s_ready, 1)
                chan_job("xbc")
                pe.wait_ge(s_evac, l * NSJ + S_JOBS.index("kiT") + 1 + 2)
                for t in range(TT):
                    ns = (t + 1) * P
                    for g in range(2):
                        for u in range(2):
                            b = begin("s", f"dot{t}{g}{u}")
                            mm(b[:, 0:2 * ns].rearrange("p (h s) -> p h s", h=2), qiT[:, g, t * P:t * P + P],
                               kiTd[:, 2 * u:2 * u + 2, 0:ns], start=True, stop=True).then_inc(s_ready, 1)
                pe.wait_ge(qk_roped, l + 1)
                for half in range(2):
                    b = begin("s", f"qT{half}")
                    for i in range(2):
                        for t in range(TT):
                            o = (2 * half + i) * 2
                            last = tr(b[:, (i * TT + t) * P:(i * TT + t + 1) * P],
                                      qk[:, t, o:o + 2, :].rearrange("p h d -> p (h d)"), ident[:, :])
                    last.then_inc(s_ready, 1)
                b = begin("s", "kT")
                for t in range(TT):
                    last = tr(b[:, t * P:t * P + P], qk[:, t, AH:AH + 2, :].rearrange("p h d -> p (h d)"),
                              ident[:, :])
                last.then_inc(s_ready, 1)
                tok_job("gv")
                pe.wait_ge(wsraw_in, (l + 1) * 16)
                b = begin("v", "wsT")
                for g in range(GG):
                    last = tr(b[:, g * P:g * P + P], wsraw[:, g, :], ident[:, :])
                last.then_inc(v_ready, 1)
                tok_job("z")
                pe.wait_ge(silu_ready, l + 1)
                for t in range(TT):
                    b = begin("s", f"xs{t}")
                    for m in range(CT):
                        last = tr(b[:, m * P:m * P + P], xbcT[:, m, t * P:t * P + P], ident[:, :])
                    last.then_inc(s_ready, 1)
                b = begin("s", "Bt")
                tr(b[:, 0:P], xbcT[:, 4, 0:P], ident[:, :]).then_inc(s_ready, 1)
                chan_job("gu")
                pe.wait_ge(s_evac, l * NSJ + S_JOBS.index("kT") + 1 + 2)
                for t in range(TT):
                    ns = (t + 1) * P
                    for i in range(4):
                        b = begin("v", f"lg{t}{i}")
                        mm(b[:, 0:2 * ns].rearrange("p (h s) -> p h s", h=2), qT[:, i, t * P:t * P + P],
                           kTd[:, :, 0:ns], start=True, stop=True).then_inc(v_ready, 1)
                pe.wait_ge(p_ready, l + 1)
                for i in range(4):
                    for u in range(2):
                        hd = i + 4 * u
                        b = begin("s", f"PT{i}{'ab'[u]}")
                        tr(b[:, 0:P], P_sb[:, hd, 0:P], ident[:, :])
                        tr(b[:, P:2 * P], P_sb[:, hd, P:2 * P], ident[:, :])
                        tr(b[:, 2 * P:3 * P], P_sb[:, hd, 2 * P:3 * P], ident[:, :]).then_inc(s_ready, 1)
                    b = begin("s", f"PV{i}")
                    pe.wait_ge(s_evac, l * NSJ + S_JOBS.index(f"PT{i}b") + 1 + 2)
                    for u in range(2):
                        pt = PT[:, (i + 4 * u) * 3 * P:(i + 4 * u + 1) * 3 * P]
                        mm(b[:, u * SEQ:u * SEQ + SEQ], v_sb[:, 0, :], pt[:, 0:SEQ], start=(u == 0), stop=False,
                           skip_group_check=True)
                        last = mm(b[:, u * SEQ + P:u * SEQ + SEQ], v_sb[:, 1, :], pt[:, SEQ:3 * P], start=False,
                                  stop=True, skip_group_check=True)
                    last.then_inc(s_ready, 1)
                pe.wait_ge(dt_ready, l + 1)
                b = begin("v", "acs")
                da = dtA[:, 1, :, :].rearrange("p c h -> p (c h)")
                mm(b[:, 0:16], tri[:, :], da, start=True, stop=True)
                mm(b[:, 16:32], ones[:, :], da, start=True, stop=True).then_inc(v_ready, 1)
                chan_job("scc")
                def cumulative(ch):
                    pe.wait_ge(R_ready, l * 2 + ch + 1)
                    for hh in range(2):
                        b = begin("v", f"ab{ch}{hh}")
                        mm(b[:, :], ones[:, :], scratch[:, ch * 1024 + hh * W:ch * 1024 + hh * W + W],
                           start=True, stop=True).then_inc(v_ready, 1)

                def chunk_output(ch):
                    b = begin("v", f"y{ch}")
                    pe.wait_ge(M_ready, l * 2 + ch + 1)
                    for hd in range(MH):
                        last = mm(b[:, hd * MP:hd * MP + MP], M_sb[:, hd, :], xdt[:, ch, hd * MP:hd * MP + MP],
                                  start=True, stop=True)
                    last.then_inc(v_ready, 1)

                cumulative(0)
                b = begin("s", "scT")
                pe.wait_ge(CTd_ready, l + 1)
                for c2 in range(TT):
                    last = mm(b[:, c2 * 256:c2 * 256 + 256].rearrange("p (g s) -> p g s", g=2),
                              xbcT[:, 4, c2 * P:c2 * P + P], CTd[:, :, c2 * P:c2 * P + P], start=True, stop=True)
                last.then_inc(s_ready, 1)
                chan_job("scx")
                chunk_output(0)
                b = begin("s", "states")
                pe.wait_ge(ssd_in, l + 1)
                mm(b[:, :], Btok[:, :], xdtd[:, :], start=True, stop=True).then_inc(s_ready, 1)
                cumulative(1)
                chan_job("scb")
                b = begin("v", "yoff")
                pe.wait_ge(s_evac, l * NSJ + S_JOBS.index("states") + 1 + 2)
                mm(b[:, :], xbcT[:, 5, P:2 * P], prevd[:, :], start=True, stop=True).then_inc(v_ready, 1)
                chunk_output(1)
                pe.wait_ge(gv_ready, l + 1)
                for q in range(2):
                    b = begin("v", f"mix{q}")
                    for g in range(2):
                        for ch in range(TT):
                            last = mm(b[:, (g * TT + ch) * P:(g * TT + ch + 1) * P],
                                      gv[:, ch, (2 * q + g) * P:(2 * q + g + 1) * P], wsT[:, 2 * q + g, :],
                                      start=True, stop=True)
                    last.then_inc(v_ready, 1)

                for n, (i, j) in enumerate(GATE_STEPS):
                    if j == 1:
                        pass
                    elif i == 1:
                        pe.wait_ge(ob_ready, l + 1)
                    elif i == 2:
                        pe.wait_ge(oc_ready, l + 1)
                    elif i == 3:
                        pe.wait_ge(od_ready, l + 1)
                        for q in range(2):
                            b = begin("s", f"odT{q}")
                            for m in range(2):
                                for t in range(TT):
                                    last = tr(b[:, (m * TT + t) * P:(m * TT + t + 1) * P],
                                              y_sb[:, t, (2 * q + m) * P:(2 * q + m + 1) * P], ident[:, :])
                            last.then_inc(s_ready, 1)
                    tok_job(f"g{i}{j}")
                    w = loaded()
                    if i == 3 and j == 0:
                        pe.wait_ge(s_evac, l * NSJ + S_JOBS.index("odT1") + 1 + 2)
                    for t in range(TT):
                        b = begin("v", f"b{i}{j}{t}")
                        for k in range(CT):
                            last = mm(b[:, :], oT[:, i, k, t * P:t * P + P], w[:, k, :],
                                      start=(k == 0), stop=(k == CT - 1))
                        last.then_inc(units_read if t else v_ready, 1)
                    for name in V_JOBS_OF_STEP.get(n, []):
                        (mod_row if name[0] == "g" else mod_columns)(
                            name, BY_CHUNK[name] - (name[0] == "m"))
                pe.wait_ge(merged_ready, l + 1)
                for q in range(4):
                    b = begin("s", f"mT{q}")
                    for k in range(2):
                        for t in range(TT):
                            last = tr(b[:, (k * TT + t) * P:(k * TT + t + 1) * P],
                                      merged[:, t, (2 * q + k) * P:(2 * q + k + 1) * P], ident[:, :])
                    last.then_inc(s_ready, 1)
                pe.wait_ge(s_evac, l * NSJ + S_JOBS.index("mT3") + 1 + 2)
                for j in range(2):
                    b2 = [begin("v", f"o{j}{t}") for t in range(TT)]
                    for h in range(2):
                        w = loaded()
                        tok_project([b[:, :] for b in b2], w, h, W).then_inc(units_read, 1)

                pe.wait_ge(xn_ready, l * 2 + 2)
                modulate_transposes(2)
                pe.wait_ge(s_evac, l * NSJ + S_JOBS.index("h2_1") + 1 + 2)
                pe.wait_ge(v_evac, l * NVJ + V_JOBS.index("h2_3") + 1 + 2)
                b = begin("v", "router")
                pe.wait_ge(rw_in, 32)
                for t in range(TT):
                    for k in range(KD):
                        last = mm(b[:, t * NE:t * NE + NE], hT[:, k, t * P:t * P + P], rw[:, k, :],
                                  start=(k == 0), stop=(k == KD - 1))
                last.then_inc(v_ready, 1)
                if "pad" in V_JOBS:
                    begin("v", "pad")

                pe.wait_ge(proj_evac, (l + 1) * NPJ + 2)
                pe.wait_ge(s_evac, (l + 1) * NSJ + 2)
                pe.wait_ge(v_evac, (l + 1) * NVJ + 2)

                def parts(n, slot):
                    pe.wait_ge(w_split, l * (NE * PER_E) + n + 1)
                    return w_high[slot % HIGHS][:, :, :], w_low[:, slot, :, :]

                def gate_up(b0, slot, n):
                    for h in range(2):
                        wh, wl = parts(n + h, slot + h)
                        for m in range(CT):
                            for k in range(HK):
                                kk, ms = HK * h + k, slice(m * P, m * P + P)
                                for q, (w, x_) in enumerate(((wh, h_high), (wh, h_low), (wl, h_high))):
                                    last = mm(bank[:, b0 + m // 2, (m % 2) * SEQ:(m % 2) * SEQ + SEQ], w[:, k, ms],
                                              x_[:, kk, :], start=(kk == 0 and m % 2 == 0 and q == 0),
                                              stop=(kk == KD - 1 and q == 2), skip_group_check=True)
                        last.then_inc(units_read, 1)

                def down(slot, n, e1):
                    pe.wait_ge(hid_ready, l * NE + e1)
                    for j in range(2):
                        wh, wl = parts(n + j, slot + j)
                        for t in range(TT):
                            for k in range(CT):
                                for q, (d, w) in enumerate(((hid_high, wh), (hid_high, wl), (hid_low, wh))):
                                    last = mm(bank[:, 4 + 2 * t + j, :], d[:, k, t * P:t * P + P], w[:, k, :],
                                              start=(k == 0 and q == 0), stop=(k == CT - 1 and q == 2))
                        last.then_inc(units_read, 1)

                pe.wait_ge(h_split, l + 1)
                gate_up(0, 0, 0)
                gate_up(2, 2, 2)
                with pe.Fori(1, NE) as e:
                    pe.wait_ge(silu_done, l * NE + e)
                    gate_up(0, 4, PER_E * e - 2)
                    pe.wait_ge(down_used, l * NE + e)
                    down(0, PER_E * e, e)
                    gate_up(2, 2, PER_E * e + 2)
                pe.wait_ge(down_used, (l + 1) * NE)
                down(4, PER_E * NE - 2, NE)

        @block.scalar
        def _(act):
            A = nc.scalar.activation
            act.wait_ge(c_in, 16)
            A(cact[:, :], c_raw[:, :], ACT.Silu).then_inc(cact_ready, 1)
            act.wait_ge(angles_ready, 1)
            A(rope[:, :, :, :], ang[:, :, :, :], ACT.Sin).then_inc(rope_ready, 1)
            act.wait_ge(x_in, 16)
            with act.Fori(0, DEPTH) as l:
                seen = {"s": 0, "proj": 0}

                def job(kind, name):
                    jobs = S_JOBS if kind == "s" else PROJ_JOBS
                    assert jobs[seen[kind]] == name, (name, jobs[seen[kind]])
                    seen[kind] += 1
                    if kind == "s":
                        act.wait_ge(s_ready, l * NSJ + seen[kind])
                    else:
                        act.wait_ge(units_read, l * UNITS_L + UNITS.index((name, 1)) + 1 + RING)
                    return ps(name) if kind == "s" else pj(name)

                def copy(dst, src):
                    return A(dst, src, ACT.Copy)

                def sum_squares(norm):
                    act.wait_ge(layer_done if norm == 1 else x_mid, l + 1)
                    for t in range(TT):
                        last = A(merged[:, t, :], x_sb[:, t, :], ACT.Square, accum_out=st[:, 0, t:t + 1])
                    last.then_inc(ss_ready, 1)

                def modulate(norm):
                    act.wait_ge(modc_ready, l * 2 + norm)
                    for q in range(2):
                        b = job("s", f"h{norm}_{q}")
                        for k in range(2):
                            kk = 2 * q + k
                            last = A(hT[:, kk, :], b[:, k * SEQ:k * SEQ + SEQ], ACT.Identity,
                                     scale=modc[:, norm - 1, 0, kk:kk + 1], bias=modc[:, norm - 1, 1, kk:kk + 1])
                        last.then_inc(s_evac, 1)

                sum_squares(1)
                act.wait_ge(mean_ready, l * 2 + 1)
                A(st[:, 2, 0:TT], st[:, 1, 0:TT], ACT.Sqrt).then_inc(rs_ready, 1)
                modulate(1)
                b = job("proj", "C")
                copy(qik[:, :, 0:IH, :], b[:, 0, :].rearrange("p (t h d) -> p t h d", t=TT, d=ID))
                copy(xbc[:, 4:6, M_K - 1:], b[:, 1, :].rearrange("p (m s) -> p m s", m=2)).then_inc(proj_evac, 1)
                b = job("proj", "B")
                o = 2 * AG * AD
                copy(qik[:, :, IH, :], b[:, :, o:o + ID])
                copy(wdt[:, :, :], b[:, :, o + ID:o + ID + IH + MH])
                copy(v_sb[:, :, :], b[:, :, AG * AD:o])
                copy(qk[:, :, AH:AH + 2, :], b[:, :, 0:AG * AD].rearrange("p t (g d) -> p t g d", g=AG)
                     ).then_inc(proj_evac, 1)
                b = job("proj", "A")
                for t in range(TT):
                    last = copy(qk[:, t, 0:AH, :].rearrange("p (i g) d -> p i g d", g=AG),
                                b[:, t, :].rearrange("p (g i d) -> p i g d", g=AG, i=4))
                last.then_inc(proj_evac, 1)
                act.wait_ge(dt_abs, l + 1)
                A(st[:, 4, 0:16], st[:, 3, 0:16], ACT.Exp, scale=-1.0).then_inc(dt_exp, 1)
                act.wait_ge(dt_exp, l + 1)
                A(st[:, 5, 0:16], st[:, 4, 0:16], ACT.Ln, bias=1.0)
                A(st[:, 7, 0:MH], mrow[:, 1, :], ACT.Exp).then_inc(dt_log, 1)
                act.wait_ge(qk_ss, l + 1)
                A(st[:, 9, 0:20], st[:, 8, 0:20], ACT.Sqrt).then_inc(qk_rs, 1)
                b = job("s", "qiT")
                copy(qiT[:, :, :], b[:, :].rearrange("p (g s) -> p g s", g=2)).then_inc(s_evac, 1)
                b = job("s", "kiT")
                for j in range(4):
                    last = copy(kiTd[32 * j:32 * j + 32, j, :], b[32 * j:32 * j + 32, 0:SEQ])
                last.then_inc(s_evac, 1)
                b = job("proj", "xbc")
                copy(xbc[:, 0:4, M_K - 1:], b[:, :, :].rearrange("p b (m s) -> p (b m) s", m=2)
                     ).then_inc(proj_evac, 1)
                act.wait_ge(qk_roped, l + 1)
                n = 0
                for t in range(TT):
                    ns = (t + 1) * P
                    for g in range(2):
                        for u in range(2):
                            b = job("s", f"dot{t}{g}{u}")
                            if n >= 2:
                                act.wait_ge(relu_used, l * 8 + n - 1)
                            A(scratch[:, (n % 2) * W:(n % 2) * W + 2 * ns], b[:, 0:2 * ns], ACT.Relu
                              ).then_inc(s_evac, 1)
                            n += 1
                for half in range(2):
                    b = job("s", f"qT{half}")
                    copy(qT[:, 2 * half:2 * half + 2, :], b[:, :].rearrange("p (i s) -> p i s", i=2)
                         ).then_inc(s_evac, 1)
                b = job("s", "kT")
                for g in range(AG):
                    last = copy(kTd[64 * g:64 * g + 64, g, :], b[64 * g:64 * g + 64, 0:SEQ])
                last.then_inc(s_evac, 1)
                b = job("proj", "gv")
                A(gv, b[:, :, :], ACT.Gelu).then_inc(proj_evac, 1)
                act.wait_ge(proj_evac, l * NPJ + PROJ_JOBS.index("gv") + 1 + 2)
                act.wait_ge(relu_used, l * 8 + 8)
                for t in range(TT):
                    last = A(scratch[:, t * W:t * W + W], gv[:, t, :], ACT.Square, accum_out=st[:, 10, t:t + 1])
                last.then_inc(gv_ss, 1)
                b = job("proj", "z")
                A(z_sb, b[:, :, :], ACT.Silu).then_inc(proj_evac, 1)
                act.wait_ge(conv_ready, l + 1)
                for m in range(6):
                    last = A(xbcT[:, m, :], xbcT[:, m, :], ACT.Silu, bias=pcol[:, PR["mcb"] + m:PR["mcb"] + m + 1])
                last.then_inc(silu_ready, 1)
                act.wait_ge(silu_ready, l + 1)
                for g in range(MG):
                    last = copy(CTd[64 * g:64 * g + 64, g, :], xbcT[64 * g:64 * g + 64, 5, :])
                last.then_inc(CTd_ready, 1)
                for t in range(TT):
                    b = job("s", f"xs{t}")
                    copy(xs_tok[:, t, :], b[:, :]).then_inc(s_evac, 1)
                b = job("s", "Bt")
                copy(Btok[:, :], b[:, 0:P]).then_inc(s_evac, 1)
                act.wait_ge(gv_mean, l + 1)
                A(st[:, 12, 0:TT], st[:, 11, 0:TT], ACT.Sqrt).then_inc(gv_rs, 1)
                b = job("proj", "gu")
                A(uT[:, :, :], b[:, :, :].rearrange("p b (m s) -> p (b m) s", m=2), ACT.Gelu).then_inc(proj_evac, 1)
                for t in range(TT):
                    act.wait_ge(max_ready, l * 2 + t + 1)
                    lo, hi = (0, P) if t == 0 else (P, 3 * P)
                    for hd in range(AH):
                        last = A(P_sb[:, hd, lo:hi], P_sb[:, hd, lo:hi], ACT.Exp, scale=AD ** -0.5,
                                 bias=st[:, 14 + t, hd:hd + 1], accum_out=st[:, 16 + t, hd:hd + 1])
                    last.then_inc(exp_ready, 1)
                for i in range(4):
                    for u in range(2):
                        hd = i + 4 * u
                        b = job("s", f"PT{i}{'ab'[u]}")
                        copy(PT[:, hd * 3 * P:(hd + 1) * 3 * P], b[:, 0:3 * P]).then_inc(s_evac, 1)
                    b = job("s", f"PV{i}")
                    for u in range(2):
                        last = copy(oT[64 * u:64 * u + 64, 0, i, :], b[64 * u:64 * u + 64, u * SEQ:u * SEQ + SEQ])
                    last.then_inc(s_evac, 1)
                b = job("proj", "scc")
                copy(scc, b[:, :, :].rearrange("p b (m s) -> p (b m) s", m=2)).then_inc(proj_evac, 1)
                act.wait_ge(acs_ready, l + 1)
                A(dtA[:, 2:4, :, :], dtA[:, 2:4, :, :], ACT.Exp).then_inc(decay_out, 1)
                b = job("s", "scT")
                copy(scT[:, :, :, :], b[:, :].rearrange("p (c g s) -> p c g s", c=2, g=2)).then_inc(s_evac, 1)
                act.wait_ge(diff_ready, l * 2 + 1)
                A(M_sb, M_sb, ACT.Exp).then_inc(dec_exp, 1)
                b = job("proj", "scx")
                copy(cx[:, :, 2:], b[:, :, :].rearrange("p b (m s) -> p (b m) s", m=2)).then_inc(proj_evac, 1)
                b = job("s", "states")
                copy(prevd[0:64, 0:256], b[0:64, 0:256])
                copy(prevd[64:128, 256:512], b[64:128, 256:512]).then_inc(s_evac, 1)
                b = job("proj", "scb")
                copy(scb, b[:, :, :].rearrange("p b (m s) -> p (b m) s", m=2)).then_inc(proj_evac, 1)
                act.wait_ge(diff_ready, l * 2 + 2)
                A(M_sb, M_sb, ACT.Exp).then_inc(dec_exp, 1)
                act.wait_ge(y_ss, l + 1)
                A(st[:, 20, 0:TT], st[:, 19, 0:TT], ACT.Sqrt).then_inc(y_rs, 1)
                for n, i in enumerate(BRANCH_ORDER):
                    if i == 3:
                        for q in range(2):
                            b = job("s", f"odT{q}")
                            for m in range(2):
                                mt = 2 * q + m
                                last = A(oT[:, 3, mt, :], b[:, m * SEQ:m * SEQ + SEQ], ACT.Copy,
                                         scale=pcol[:, PR["mng"] + mt:PR["mng"] + mt + 1])
                            last.then_inc(s_evac, 1)
                    for j in range(2):
                        b = job("proj", f"g{i}{j}")
                        if 2 * n + j >= 2:
                            act.wait_ge(gsig_used, l * 8 + 2 * n + j - 1)
                        A(gsig[j], b[:, :, :], ACT.Sigmoid).then_inc(proj_evac, 1)
                for q in range(4):
                    b = job("s", f"mT{q}")
                    copy(hT[:, 2 * q:2 * q + 2, :], b[:, :].rearrange("p (k s) -> p k s", k=2)).then_inc(s_evac, 1)

                def round_unit(n, slot, uses, free=True):
                    act.wait_ge(slot_loaded[slot], l * (16 * SLOT_L[slot]) + 16 * (SLOT_MIX[slot] + uses))
                    if free:
                        act.wait_ge(units_read, l * UNITS_L + MOE0 + n - HIGHS + 1 + RING)
                    A(w_high[slot % HIGHS][:, :, :], ring[:, slot, :, :], ACT.Copy).then_inc(w_rounded, 1)

                for n in range(HIGHS):
                    round_unit(n, n, 1, free=False)
                sum_squares(2)
                act.wait_ge(mean_ready, l * 2 + 2)
                A(st[:, 2, 0:TT], st[:, 1, 0:TT], ACT.Sqrt).then_inc(rs_ready, 1)
                modulate(2)
                act.wait_ge(s_evac, l * NSJ + S_JOBS.index("h2_1") + 1 + 2)
                act.wait_ge(v_evac, l * NVJ + V_JOBS.index("h2_3") + 1 + 2)
                A(h_high[:, :, :], hT[:, :, :], ACT.Copy).then_inc(h_rounded, 1)
                act.wait_ge(logit_ready, l + 1)
                A(rt1[:, 0, :, :], rt1[:, 0, :, :], ACT.Sigmoid).then_inc(sig_ready, 1)
                def silu_gate(read, e):
                    act.wait_ge(units_read, l * UNITS_L + MOE0 + read + RING)
                    act.wait_ge(hid_made, l * NE + e + 1)
                    A(sg.rearrange("p (b m) s -> p b (m s)", b=2), bank[:, 0:2, :], ACT.Silu).then_inc(silu_done, 1)

                def round_hidden(e):
                    act.wait_ge(hid_made, l * NE + e + 2)
                    A(hid_high[:, :, :], hid, ACT.Copy).then_inc(hid_rounded, 1)

                round_unit(3, 3, 1)
                round_unit(4, 4, 1)
                silu_gate(2, 0)
                round_unit(5, 5, 1)
                with act.Fori(1, NE) as e:
                    u = PER_E * e
                    round_unit(u, 0, e + 1)
                    round_hidden(e - 1)
                    round_unit(u + 1, 1, e + 1)
                    round_unit(u + 2, 2, e + 1)
                    silu_gate(u, e)
                    round_unit(u + 3, 3, e + 1)
                    round_unit(u + 4, 4, e + 1)
                    round_unit(u + 5, 5, e + 1)
                round_hidden(NE - 1)

        @block.vector
        def _(dve):
            V = nc.vector
            count = [0]

            def step(ins):
                count[0] += 1
                return ins.then_inc(dve_step, 1)

            def settle():
                dve.wait_ge(dve_step, count[0])

            def arrive():
                count[0] += 1
                dve.sem_inc(dve_step, 1)

            for started in (pcol_ready, layer_done, down_used, acc_ready, hid_made):
                dve.sem_inc(started, 1)
            dve.wait_ge(pos_in, 16)
            dve.wait_ge(consts, FILLS + 4)
            step(V.tensor_copy(pos_f[:, :], pos_i[:, :]))
            settle()
            for i in range(2):
                step(V.tensor_tensor(ang[:, i, :, :], bcast(pos_f[:, :], 2, AROT // 2),
                                     bcast(invf[:, :], 1, TT), ALU.mult))
            settle()
            round_up = 1.5 * 2.0 ** 23
            for i in range(2):
                step(V.tensor_scalar(turns[:, i, :, :], ang[:, i, :, :], 1.0 / (2 * math.pi), 0.25 * i,
                                     ALU.mult, ALU.add))
            settle()
            step(V.tensor_scalar(turns[:, :, :, :], turns[:, :, :, :], round_up, None, ALU.add))
            settle()
            step(V.tensor_scalar(turns[:, :, :, :], turns[:, :, :, :], round_up, None, ALU.subtract))
            settle()
            c1 = 6.28125
            c2 = float(np.float32(round((2 * math.pi - c1) * 2 ** 20) / 2 ** 20))
            c3 = 2 * math.pi - c1 - c2
            for part in (c1, c2, c3):
                step(V.scalar_tensor_tensor(out=ang[:, :, :, :].rearrange("p a t f -> p (a t f)"),
                                            in0=turns[:, :, :, :].rearrange("p a t f -> p (a t f)"), scalar=-part,
                                            in1=ang[:, :, :, :].rearrange("p a t f -> p (a t f)"),
                                            op0=ALU.mult, op1=ALU.add))
                settle()
            step(V.tensor_scalar(ang[:, 1, :, :], ang[:, 1, :, :], math.pi / 2, None, ALU.add))
            settle()
            V.tensor_scalar(ang[:, :, :, :], ang[:, :, :, :], 3.1415925, -3.1415925, ALU.min, ALU.max
                            ).then_inc(angles_ready, 1)
            def ada_chunk(n, at):
                dve.wait_ge(acc_used, at + 1)
                acc = ada_acc[:, n % 2, :]
                for q in range(4):
                    dve.wait_ge(ada_loaded[q], (at + 1) * 16)
                    for k in range(2):
                        w, ck = ada_place[q][:, k, :], cact[:, 2 * q + k:2 * q + k + 1]
                        if q == 0 and k == 0:
                            ins = V.tensor_scalar(acc, w, ck, None, ALU.mult)
                        else:
                            ins = V.scalar_tensor_tensor(out=acc, in0=w, scalar=ck, in1=acc, op0=ALU.mult,
                                                         op1=ALU.add)
                        if k == 1:
                            ins.then_inc(ada_freed, 1)
                            dve.wait_ge(ada_freed, 4 * at + q + 1 + 4)
                        else:
                            step(ins)
                            settle()
                dve.sem_inc(acc_ready, 1)

            dve.wait_ge(cact_ready, 1)
            for n in range(ADA_0):
                ada_chunk(n, n)
            dve.wait_ge(acc_used, ADA_0 + 2)
            V.tensor_copy(mod_sum[:, 0, :], bank[:, 4, 0:2 * KD]).then_inc(mod0_read, 1)
            dve.wait_ge(mod0_read, 1)
            dve.wait_ge(rope_ready, 1)
            dve.sem_clear(dve_step)
            count[0] = 0

            with dve.Fori(0, DEPTH) as l:
                seen = [0]

                def job(name):
                    assert V_JOBS[seen[0]] == name, (name, V_JOBS[seen[0]])
                    seen[0] += 1
                    if name in BY_UNIT:
                        dve.wait_ge(units_read, l * UNITS_L + BY_UNIT[name] + 1 + RING)
                    elif name in BY_CHUNK:
                        dve.wait_ge(acc_used, ADA_0 + l * MOD_CHUNKS + BY_CHUNK[name] + 1 + 2)
                    else:
                        dve.wait_ge(v_ready, l * NVR + V_PLAIN.index(name) + 1)
                    return ps(name)

                def evacuated():
                    dve.wait_ge(v_evac, l * NVJ + seen[0] + 2)

                def col(name, i=0, n=1):
                    return pcol[:, PR[name] + i:PR[name] + i + n]

                def norm_scale(norm):
                    dve.wait_ge(ss_ready, l * 2 + norm)
                    V.tensor_scalar(st[:, 1, 0:TT], st[:, 0, 0:TT], 1.0 / D_MODEL, EPS, ALU.mult, ALU.add
                                    ).then_inc(mean_ready, 1)
                    dve.wait_ge(rs_ready, l * 2 + norm)
                    step(V.reciprocal(st[:, 2, 2:2 + TT], st[:, 2, 0:TT]))
                    settle()
                    for t in range(TT):
                        last = V.tensor_scalar(merged[:, t, :], x_sb[:, t, :], st[:, 2, 2 + t:3 + t], None, ALU.mult)
                    last.then_inc(xn_ready, 1)

                def mod_cols(norm):
                    a0 = (0 if norm == 1 else 3) * KD
                    step(V.tensor_tensor(modc[:, norm - 1, 1, :], mod_sum[:, norm - 1, 0:KD], col("adab", a0, KD),
                                         ALU.add))
                    step(V.tensor_tensor(modc[:, norm - 1, 0, :], mod_sum[:, norm - 1, KD:], col("adab", a0 + KD, KD),
                                         ALU.add))
                    settle()
                    V.scalar_tensor_tensor(out=modc[:, norm - 1, 0, :], in0=modc[:, norm - 1, 0, :], scalar=1.0,
                                           in1=col(f"norm{norm}", 0, KD), op0=ALU.add, op1=ALU.mult
                                           ).then_inc(modc_ready, 1)
                    dve.wait_ge(modc_ready, l * 2 + norm)

                def modulate(norm):
                    for q in range(2, 4):
                        b = job(f"h{norm}_{q}")
                        for k in range(2):
                            kk = 2 * q + k
                            last = V.tensor_scalar(hT[:, kk, :], b[:, k * SEQ:k * SEQ + SEQ],
                                                   modc[:, norm - 1, 0, kk:kk + 1], modc[:, norm - 1, 1, kk:kk + 1],
                                                   ALU.mult, ALU.add)
                        last.then_inc(v_evac, 1)

                b = job(PCOL)
                V.tensor_copy(pcol[:, 0:PROWS], b[:, 0:PROWS]).then_inc(v_evac, 1)
                evacuated()
                dve.sem_inc(pcol_ready, 1)
                mod_cols(1)
                norm_scale(1)
                modulate(1)

                def rotate(v, nh, half, freq_step, done):
                    x1, x2 = v[:, :, :, 0:half], v[:, :, :, half:2 * half]
                    sin = bcast(rope[:, 0, :, 0:AROT // 2:freq_step], 2, nh)
                    cos = bcast(rope[:, 1, :, 0:AROT // 2:freq_step], 2, nh)
                    tmp = [rt[:, i, 0:TT * nh, 0:half].rearrange("p (t h) f -> p t h f", t=TT) for i in range(4)]
                    step(V.tensor_tensor(tmp[0], x1, cos, ALU.mult))
                    step(V.tensor_tensor(tmp[1], x2, sin, ALU.mult))
                    step(V.tensor_tensor(tmp[2], x2, cos, ALU.mult))
                    step(V.tensor_tensor(tmp[3], x1, sin, ALU.mult))
                    settle()
                    step(V.tensor_tensor(x1, tmp[0], tmp[1], ALU.subtract))
                    last = V.tensor_tensor(x2, tmp[2], tmp[3], ALU.add)
                    if done is None:
                        step(last)
                        settle()
                    else:
                        last.then_inc(done, 1)

                dve.wait_ge(proj_evac, l * NPJ + 2 + 2)
                rotate(qik[:, :, :, :], IH + 1, IROT // 2, 2, None)
                V.tensor_copy(kirep[:, :, :, :], bcast(qik[:, :, IH, :], 2, 4)).then_inc(idx_rope, 1)
                dve.wait_ge(rows_in, (l + 1) * (6 * 16))
                r16 = lambda i: st[:, i, 0:16].rearrange("p (t h) -> p t h", t=TT)
                step(V.tensor_tensor(r16(6), wdt[:, :, IH:], bcast(mrow[:, 0, :], 1, TT), ALU.add))
                step(V.tensor_scalar(wdt[:, :, 0:IH], wdt[:, :, 0:IH], float(np.float32(IH ** -0.5 * ID ** -0.5)),
                                     None, ALU.mult))
                settle()
                step(V.tensor_scalar(st[:, 3, 0:16], st[:, 6, 0:16], -1.0, None, ALU.mult))
                settle()
                V.tensor_tensor(st[:, 3, 0:16], st[:, 3, 0:16], st[:, 6, 0:16], ALU.max).then_inc(dt_abs, 1)
                dve.wait_ge(dt_log, l + 1)
                step(V.tensor_scalar(st[:, 3, 0:16], st[:, 4, 0:16], 1.0, None, ALU.add))
                settle()
                step(V.tensor_scalar(st[:, 3, 0:16], st[:, 3, 0:16], 1.0, 1e-30, ALU.subtract, ALU.max))
                settle()
                step(V.reciprocal(st[:, 3, 0:16], st[:, 3, 0:16]))
                step(V.tensor_tensor(st[:, 5, 0:16], st[:, 5, 0:16], st[:, 4, 0:16], ALU.mult))
                settle()
                step(V.tensor_tensor(st[:, 5, 0:16], st[:, 5, 0:16], st[:, 3, 0:16], ALU.mult))
                settle()
                step(V.scalar_tensor_tensor(out=dtA[:, 0, :, :].rearrange("p t h -> p (t h)"), in0=st[:, 6, 0:16],
                                            scalar=0.0, in1=st[:, 5, 0:16], op0=ALU.max, op1=ALU.add))
                step(V.tensor_scalar(st[:, 7, 0:MH], st[:, 7, 0:MH], -1.0, None, ALU.mult))
                settle()
                V.tensor_tensor(dtA[:, 1, :, :], dtA[:, 0, :, :], bcast(st[:, 7, 0:MH], 1, TT), ALU.mult
                                ).then_inc(dt_ready, 1)

                dve.wait_ge(proj_evac, l * NPJ + 3 + 2)
                NQ = TT * (AH + AG)
                qk2 = qk[:, :, :, :].rearrange("p t h d -> p (t h) d")
                sq = scratch[:, 0:NQ * AD].rearrange("p (h d) -> p h d", d=AD)
                step(V.tensor_tensor(sq, qk2, qk2, ALU.mult))
                settle()
                step(V.tensor_reduce(st[:, 8, 0:NQ], sq, AX_X, ALU.add))
                settle()
                V.tensor_scalar(st[:, 8, 0:NQ], st[:, 8, 0:NQ], 1.0 / AD, EPS, ALU.mult, ALU.add).then_inc(qk_ss, 1)
                dve.wait_ge(qk_rs, l + 1)
                step(V.reciprocal(st[:, 9, 0:NQ], st[:, 9, 0:NQ]))
                settle()
                step(V.tensor_tensor(qk2, qk2, bcast(st[:, 9, 0:NQ], 2, AD), ALU.mult))
                settle()
                for t in range(TT):
                    step(V.tensor_tensor(qk[:, t, 0:AH, :], qk[:, t, 0:AH, :], bcast(gain[:, 0, :], 1, AH), ALU.mult))
                    step(V.tensor_tensor(qk[:, t, AH:, :], qk[:, t, AH:, :], bcast(gain[:, 1, :], 1, AG), ALU.mult))
                settle()
                rotate(qk[:, :, :, :], AH + AG, AROT // 2, 1, qk_roped)

                spans = [score[:, 0:P], score[:, P:3 * P]]
                masks = [mask[:, 0:P], mask[:, P:3 * P]]
                causal = [future[:, P:2 * P], future[:, :]]
                n = 0
                for t in range(TT):
                    ns = (t + 1) * P
                    for g in range(2):
                        for u in range(2):
                            dve.wait_ge(s_evac, l * NSJ + S_JOBS.index(f"dot{t}{g}{u}") + 1 + 2)
                            for q in range(2):
                                hd = 4 * g + 2 * u + q
                                prev = causal[t] if hd == 0 else spans[t]
                                ins = V.scalar_tensor_tensor(
                                    out=spans[t], in0=scratch[:, (n % 2) * W + q * ns:(n % 2) * W + (q + 1) * ns],
                                    scalar=wdt[:, t, hd:hd + 1], in1=prev, op0=ALU.mult, op1=ALU.add)
                                if q == 1:
                                    ins.then_inc(relu_used, 1)
                                    dve.wait_ge(relu_used, l * 8 + n + 1)
                                else:
                                    step(ins)
                                    settle()
                            n += 1
                arrive()
                for r in range(TOPK // 8):
                    for t in range(TT):
                        step(V.max(top8[:, t, :], spans[t]))
                    settle()
                    for t in range(TT):
                        step(V.match_replace(spans[t], top8[:, t, :], spans[t], TAKEN))
                    settle()
                for t in range(TT):
                    step(V.tensor_scalar(masks[t], spans[t], TAKEN / 2, -BIG, ALU.is_gt, ALU.mult))
                settle()
                for t in range(TT):
                    step(V.tensor_tensor(masks[t], masks[t], causal[t], ALU.add))
                dve.wait_ge(proj_evac, l * NPJ + PROJ_JOBS.index("xbc") + 1 + 2)
                for k in range(M_K):
                    for m in range(6):
                        tap, wk = xbc[:, m, k:k + SEQ], col("mcw", k * 6 + m)
                        if k == 0:
                            step(V.tensor_scalar(xbcT[:, m, :], tap, wk, None, ALU.mult))
                        else:
                            ins = V.scalar_tensor_tensor(out=xbcT[:, m, :], in0=tap, scalar=wk, in1=xbcT[:, m, :],
                                                         op0=ALU.mult, op1=ALU.add)
                            if k == M_K - 1 and m == 5:
                                ins.then_inc(conv_ready, 1)
                            else:
                                step(ins)
                    if k < M_K - 1:
                        settle()
                b = job("wsT")
                V.tensor_tensor(wsT[:, :, :], b[:, :].rearrange("p (g t) -> p g t", g=GG), bcast(tri[:, :], 1, GG),
                                ALU.mult).then_inc(v_evac, 1)
                dve.wait_ge(gv_ss, l + 1)
                V.tensor_scalar(st[:, 11, 0:TT], st[:, 10, 0:TT], 1.0 / W, EPS, ALU.mult, ALU.add).then_inc(gv_mean, 1)
                dve.wait_ge(gv_rs, l + 1)
                step(V.reciprocal(st[:, 12, 0:TT], st[:, 12, 0:TT]))
                settle()
                for t in range(TT):
                    last = V.tensor_scalar(gv[:, t, :], gv[:, t, :], st[:, 12, t:t + 1], None, ALU.mult)
                last.then_inc(gv_ready, 1)

                for t in range(TT):
                    lo, hi = (0, P) if t == 0 else (P, 3 * P)
                    for i in range(4):
                        b = job(f"lg{t}{i}")
                        settle()
                        arrive()
                        for u in range(2):
                            hd = i + 4 * u
                            ns = hi - lo
                            ins = V.tensor_tensor_reduce(P_sb[:, hd, lo:hi], b[:, u * ns:(u + 1) * ns], masks[t], 1.0,
                                                         -3e38, ALU.add, ALU.max, st[:, 13, t * 8 + hd:t * 8 + hd + 1])
                            if u == 1:
                                ins.then_inc(v_evac, 1)
                    evacuated()
                    V.tensor_scalar(st[:, 14 + t, 0:AH], st[:, 13, t * 8:t * 8 + 8], -AD ** -0.5, None, ALU.mult
                                    ).then_inc(max_ready, 1)
                for t in range(TT):
                    lo, hi = (0, P) if t == 0 else (P, 3 * P)
                    dve.wait_ge(exp_ready, l * 2 + t + 1)
                    step(V.reciprocal(st[:, 16 + t, 8:16], st[:, 16 + t, 0:8]))
                    settle()
                    for hd in range(AH):
                        last = V.tensor_scalar(P_sb[:, hd, lo:hi], P_sb[:, hd, lo:hi], st[:, 16 + t, 8 + hd:9 + hd],
                                               None, ALU.mult)
                        if t < TT - 1 or hd < AH - 1:
                            step(last)
                last.then_inc(p_ready, 1)

                b = job("acs")
                V.tensor_copy(acs[:, :, :, :].rearrange("p a c h -> p (a c h)"), b[:, 0:32]).then_inc(v_evac, 1)
                evacuated()
                step(V.tensor_tensor(dtA[:, 2, :, :], acs[:, 1, :, :], acs[:, 0, :, :], ALU.subtract))
                V.tensor_copy(dtA[:, 3, :, :], acs[:, 0, :, :]).then_inc(acs_ready, 1)
                for ch in range(TT):
                    V.tensor_tensor(scratch[:, ch * 1024:ch * 1024 + 1024].rearrange("p (h l) -> p h l", h=MH),
                                    bcast(dtA[:, 1, ch, :], 2, P), bcast(tri[:, :], 1, MH), ALU.mult
                                    ).then_inc(R_ready, 1)
                dve.wait_ge(s_evac, l * NSJ + S_JOBS.index("PV3") + 1 + 2)
                for ch in range(TT):
                    step(V.tensor_tensor(xdt[:, ch, :].rearrange("p (h q) -> p h q", h=MH),
                                         xs_tok[:, ch, :].rearrange("p (h q) -> p h q", h=MH),
                                         bcast(dtA[:, 0, ch, :], 2, MP), ALU.mult))
                settle()
                dve.wait_ge(decay_out, l + 1)
                V.tensor_tensor(xdtd[:, :].rearrange("p (h q) -> p h q", h=MH),
                                xdt[:, 0, :].rearrange("p (h q) -> p h q", h=MH),
                                bcast(dtA[:, 2, 0, :], 2, MP), ALU.mult).then_inc(ssd_in, 1)

                def decay(ch):
                    if ch:
                        dve.wait_ge(v_ready, l * NVR + V_PLAIN.index("y0") + 1)
                    for hh in range(2):
                        b = job(f"ab{ch}{hh}")
                        V.tensor_tensor(M_sb[:, 4 * hh:4 * hh + 4, :], b[:, :].rearrange("p (h l) -> p h l", h=4),
                                        bcast(acs[:, 0, ch, 4 * hh:4 * hh + 4], 2, P), ALU.subtract
                                        ).then_inc(v_evac, 1)
                    evacuated()
                    V.tensor_tensor(M_sb, M_sb, bcast(late[:, :], 1, MH), ALU.add).then_inc(diff_ready, 1)

                def weigh(ch):
                    dve.wait_ge(dec_exp, l * 2 + ch + 1)
                    dve.wait_ge(s_evac, l * NSJ + S_JOBS.index("scT") + 1 + 2)
                    for g in range(MG):
                        last = V.tensor_tensor(M_sb[:, 4 * g:4 * g + 4, :], M_sb[:, 4 * g:4 * g + 4, :],
                                               bcast(scT[:, ch, g, :], 1, 4), ALU.mult)
                        if g == 0:
                            step(last)
                    last.then_inc(M_ready, 1)

                def skip_y(ch):
                    b = job(f"y{ch}")
                    V.tensor_tensor(y_sb[:, ch, :], y_sb[:, ch, :], b[:, :], ALU.add).then_inc(v_evac, 1)
                    evacuated()

                decay(0)
                for ch in range(TT):
                    step(V.tensor_tensor(y_sb[:, ch, :].rearrange("p (h q) -> p h q", h=MH),
                                         xs_tok[:, ch, :].rearrange("p (h q) -> p h q", h=MH),
                                         bcast(mrow[:, 2, :], 2, MP), ALU.mult))
                weigh(0)
                settle()
                skip_y(0)
                decay(1)
                dve.wait_ge(proj_evac, l * NPJ + PROJ_JOBS.index("scx") + 1 + 2)
                step(V.memset(cx[:, :, 0:2], 0.0))
                step(V.tensor_tensor(cx[:, :, 2:], cx[:, :, 2:], scc, ALU.mult))
                settle()
                for k in range(SC_K):
                    for m in range(CT):
                        tap, wk = cx[:, m, k:k + SEQ], col("scw", k * CT + m)
                        if k == 0:
                            step(V.tensor_scalar(oT[:, 1, m, :], tap, wk, None, ALU.mult))
                        else:
                            step(V.scalar_tensor_tensor(out=oT[:, 1, m, :], in0=tap, scalar=wk, in1=oT[:, 1, m, :],
                                                        op0=ALU.mult, op1=ALU.add))
                    settle()
                weigh(1)
                b = job("yoff")
                yo = scratch[:, 0:W]
                V.tensor_tensor(yo.rearrange("p (h q) -> p h q", h=MH), b[:, :].rearrange("p (h q) -> p h q", h=MH),
                                bcast(dtA[:, 3, 1, :], 2, MP), ALU.mult).then_inc(v_evac, 1)
                evacuated()
                step(V.tensor_tensor(y_sb[:, 1, :], y_sb[:, 1, :], yo, ALU.add))
                settle()
                skip_y(1)
                dve.wait_ge(proj_evac, l * NPJ + PROJ_JOBS.index("z") + 1 + 2)
                step(V.tensor_tensor(y_sb, y_sb, z_sb, ALU.mult))
                settle()
                for t in range(TT):
                    step(V.tensor_tensor_reduce(scratch[:, t * W:t * W + W], y_sb[:, t, :], y_sb[:, t, :], 1.0, 0.0,
                                                ALU.mult, ALU.add, st[:, 19, 8 + t:9 + t]))
                settle()
                V.tensor_scalar(st[:, 19, 0:TT], st[:, 19, 8:8 + TT], 1.0 / W, EPS, ALU.mult, ALU.add
                                ).then_inc(y_ss, 1)
                dve.wait_ge(proj_evac, l * NPJ + PROJ_JOBS.index("scb") + 1 + 2)
                V.tensor_tensor(oT[:, 1, :, :], oT[:, 1, :, :], scb, ALU.mult).then_inc(ob_ready, 1)
                dve.wait_ge(y_rs, l + 1)
                step(V.reciprocal(st[:, 20, 0:TT], st[:, 20, 0:TT]))
                settle()
                for t in range(TT):
                    last = V.tensor_scalar(y_sb[:, t, :], y_sb[:, t, :], st[:, 20, t:t + 1], None, ALU.mult)
                last.then_inc(od_ready, 1)
                dve.wait_ge(proj_evac, l * NPJ + PROJ_JOBS.index("gu") + 1 + 2)
                for q in range(2):
                    b = job(f"mix{q}")
                    for g in range(2):
                        m = 2 * q + g
                        last = V.scalar_tensor_tensor(
                            out=oT[:, 2, m, :].rearrange("p (c t) -> p c t", c=TT),
                            in0=b[:, g * SEQ:g * SEQ + SEQ].rearrange("p (c t) -> p c t", c=TT),
                            scalar=col("gvg", m), in1=bcast(gsb[:, m, :], 1, TT), op0=ALU.mult, op1=ALU.add)
                    last.then_inc(v_evac, 1)
                evacuated()
                V.tensor_tensor(oT[:, 2, :, :], oT[:, 2, :, :], uT[:, :, :], ALU.mult).then_inc(oc_ready, 1)

                dve.wait_ge(gateb_in, (l + 1) * 32)

                def take_sums(name):
                    b = job(name)
                    if name[0] == "g":
                        i, j = int(name[4]) - 1, int(name[5])
                        V.tensor_tensor(gate_bc[:, i, j * W:j * W + W], gate_bc[:, i, j * W:j * W + W], b[:, :],
                                        ALU.add).then_inc(v_evac, 1)
                    else:
                        norm, part = {"mod01": (0, 0), "mod23": (0, 1), "mod67": (1, 0), "mod89": (1, 1)}[name]
                        V.tensor_copy(mod_sum[:, norm, part * KD:part * KD + KD], b[:, 0:KD]).then_inc(v_evac, 1)

                for n, (i, j) in enumerate(GATE_STEPS):
                    dve.wait_ge(proj_evac, l * NPJ + PROJ_JOBS.index(f"g{i}{j}") + 1 + 2)
                    for t in range(TT):
                        b = job(f"b{i}{j}{t}")
                        part = merged[:, t, j * W:j * W + W]
                        dst = part if n < 2 else gsig[j][:, t, :]
                        V.tensor_tensor(dst, gsig[j][:, t, :], b[:, :], ALU.mult).then_inc(v_evac, 1)
                    evacuated()
                    if n < 2:
                        dve.sem_inc(gsig_used, 1)
                    else:
                        for t in range(TT):
                            part = merged[:, t, j * W:j * W + W]
                            last = V.tensor_tensor(part, part, gsig[j][:, t, :], ALU.add)
                            if t == 0:
                                step(last)
                        last.then_inc(gsig_used, 1)
                        dve.wait_ge(gsig_used, l * 8 + n + 1)
                    if n == len(GATE_STEPS) - 1:
                        dve.sem_inc(merged_ready, 1)
                    for name in V_JOBS_OF_STEP.get(n, []):
                        take_sums(name)
                    if n < len(CHUNKS) // 2:
                        for m in (2 * n, 2 * n + 1):
                            ada_chunk(m, ADA_0 + l * MOD_CHUNKS + m)
                evacuated()
                mod_cols(2)

                def split_unit(n, slot):
                    dve.wait_ge(w_rounded, l * (NE * PER_E) + n + 1)
                    V.tensor_tensor(w_low[:, slot, :, :], ring[:, slot, :, :],
                                    w_high[slot % HIGHS][:, :, :],
                                    ALU.subtract).then_inc(w_split, 1)

                split_unit(0, 0)
                split_unit(1, 1)
                for j in range(2):
                    for t in range(TT):
                        b = job(f"o{j}{t}")
                        V.tensor_tensor(merged[:, t, j * W:j * W + W], b[:, :], gate_bc[:, 0, j * W:j * W + W],
                                        ALU.mult).then_inc(v_evac, 1)
                    if j == 0:
                        split_unit(2, 2)
                evacuated()
                V.tensor_tensor(x_sb[:, :, :], x_sb[:, :, :], merged, ALU.add).then_inc(x_mid, 1)
                norm_scale(2)
                modulate(2)

                R = lambda i: rt1[:, i, :, :]
                G = lambda i: rt1[:, i, :, :].rearrange("p t (g k) -> p t g k", g=EG)
                LG = lambda i: rt1[:, i, :, 0:EG]

                def op(out_, a, b_, o):
                    step(V.tensor_tensor(out_, a, b_, o))

                b = job("router")
                V.tensor_copy(R(0), b[:, 0:TT * NE].rearrange("p (t e) -> p t e", t=TT)).then_inc(v_evac, 1)
                if "pad" in V_JOBS:
                    seen[0] += 1
                    dve.wait_ge(v_evac, l * NVJ + NVJ - 1 + 2)
                    dve.sem_inc(v_evac, 1)
                evacuated()
                dve.sem_inc(logit_ready, 1)
                dve.wait_ge(h_rounded, l + 1)
                V.tensor_tensor(h_low[:, :, :], hT[:, :, :], h_high[:, :, :],
                                ALU.subtract).then_inc(h_split, 1)
                dve.wait_ge(sig_ready, l + 1)
                op(R(1), R(0), bcast(rbias[:, :], 1, TT), ALU.add)
                settle()
                op(rt1[:, 2, :, 0:2 * EG].rearrange("p t (g k) -> p t g k", g=EG), G(1)[:, :, :, 0:2], G(1)[:, :, :, 2:4],
                   ALU.max)
                op(rt1[:, 3, :, 0:2 * EG].rearrange("p t (g k) -> p t g k", g=EG), G(1)[:, :, :, 0:2], G(1)[:, :, :, 2:4],
                   ALU.min)
                settle()
                hi = rt1[:, 2, :, 0:2 * EG].rearrange("p t (g k) -> p t g k", g=EG)
                lo = rt1[:, 3, :, 0:2 * EG].rearrange("p t (g k) -> p t g k", g=EG)
                op(LG(4), hi[:, :, :, 0], hi[:, :, :, 1], ALU.max)
                op(LG(5), hi[:, :, :, 0], hi[:, :, :, 1], ALU.min)
                op(LG(6), lo[:, :, :, 0], lo[:, :, :, 1], ALU.max)
                settle()
                op(LG(5), LG(5), LG(6), ALU.max)
                settle()
                op(LG(4), LG(4), LG(5), ALU.add)
                settle()

                def first_of(val, n_, rank, tmp, dst):
                    step(V.tensor_reduce(rt1[:, tmp, :, 0], val, AX_X, ALU.max))
                    settle()
                    op(dst, val, bcast(rt1[:, tmp, :, 0], 2, n_), ALU.is_equal)
                    settle()
                    op(dst, dst, bcast(rank[:, 0:n_], 1, TT), ALU.mult)
                    settle()
                    step(V.tensor_reduce(rt1[:, tmp, :, 1], dst, AX_X, ALU.max))
                    settle()
                    op(dst, dst, bcast(rt1[:, tmp, :, 1], 2, n_), ALU.is_equal)
                    settle()

                first_of(LG(4), EG, rank, 6, LG(5))
                step(V.tensor_scalar(LG(5), LG(5), 1.0, BIG, ALU.subtract, ALU.mult))
                settle()
                op(G(2), G(1), bcast(LG(5), 3, EPG), ALU.add)
                settle()
                first_of(R(2), NE, rank, 6, R(3))
                split_unit(3, 3)
                step(V.scalar_tensor_tensor(out=R(4), in0=R(3), scalar=-2 * BIG, in1=R(2), op0=ALU.mult, op1=ALU.add))
                settle()
                first_of(R(4), NE, rank, 6, R(5))
                op(R(3), R(3), R(5), ALU.add)
                settle()
                op(R(3), R(3), R(0), ALU.mult)
                settle()
                step(V.tensor_reduce(rt1[:, 6, :, 0], R(3), AX_X, ALU.add))
                settle()
                step(V.reciprocal(rt1[:, 6, :, 1], rt1[:, 6, :, 0]))
                settle()
                op(comb[:, :, :], R(3), bcast(rt1[:, 6, :, 1], 2, NE), ALU.mult)
                settle()
                dve.sem_clear(dve_step)
                count[0] = 0

                def hidden(read, e):
                    dve.wait_ge(silu_done, l * NE + e + 1)
                    dve.wait_ge(units_read, l * UNITS_L + MOE0 + read + RING)
                    V.tensor_tensor(hid.rearrange("p (b m) s -> p b (m s)", b=2),
                                    sg.rearrange("p (b m) s -> p b (m s)", b=2), bank[:, 2:4, :], ALU.mult
                                    ).then_inc(hid_made, 1)

                def split_hidden(e):
                    dve.wait_ge(hid_rounded, l * NE + e + 1)
                    V.tensor_tensor(hid_low[:, :, :], hid, hid_high[:, :, :],
                                    ALU.subtract).then_inc(hid_ready, 1)

                def add_expert(read, e):
                    V.tensor_copy(cw[:, :], comb[:, :, bass.ds(e, 1)].rearrange("p t o -> p (t o)")
                                  ).then_inc(moe_step, 1)
                    dve.wait_ge(moe_step, 1)
                    dve.wait_ge(units_read, l * UNITS_L + MOE0 + read + RING)
                    for t in range(TT):
                        o = merged[:, t, :].rearrange("p (b n) -> p b n", b=2)
                        last = V.scalar_tensor_tensor(out=o, in0=bank[:, 4 + 2 * t:6 + 2 * t, :],
                                                      scalar=cw[:, t:t + 1], in1=o, op0=ALU.mult, op1=ALU.add)
                    last.then_inc(down_used, 1)
                    dve.wait_ge(down_used, l * NE + e + 2)
                    dve.sem_inc(moe_step, 1)
                    dve.sem_clear(moe_step)

                V.memset(scratch[:, :], 0.0).then_inc(moe_step, 1)
                dve.wait_ge(moe_step, 1)
                dve.sem_clear(moe_step)
                split_unit(4, 4)
                split_unit(5, 5)
                hidden(4, 0)
                with dve.Fori(1, NE) as e:
                    u = PER_E * e
                    split_unit(u, 0)
                    split_hidden(e - 1)
                    for n in range(1, 4):
                        split_unit(u + n, n)
                    add_expert(u + 2, e - 1)
                    split_unit(u + 4, 4)
                    split_unit(u + 5, 5)
                    hidden(u + 4, e)
                split_hidden(NE - 1)
                add_expert(PER_E * NE, NE - 1)
                for t in range(TT):
                    step(V.tensor_tensor(merged[:, t, :], merged[:, t, :], gate_bc[:, 1, :], ALU.mult))
                settle()
                V.tensor_tensor(x_sb[:, :, :], x_sb[:, :, :], merged, ALU.add).then_inc(layer_done, 1)
                dve.wait_ge(layer_done, l + 2)
                arrive()
                dve.sem_clear(dve_step)
                count[0] = 0


_INS = ["x", "c", "positions", "ada_w", "ada_b", "norm1_g", "w_in", "q_norm_g", "k_norm_g", "sc_conv_w",
        "g_v_norm_g", "g_spatial_w", "g_spatial_b", "m_conv_w", "m_conv_b", "m_dt_bias", "m_a_log", "m_d",
        "m_norm_g", "w_branch", "w_out", "norm2_g", "router_w", "router_bias", "exp_w_gate", "exp_w_up",
        "exp_w_down"]


def kernel(**inputs):
    import concourse.bacc as bacc
    from concourse.bass_utils import run_bass_kernel_spmd

    nc = bacc.Bacc("TRN2", target_bir_lowering=False, num_devices=1)
    arrays, args = {}, []
    for name in _INS:
        a = np.ascontiguousarray(inputs[name])
        arrays[f"in_{name}"] = a
        args.append(nc.dram_tensor(f"in_{name}", a.shape, mybir.dt.from_np(a.dtype), kind="ExternalInput").ap())
    out = nc.dram_tensor("out", (1, SEQ, D_MODEL), F32, kind="ExternalOutput").ap()
    hybrid_trunk(nc, *args, out)
    r = run_bass_kernel_spmd(nc, [arrays], core_ids=[0])
    return r.results[0]["out"]
```

```python
import math
from contextlib import ExitStack

import numpy as np

import concourse.bass as bass
from concourse import mybir

F32 = mybir.dt.float32
F32R = mybir.dt.float32r
I32 = mybir.dt.int32
ALU = mybir.AluOpType
ACT = mybir.ActivationFunctionType
AX_X = mybir.AxisListType.X

P = 128
D_MODEL, SEQ, DEPTH = 1024, 256, 2
TT = SEQ // P
KD = D_MODEL // P
W = 512
HK = KD // 2
EPS = 1e-6
ROPE_THETA = 500000.0
AH, AG, AD, AROT = 8, 2, 64, 16
IH, ID, IROT = 8, 32, 8
TOPK = 64
SC_K, M_K = 3, 4
GG, MH, MP, MG, MN = 4, 8, 64, 2, 64
NE, EG, EPG, FF = 16, 4, 4, 512
CT = W // P
NB = 4

CQ, CK, CV, CQI, CKI, CWI = 0, 512, 640, 768, 1024, 1056
CSB, CSC, CSX, CGU, CGV, CZ, CXBC, CDT, CG = 1064, 1576, 2088, 2600, 3112, 3624, 4136, 4904, 4912
SMALL = AG * AD * 2 + ID + IH + MH
BRANCH_ORDER = (1, 2, 0, 3)

PR = {}
PROWS = 0
for _name, _n in (("norm1", KD), ("norm2", KD), ("adab", 6 * KD), ("scw", SC_K * CT), ("gvg", CT),
                  ("mcw", M_K * 6), ("mcb", 6), ("mng", CT)):
    PR[_name] = PROWS
    PROWS += _n

BIG = 1e30
FILLS = 5 + AROT // 2 + NE + 5
TAKEN = -3e38

RING = 6
HIGHS = 3
UNITS = [(n, h) for n in ("C", "B", "A", "xbc", "gv", "z", "gu", "scc", "scx", "scb") for h in range(2)]
for _i in BRANCH_ORDER:
    for _j in range(2):
        UNITS += [(f"g{_i}{_j}", 0), (f"g{_i}{_j}", 1), (f"b{_i}{_j}", 0)]
UNITS += [("o0", 0), ("o0", 1), ("o1", 0), ("o1", 1)]
MOE0 = len(UNITS)
GATE0 = UNITS.index(("g10", 0))
SC0 = UNITS.index(("scc", 0))
PER_E = 6
UNITS_L = MOE0 + NE * PER_E
LAST_IN = [n - 2 if SC0 < n < GATE0 else n - HIGHS for n in range(MOE0)]
for _n in (0, 1, 2, SC0, GATE0, GATE0 + 1, GATE0 + 2):
    LAST_IN[_n] = None
N_POOL = GATE0 - HIGHS
N_DVE = UNITS_L - N_POOL
ROUND_BEFORE = {"C": 3, "B": 5, "A": 7, "xbc": 9, "gv": 11, "z": 13, "scx": 18}
ROUND_AFTER = {"C": 4, "B": 6, "A": 8, "xbc": 10, "gv": 12, "z": 14, "gu": 15, "scx": 19}
assert MOE0 % RING == 0 and PER_E == RING and RING % HIGHS == 0
PARTS = [3 if n == "B" else 2 if n == "C" or n[:2] == "b0" else 1 for n, _ in UNITS]
LANDED = [sum(PARTS[m] for m in range(n % RING, n + 1, RING)) for n in range(MOE0)]
SLOT_MIX = [sum(PARTS[m] for m in range(s, MOE0, RING)) for s in range(RING)]
SLOT_L = [SLOT_MIX[s] + NE for s in range(RING)]

PROJ_JOBS = ["C", "B", "A", "xbc", "gv", "z", "gu", "scc", "scx", "scb"]
PROJ_JOBS += [f"g{i}{j}" for i in BRANCH_ORDER for j in range(2)]
S_JOBS = ["h1_0", "h1_1", "qiT", "kiT"]
S_JOBS += [f"dot{t}{g}{u}" for t in range(TT) for g in range(2) for u in range(2)]
S_JOBS += ["qT0", "qT1", "kT", "xs0", "xs1", "Bt"]
S_JOBS += [x for i in range(4) for x in (f"PT{i}a", f"PT{i}b", f"PV{i}")]
S_JOBS += ["scT", "states", "odT0", "odT1", "mT0", "mT1", "mT2", "mT3", "h2_0", "h2_1"]
V_JOBS = ["h1_2", "h1_3", "wsT"]
V_JOBS += [f"lg{t}{i}" for t in range(TT) for i in range(4)]
V_JOBS += ["acs", "ab00", "ab01", "y0", "ab10", "ab11", "yoff", "y1", "mix0", "mix1"]
CHUNKS = [4, 5, 6, 7, 8, 9, 10, 11, 0, 1, 2, 3]
GATE_CHUNKS = 6
MOE_CHUNKS = len(CHUNKS) - GATE_CHUNKS
GATE_STEPS = [(i, j) for i in BRANCH_ORDER for j in range(2)]
SUM_OF_STEP = {1: "gate10", 2: "gate11", 4: "mod67", 6: "mod89"}
for _n, (_i, _j) in enumerate(GATE_STEPS):
    V_JOBS += [f"b{_i}{_j}{t}" for t in range(TT)] + ([SUM_OF_STEP[_n]] if _n in SUM_OF_STEP else [])
V_JOBS += [f"o{j}{t}" for j in range(2) for t in range(TT)]
V_JOBS += ["h2_2", "h2_3", "router", "pad"]
PCOL = "pcol"
V_JOBS = [PCOL] + V_JOBS
if len(V_JOBS) % 2:
    V_JOBS.remove("pad")
assert len(PROJ_JOBS) % 2 == 0 and len(S_JOBS) % 2 == 0 and len(V_JOBS) % 2 == 0
BY_UNIT = {f"b{i}{j}1": UNITS.index((f"b{i}{j}", 0)) for i in BRANCH_ORDER for j in range(2)}
BY_UNIT |= {f"o{j}{t}": UNITS.index((f"o{j}", 1)) for j in range(2) for t in range(TT)}
BY_CHUNK = {"gate10": 0, "gate11": 1, "mod67": 3, "mod89": 5}
V_PLAIN = [n for n in V_JOBS if n not in BY_UNIT and n not in BY_CHUNK and n != "pad"]
NVR = len(V_PLAIN)
NPJ, NSJ, NVJ = len(PROJ_JOBS), len(S_JOBS), len(V_JOBS)
MOD_CHUNKS = 6 * D_MODEL // W
ADA_0 = 4


def bcast(ap, axis, n):
    a = ap.unsqueeze(axis)
    shape = list(a.shape)
    shape[axis] = n
    return a.to_broadcast(shape)


def hybrid_trunk(nc, x, c, positions, ada_w, ada_b, norm1_g, w_in, q_norm_g, k_norm_g, sc_conv_w,
                 g_v_norm_g, g_spatial_w, g_spatial_b, m_conv_w, m_conv_b, m_dt_bias, m_a_log, m_d,
                 m_norm_g, w_branch, w_out, norm2_g, router_w, router_bias, exp_w_gate, exp_w_up,
                 exp_w_down, out):
    ctx = ExitStack()
    with ctx:
        place = {}

        def sb(name, shape, dt=F32):
            place[name] = (nc.sbuf_base + 31) // 32 * 32
            return ctx.enter_context(nc.sbuf_tensor(name, [P] + shape, dt))

        def part_of(whole, name, word, shape):
            return nc.alloc_sbuf_tensor_at(name, [P] + shape, F32R, offset=place[whole] + 4 * word)

        def sem(name):
            return ctx.enter_context(nc.semaphore(name))

        bank = ctx.enter_context(nc.psum_tensor("bank", [P, 8, W], F32))

        ring = sb("ring", [RING, HK, W])
        ada_buf = sb("ada_buf", [2, 2, W])
        x_sb = sb("x_sb", [TT, D_MODEL])
        hT = sb("hT", [KD, SEQ])
        scratch = sb("scratch", [TT * D_MODEL])
        merged = scratch[:, :].rearrange("p (t d) -> p t d", t=TT)
        gate_bc = sb("gate_bc", [2, D_MODEL])
        ada_acc = sb("ada_acc", [2, W])
        ident = sb("ident", [P])
        tri = sb("tri", [P])
        late = sb("late", [P])
        future = sb("future", [SEQ])
        ones = sb("ones", [P])
        invf = sb("invf", [AROT // 2])
        prow = sb("prow", [P])
        c_raw = sb("c_raw", [KD])
        mod_sum = sb("mod_sum", [2, 2 * KD])
        pcol = sb("pcol", [P])
        cact = sb("cact", [KD])
        gain = sb("gain", [2, AD])
        mrow = sb("mrow", [3, MH])
        gsb = sb("gsb", [GG, P])
        rbias = sb("rbias", [NE])
        rw = sb("rw", [KD, NE])
        wsraw = sb("wsraw", [GG, P])
        wsT = sb("wsT", [GG, P])
        pos_i = sb("pos_i", [TT], I32)
        pos_f = sb("pos_f", [TT])
        rope = sb("rope", [2, TT, AROT // 2])
        ang = sb("ang", [2, TT, AROT // 2])
        turns = sb("turns", [2, TT, AROT // 2])
        st = sb("st", [21, 32])
        modc = sb("modc", [2, 2, KD])
        qk_score = sb("qk_score", [HK * W])
        qk = qk_score[:, 0:TT * (AH + AG) * AD].rearrange("p (t h d) -> p t h d", t=TT, d=AD)
        xs_tok = qk_score[:, 0:TT * W].rearrange("p (t d) -> p t d", t=TT)
        qik = sb("qik", [TT, IH + 1, ID])
        kirep = sb("kirep", [TT, 4, ID])
        wdt = sb("wdt", [TT, IH + MH])
        v_sb = sb("v_sb", [TT, AG * AD])
        qiT = sb("qiT", [2, SEQ])
        bd_qt = sb("bd_qt", [2, 4, SEQ])
        kiTd = bd_qt[:, 0, :, :]
        qT = bd_qt[:, 1, :, :]
        kTd = sb("kTd", [AG, SEQ])
        score = qk_score[:, HK * W - 6 * P:HK * W - 3 * P]
        top8 = sb("top8", [TT, 8])
        mask = qk_score[:, HK * W - 3 * P:]
        P_sb = sb("P_sb", [AH, 3 * P])
        p_flat = P_sb[:, :, :].rearrange("p h s -> p (h s)")
        M_sb = p_flat[:, 0:1024].rearrange("p (h l) -> p h l", h=MH)
        y_sb = p_flat[:, 1024:2048].rearrange("p (t d) -> p t d", t=TT)
        xdt = p_flat[:, 2048:3072].rearrange("p (t d) -> p t d", t=TT)
        PT = sb("PT", [AH * 3 * P + 8])
        ada_place = [ada_buf[:, 0, :, :], ada_buf[:, 1, :, :]] + [
            PT[:, i * 2 * W:(i + 1) * 2 * W].rearrange("p (k n) -> p k n", k=2) for i in range(2)]
        scc = PT[:, 0:CT * SEQ].rearrange("p (m s) -> p m s", m=CT)
        cx = PT[:, CT * SEQ:CT * SEQ + CT * (SEQ + 2)].rearrange("p (m s) -> p m s", m=CT)
        scb = PT[:, CT * (2 * SEQ + 2):CT * (3 * SEQ + 2)].rearrange("p (m s) -> p m s", m=CT)
        oT_gv = sb("oT_gv", [NB * CT * SEQ + TT * W])
        oT = oT_gv[:, 0:NB * CT * SEQ].rearrange("p (i m s) -> p i m s", i=NB, m=CT)
        gv = oT_gv[:, NB * CT * SEQ:].rearrange("p (t d) -> p t d", t=TT)
        ada_sums = oT_gv[:, NB * CT * SEQ + TT * W - MOE_CHUNKS * W:]
        xbc = sb("xbc", [6, SEQ + M_K - 1])
        xbc_sc = sb("xbc_sc", [6 * SEQ + TT * MG * P])
        xbcT = xbc_sc[:, 0:6 * SEQ].rearrange("p (m s) -> p m s", m=6)
        Btok = sb("Btok", [P])
        CTd = sb("CTd", [MG, SEQ])
        dtA = sb("dtA", [4, TT, MH])
        acs = sb("acs", [2, TT, MH])
        xdtd = sb("xdtd", [W])
        zu = sb("zu", [TT * W + CT * SEQ])
        z_sb = zu[:, 0:TT * W].rearrange("p (t d) -> p t d", t=TT)
        rt = zu[:, 0:4 * TT * (AH + AG) * AROT // 2].rearrange(
            "p (i h f) -> p i h f", i=4, f=AROT // 2)
        prevd = sb("prevd", [W])
        scT = xbc_sc[:, 6 * SEQ:].rearrange("p (c g s) -> p c g s", c=TT, g=MG)
        uT = zu[:, TT * W:].rearrange("p (m s) -> p m s", m=CT)
        gsig = [qT.rearrange("p i s -> p (i s)").rearrange("p (t n) -> p t n", t=TT), gv]
        rt1 = sb("rt1", [7, TT, NE])
        comb = sb("comb", [TT, NE])
        cw = sb("cw", [TT])
        rank = sb("rank", [NE])
        sg = p_flat[:, 0:1024].rearrange("p (m s) -> p m s", m=CT)
        hid = p_flat[:, 1024:2048].rearrange("p (m s) -> p m s", m=CT)

        w_low = part_of("ring", "w_low", 0, [RING, HK, W])
        w_high = [part_of(whole, f"w_high_{whole}", 0, [HK, W]) for whole in ("xbc_sc", "zu", "qk_score")]
        early_high = [part_of("oT_gv", "early_high0", 0, [HK, W]), part_of("oT_gv", "early_high1", HK * W, [HK, W]),
                      part_of("PT", "early_high2", 0, [HK, W])]
        sc_high = [part_of("gate_bc", "sc_high0", 0, [HK, W]), early_high[1]]
        mixer_high = [early_high[n % HIGHS] if n < SC0 else sc_high[(n - SC0) % 2] if n < GATE0 else
                      w_high[n % HIGHS] for n in range(MOE0)]
        h_low = part_of("hT", "h_low", 0, [KD, SEQ])
        h_high = part_of("ada_buf", "h_high", 0, [KD, SEQ])
        h1_high = [part_of("P_sb", "h1_high0", 0, [HK, SEQ]), part_of("P_sb", "h1_high1", 2048, [HK, SEQ])]
        h2_high = part_of("oT_gv", "h2_high", 0, [KD, SEQ])
        rw_high = sb("rw_high", [KD, NE], F32R)
        rw_low = part_of("rw", "rw_low", 0, [KD, NE])
        o_low, o_high = part_of("oT_gv", "o_low", 0, [NB, CT, SEQ]), part_of("PT", "o_high", 2048, [CT, SEQ])
        hid_low = part_of("P_sb", "hid_low", 1024, [CT, SEQ])
        hid_high = part_of("P_sb", "hid_high", 2048, [CT, SEQ])

        slot_loaded = [sem(f"slot_loaded{s}") for s in range(RING)]
        units_read = sem("units_read")
        unit_turn = sem("unit_turn")
        ada_loaded = [sem(f"ada_loaded{s}") for s in range(4)]
        ada_freed = sem("ada_freed")
        c_in = sem("c_in")
        acc_ready, acc_used = sem("acc_ready"), sem("acc_used")
        proj_evac = sem("proj_evac")
        s_ready, s_evac = sem("s_ready"), sem("s_evac")
        v_ready, v_evac = sem("v_ready"), sem("v_evac")
        consts, x_in, pos_in, rw_in = sem("consts"), sem("x_in"), sem("pos_in"), sem("rw_in")
        prow_in, wsraw_in, rows_in, gateb_in = sem("prow_in"), sem("wsraw_in"), sem("rows_in"), sem("gateb_in")
        dve_step, moe_step, CTd_ready = sem("dve_step"), sem("moe_step"), sem("CTd_ready")
        angles_ready, rope_ready = sem("angles_ready"), sem("rope_ready")
        pcol_ready, cact_ready = sem("pcol_ready"), sem("cact_ready")
        ss_ready, mean_ready, rs_ready = sem("ss_ready"), sem("mean_ready"), sem("rs_ready")
        xn_ready, modc_ready = sem("xn_ready"), sem("modc_ready")
        idx_rope, qk_ss, qk_rs, qk_roped = sem("idx_rope"), sem("qk_ss"), sem("qk_rs"), sem("qk_roped")
        dt_abs, dt_exp, dt_log, dt_ready = sem("dt_abs"), sem("dt_exp"), sem("dt_log"), sem("dt_ready")
        relu_used, mask_ready = sem("relu_used"), sem("mask_ready")
        max_ready, exp_ready, p_ready = sem("max_ready"), sem("exp_ready"), sem("p_ready")
        conv_ready, silu_ready = sem("conv_ready"), sem("silu_ready")
        ssd_in, acs_ready, R_ready, dec_exp, diff_ready = (
            sem("ssd_in"), sem("acs_ready"), sem("R_ready"), sem("dec_exp"), sem("diff_ready"))
        decay_out, M_ready = sem("decay_out"), sem("M_ready")
        y_ss, y_rs, od_ready = sem("y_ss"), sem("y_rs"), sem("od_ready")
        gv_ss, gv_mean, gv_rs, gv_ready = sem("gv_ss"), sem("gv_mean"), sem("gv_rs"), sem("gv_ready")
        oc_ready, ob_ready, gsig_used, merged_ready = (
            sem("oc_ready"), sem("ob_ready"), sem("gsig_used"), sem("merged_ready"))
        sums_ready, gate2_ready = sem("sums_ready"), sem("gate2_ready")
        logit_ready, sig_ready = sem("logit_ready"), sem("sig_ready")
        silu_done, hid_ready, down_used = sem("silu_done"), sem("hid_ready"), sem("down_used")
        w_rounded, w_split, w_split_pool = sem("w_rounded"), sem("w_split"), sem("w_split_pool")
        x_tile, x_half, rstd_ready = sem("x_tile"), sem("x_half"), sem("rstd_ready")
        rw_rounded, rw_split = sem("rw_rounded"), sem("rw_split")
        h_moved, h2_rounded, h2_split = sem("h_moved"), sem("h2_rounded"), sem("h2_split")
        mT_rounded = sem("mT_rounded")
        o_rounded, o_split = sem("o_rounded"), sem("o_split")
        h_rounded, h_split = sem("h_rounded"), sem("h_split")
        hid_made, hid_rounded = sem("hid_made"), sem("hid_rounded")
        layer_done, stored = sem("layer_done"), sem("stored")

        def load_rows(queue, layer):
            rows = (("norm1", norm1_g[layer]), ("norm2", norm2_g[layer]), ("adab", ada_b[layer]),
                    ("scw", sc_conv_w[layer].rearrange("k n -> (k n)")), ("gvg", g_v_norm_g[layer]),
                    ("mcw", m_conv_w[layer].rearrange("k n -> (k n)")), ("mcb", m_conv_b[layer]),
                    ("mng", m_norm_g[layer]))
            for name, src in rows:
                v = src.rearrange("(r j) -> r j", j=P)
                queue.dma_start(prow[PR[name]:PR[name] + v.shape[0], :], v).then_inc(prow_in, 16)

        def columns_of(n):
            return slice(0, SMALL if UNITS[n][0] == "B" else W)

        def ps(name):
            if name in S_JOBS:
                return bank[:, 6 + S_JOBS.index(name) % 2, :]
            return bank[:, 4 + V_JOBS.index(name) % 2, :]

        def pj(name):
            b = 2 * (PROJ_JOBS.index(name) % 2)
            return bank[:, b:b + 2, :]

        block = ctx.enter_context(nc.Block())

        @block.sync
        def _(sp):
            w_in_v = w_in.rearrange("l (k p) n -> l p k n", p=P)
            w_br_v = w_branch.rearrange("l b (k p) n -> l b p k n", p=P)
            w_a_v = w_branch.rearrange("l b (g k p) n -> l b g p k n", g=AG, p=AD)
            w_out_v = w_out.rearrange("l (k p) n -> l p k n", p=P)
            wg_v = exp_w_gate.rearrange("l e (k p) n -> (l e) p k n", p=P)
            wu_v = exp_w_up.rearrange("l e (k p) n -> (l e) p k n", p=P)
            wd_v = exp_w_down.rearrange("l e (k p) n -> (l e) p k n", p=P)
            start = {"A": CQ, "xbc": CXBC, "gv": CGV, "z": CZ, "gu": CGU, "scc": CSC, "scx": CSX, "scb": CSB}

            sp.dma_start(c_raw[:, :], c[0].rearrange("(k p) -> p k", p=P),
                         allow_slow_non_contiguous=True).then_inc(c_in, 16)
            sp.dma_start(pos_i[:, :], positions[0].rearrange("(t p) -> p t", p=P),
                         allow_slow_non_contiguous=True).then_inc(pos_in, 16)
            load_rows(sp, 0)
            sp.sem_inc(units_read, RING)
            sp.dma_start(x_sb[:, :, :], x[0].rearrange("(t p) d -> p t d", p=P)).then_inc(x_in, 16)
            sp.dma_start(rw[:, :, :], router_w.rearrange("(k p) e -> p k e", p=P)).then_inc(rw_in, 16)
            sp.dma_start(rbias[:, :], router_bias.partition_broadcast(P)).then_inc(rw_in, 16)
            sp.wait_ge(ada_loaded[3], ADA_0 * 16)
            with sp.Fori(0, DEPTH) as l:
                def load(n, src, dst=None):
                    s = n % RING
                    dst = ring[:, s, :, :] if dst is None else dst
                    sp.dma_start(dst, src).then_inc(slot_loaded[s], 16)

                for n, (name, h) in enumerate(UNITS):
                    s = n % RING
                    ks = slice(HK * h, HK * h + HK)
                    sp.wait_ge(units_read, l * UNITS_L + n + 1)
                    sp.sem_inc(unit_turn, 1)
                    if name == "C":
                        load(n, w_in_v[l, :, ks, CQI:CQI + 256], ring[:, s, :, 0:256])
                        load(n, w_in_v[l, :, ks, CXBC + W:CXBC + W + 256], ring[:, s, :, 256:512])
                    elif name == "B":
                        load(n, w_in_v[l, :, ks, CK:CK + 256], ring[:, s, :, 0:256])
                        load(n, w_in_v[l, :, ks, CKI:CKI + ID + IH], ring[:, s, :, 256:256 + ID + IH])
                        load(n, w_in_v[l, :, ks, CDT:CDT + MH], ring[:, s, :, 256 + ID + IH:SMALL])
                    elif name in start:
                        load(n, w_in_v[l, :, ks, start[name]:start[name] + W])
                    elif name[0] == "g":
                        c0 = CG + int(name[1]) * D_MODEL + int(name[2]) * W
                        load(n, w_in_v[l, :, ks, c0:c0 + W])
                    elif name[0:2] == "b0":
                        for g in range(AG):
                            load(n, w_a_v[l, 0, g, :, :, int(name[2]) * W:int(name[2]) * W + W],
                                 ring[AD * g:AD * g + AD, s, :, :])
                    elif name[0] == "b":
                        load(n, w_br_v[l, int(name[1]), :, :, int(name[2]) * W:int(name[2]) * W + W])
                    else:
                        load(n, w_out_v[l, :, ks, int(name[1]) * W:int(name[1]) * W + W])

                def gate_up(n, slot, view, e):
                    for h in range(2):
                        sp.wait_ge(units_read, l * UNITS_L + n + h + 1)
                        load(slot + h, view[e, :, HK * h:HK * h + HK, :])

                def down(n, slot, e):
                    for j in range(2):
                        sp.wait_ge(units_read, l * UNITS_L + n + j + 1)
                        load(slot + j, wd_v[e, :, :, j * W:j * W + W])

                after = sp.snap((l + 1) % DEPTH)
                sp.wait_ge(pcol_ready, l + 2)
                load_rows(sp, after)

                first = sp.snap(l * NE)
                gate_up(MOE0, 0, wg_v, first)
                gate_up(MOE0 + 2, 2, wu_v, first)
                with sp.Fori(1, NE) as e:
                    n = MOE0 + 4 + (e - 1) * PER_E
                    this = sp.snap(l * NE + e)
                    last = sp.snap(l * NE + e - 1)
                    gate_up(n, 4, wg_v, this)
                    down(n + 2, 0, last)
                    gate_up(n + 4, 2, wu_v, this)
                down(UNITS_L - 2, 4, sp.snap(l * NE + NE - 1))
            for t in range(TT):
                sp.wait_ge(x_tile, DEPTH * TT + t + 1)
                sp.dma_start(out[0, t * P:t * P + P, :], x_sb[:, t, :]).then_inc(stored, 16)
            sp.wait_ge(stored, TT * 16)
            sp.wait_ge(prow_in, (DEPTH + 1) * 8 * 16)

        @block.gpsimd
        def _(pool):
            ada_v = ada_w.rearrange("l (k p) n -> l p k n", p=P)
            pool.sem_inc(ada_freed, 4)

            def ada(layer, chunk, at):
                for q in range(4):
                    pool.wait_ge(ada_freed, 4 * at + q + 1)
                    pool.dma_start(ada_place[q], ada_v[layer, :, 2 * q:2 * q + 2, chunk * W:chunk * W + W]
                                   ).then_inc(ada_loaded[q], 16)

            ada(0, 0, 0)
            for tile, val in ((ident, 0.0), (tri, 1.0), (late, 0.0), (future, 0.0), (ones, 1.0)):
                pool.memset(tile[:, :], val).then_inc(consts, 1)
            for f in range(AROT // 2):
                val = float(np.exp(np.float32(-math.log(ROPE_THETA)) * np.float32(f) * np.float32(2.0)
                                   / np.float32(AROT)))
                pool.memset(invf[:, f:f + 1], val).then_inc(consts, 1)
            pool.wait_ge(consts, 5 + AROT // 2)
            pool.affine_select(out=ident[:, :], in_=ident[:, :], compare_op=ALU.not_equal, fill=1.0,
                               base=0, pattern=[[-1, P]], channel_multiplier=1).then_inc(consts, 1)
            ada(0, 1, 1)
            pool.affine_select(out=tri[:, :], in_=tri[:, :], compare_op=ALU.is_ge, fill=0.0,
                               base=0, pattern=[[1, P]], channel_multiplier=-1).then_inc(consts, 1)
            pool.affine_select(out=late[:, :], in_=late[:, :], compare_op=ALU.is_ge, fill=-BIG,
                               base=0, pattern=[[1, P]], channel_multiplier=-1).then_inc(consts, 1)
            pool.affine_select(out=future[:, :], in_=future[:, :], compare_op=ALU.is_ge, fill=-BIG,
                               base=P, pattern=[[-1, SEQ]], channel_multiplier=1).then_inc(consts, 1)
            ada(0, 2, 2)
            for f in range(NE):
                pool.memset(rank[:, f:f + 1], float(NE - f)).then_inc(consts, 1)
            for tile in (kTd[:, :, :], CTd[:, :, :], prevd[:, :], xbc[:, :, 0:M_K - 1]):
                pool.memset(tile, 0.0).then_inc(consts, 1)
            ada(0, 3, 3)
            pool.memset(bd_qt[:, 0, :, :], 0.0).then_inc(consts, 1)
            with pool.Fori(0, DEPTH) as l:
                pool.wait_ge(layer_done, l + 1)
                pool.dma_start(gain[:, 0, :], q_norm_g[l].partition_broadcast(P)).then_inc(rows_in, 16)
                pool.dma_start(gain[:, 1, :], k_norm_g[l].partition_broadcast(P)).then_inc(rows_in, 16)
                for i, src in enumerate((m_dt_bias, m_a_log, m_d)):
                    pool.dma_start(mrow[:, i, :], src[l].partition_broadcast(P)).then_inc(rows_in, 16)
                pool.dma_start(gsb[:, :, :], g_spatial_b[l].partition_broadcast(P)).then_inc(rows_in, 16)
                pool.dma_start(wsraw[:, :, :], g_spatial_w[l].rearrange("g t s -> t g s")).then_inc(wsraw_in, 16)
                for n in range(HIGHS, GATE0):
                    cols = columns_of(n)
                    pool.wait_ge(w_rounded, l * UNITS_L + n + 1)
                    nc.gpsimd.tensor_tensor(w_low[:, n % RING, :, cols], ring[:, n % RING, :, cols],
                                            mixer_high[n][:, :, cols], ALU.subtract).then_inc(w_split_pool, 1)
                pool.wait_ge(units_read, l * UNITS_L + GATE0 - 2 + 1 + RING)
                for i in range(2):
                    c0 = (2 + 3 * i) * D_MODEL
                    pool.dma_start(gate_bc[:, i, :], ada_b[l, c0:c0 + D_MODEL].partition_broadcast(P)
                                   ).then_inc(gateb_in, 16)
                next_l = pool.snap((l + 1) % DEPTH)
                pool.wait_ge(ob_ready, l + 1)
                pool.wait_ge(h_moved, l + 1)
                for n, chunk in enumerate(CHUNKS):
                    ada(l if n < 8 else next_l, chunk, ADA_0 + l * MOD_CHUNKS + n)

        @block.tensor
        def _(pe):
            mm, tr = nc.tensor.matmul, nc.tensor.transpose
            pe.sem_inc(proj_evac, 2)
            pe.sem_inc(s_evac, 2)
            pe.sem_inc(v_evac, 2)
            pe.sem_inc(acc_used, 2)
            pe.wait_ge(consts, FILLS + 4)

            def chunk_columns(b, c0, acc):
                for q in range(4):
                    last = mm(b[:, c0 + q:c0 + q + 1], acc[:, q * P:q * P + P], ones[:, 0:1], start=True, stop=True)
                return last

            with pe.Fori(0, DEPTH) as l:
                done = {"proj": 0, "s": 0, "v": 0, "unit": 0}
                NJ = {"proj": NPJ, "s": NSJ, "v": NVJ}
                JOBS = {"proj": PROJ_JOBS, "s": S_JOBS, "v": V_JOBS}
                EVAC = {"proj": proj_evac, "s": s_evac, "v": v_evac}

                def begin(kind, name):
                    assert JOBS[kind][done[kind]] == name, (name, JOBS[kind][done[kind]])
                    pe.wait_ge(EVAC[kind], l * NJ[kind] + done[kind] + 1)
                    done[kind] += 1
                    return pj(name) if kind == "proj" else ps(name)

                def parts(n, slot):
                    if isinstance(n, int) and HIGHS <= n < GATE0:
                        pe.wait_ge(w_split_pool, l * N_POOL + n - HIGHS + 1)
                    elif isinstance(n, int) and n < HIGHS:
                        pe.wait_ge(w_split, l * N_DVE + n + 1)
                    else:
                        pe.wait_ge(w_split, l * N_DVE + n - N_POOL + 1)
                    high = mixer_high[n] if isinstance(n, int) and n < MOE0 else w_high[slot % HIGHS]
                    return high[:, :, :], w_low[:, slot, :, :]

                def split_unit():
                    n = done["unit"]
                    done["unit"] += 1
                    return parts(n, n % RING)

                def exact_mm(out_, lhs, rhs, start, stop):
                    (lh, ll), (rh, rl) = lhs, rhs
                    mm(out_, lh, rh, start=start, stop=False, skip_group_check=True)
                    mm(out_, lh, rl, start=False, stop=False, skip_group_check=True)
                    return mm(out_, ll, rh, start=False, stop=stop, skip_group_check=True)

                def h_early(kk):
                    return h_high[:, kk, :], h_low[:, kk, :]

                def h_late(kk):
                    return h1_high[kk // HK][:, kk % HK, :], h_low[:, kk, :]

                def tok_project(out2, w, h, c0, n, hs, shared=False):
                    for t in range(TT):
                        for k in range(HK):
                            last = exact_mm(out2[t], [part[:, t * P:t * P + P] for part in hs(HK * h + k)],
                                            [part[:, k, c0:c0 + n] for part in w],
                                            h == 0 and k == 0 and not (shared and t), h == 1 and k == HK - 1)
                    return last

                def chan_project(b, w, h, c0, tiles, hs):
                    for m in range(tiles):
                        for k in range(HK):
                            last = exact_mm(b[:, m // 2, (m % 2) * SEQ:(m % 2) * SEQ + SEQ],
                                            [part[:, k, c0 + m * P:c0 + m * P + P] for part in w], hs(HK * h + k),
                                            h == 0 and k == 0 and m % 2 == 0, h == 1 and k == HK - 1)
                    return last

                def tok_job(name, n=W, hs=h_early):
                    b = begin("proj", name)
                    for h in range(2):
                        tok_project([b[:, t, 0:n] for t in range(TT)], split_unit(), h, 0, n, hs).then_inc(units_read, 1)

                def chan_job(name):
                    b = begin("proj", name)
                    for h in range(2):
                        chan_project(b, split_unit(), h, 0, CT, h_early).then_inc(units_read, 1)

                def modulate_transposes(norm):
                    for q in range(4):
                        b = begin("s" if q < 2 else "v", f"h{norm}_{q}")
                        for k in range(2):
                            for t in range(TT):
                                last = tr(b[:, (k * TT + t) * P:(k * TT + t + 1) * P],
                                          merged[:, t, (2 * q + k) * P:(2 * q + k + 1) * P], ident[:, :])
                        last.then_inc(s_ready if q < 2 else v_ready, 1)

                def mod_columns(name, n):
                    b = begin("v", name)
                    for i in range(2):
                        pe.wait_ge(acc_ready, l * GATE_CHUNKS + n + i + 2)
                        chunk_columns(b, 4 * i, ada_acc[:, (n + i) % 2, :]).then_inc(acc_used, 1)

                def mod_row(name, n):
                    b = begin("v", name)
                    pe.wait_ge(acc_ready, l * GATE_CHUNKS + n + 2)
                    mm(b[:, :], ones[:, :], ada_acc[:, n % 2, :], start=True, stop=True).then_inc(acc_used, 1)

                pe.wait_ge(down_used, l * NE + 1)
                b = begin("v", PCOL)
                pe.wait_ge(prow_in, (l + 1) * (8 * 16))
                tr(b[:, 0:PROWS], prow[0:PROWS, :], ident[0:PROWS, 0:PROWS])
                pe.wait_ge(sums_ready, l + 1)
                for n in range(ADA_0):
                    c0 = (MOE_CHUNKS - ADA_0 + n) * W
                    last = chunk_columns(b, PROWS + 4 * n, ada_sums[:, c0:c0 + W])
                last.then_inc(v_ready, 1)
                pe.wait_ge(xn_ready, l * 4 + 2)
                modulate_transposes(1)

                b = begin("proj", "C")
                for h in range(2):
                    pe.wait_ge(h_split, l * 2 + h + 1)
                    w = split_unit()
                    tok_project([b[:, 0, t * 256:t * 256 + 256] for t in range(TT)], w, h, 0, 256, h_early, True)
                    chan_project(b[:, 1:2, :], w, h, 256, 2, h_early).then_inc(units_read, 1)
                tok_job("B", SMALL)
                tok_job("A")

                pe.wait_ge(idx_rope, l + 1)
                b = begin("s", "qiT")
                for g in range(2):
                    for t in range(TT):
                        last = tr(b[:, (g * TT + t) * P:(g * TT + t + 1) * P],
                                  qik[:, t, 4 * g:4 * g + 4, :].rearrange("p h d -> p (h d)"), ident[:, :])
                last.then_inc(s_ready, 1)
                b = begin("s", "kiT")
                for t in range(TT):
                    last = tr(b[:, t * P:t * P + P], kirep[:, t, :, :].rearrange("p r d -> p (r d)"), ident[:, :])
                last.then_inc(s_ready, 1)
                chan_job("xbc")
                b_gv = begin("proj", "gv")
                tok_project([b_gv[:, t, :] for t in range(TT)], split_unit(), 0, 0, W, h_early).then_inc(units_read, 1)
                pe.wait_ge(s_evac, l * NSJ + S_JOBS.index("kiT") + 1 + 2)
                for t in range(TT):
                    ns = (t + 1) * P
                    for g in range(2):
                        for u in range(2):
                            b = begin("s", f"dot{t}{g}{u}")
                            mm(b[:, 0:2 * ns].rearrange("p (h s) -> p h s", h=2), qiT[:, g, t * P:t * P + P],
                               kiTd[:, 2 * u:2 * u + 2, 0:ns], start=True, stop=True).then_inc(s_ready, 1)
                pe.wait_ge(qk_roped, l + 1)
                for half in range(2):
                    b = begin("s", f"qT{half}")
                    for i in range(2):
                        for t in range(TT):
                            o = (2 * half + i) * 2
                            last = tr(b[:, (i * TT + t) * P:(i * TT + t + 1) * P],
                                      qk[:, t, o:o + 2, :].rearrange("p h d -> p (h d)"), ident[:, :])
                    last.then_inc(s_ready, 1)
                b = begin("s", "kT")
                for t in range(TT):
                    last = tr(b[:, t * P:t * P + P], qk[:, t, AH:AH + 2, :].rearrange("p h d -> p (h d)"),
                              ident[:, :])
                last.then_inc(s_ready, 1)
                tok_project([b_gv[:, t, :] for t in range(TT)], split_unit(), 1, 0, W, h_early).then_inc(units_read, 1)
                pe.wait_ge(wsraw_in, (l + 1) * 16)
                b = begin("v", "wsT")
                for g in range(GG):
                    last = tr(b[:, g * P:g * P + P], wsraw[:, g, :], ident[:, :])
                last.then_inc(v_ready, 1)
                tok_job("z")
                chan_job("gu")
                pe.wait_ge(s_evac, l * NSJ + S_JOBS.index("kT") + 1 + 2)
                for t in range(TT):
                    ns = (t + 1) * P
                    for i in range(4):
                        b = begin("v", f"lg{t}{i}")
                        mm(b[:, 0:2 * ns].rearrange("p (h s) -> p h s", h=2), qT[:, i, t * P:t * P + P],
                           kTd[:, :, 0:ns], start=True, stop=True).then_inc(v_ready, 1)
                chan_job("scc")
                pe.wait_ge(silu_ready, l + 1)
                for t in range(TT):
                    b = begin("s", f"xs{t}")
                    for m in range(CT):
                        last = tr(b[:, m * P:m * P + P], xbcT[:, m, t * P:t * P + P], ident[:, :])
                    last.then_inc(s_ready, 1)
                b = begin("s", "Bt")
                tr(b[:, 0:P], xbcT[:, 4, 0:P], ident[:, :]).then_inc(s_ready, 1)
                pe.wait_ge(p_ready, l + 1)
                for i in range(4):
                    for u in range(2):
                        hd = i + 4 * u
                        b = begin("s", f"PT{i}{'ab'[u]}")
                        tr(b[:, 0:P], P_sb[:, hd, 0:P], ident[:, :])
                        tr(b[:, P:2 * P], P_sb[:, hd, P:2 * P], ident[:, :])
                        tr(b[:, 2 * P:3 * P], P_sb[:, hd, 2 * P:3 * P], ident[:, :]).then_inc(s_ready, 1)
                    b = begin("s", f"PV{i}")
                    pe.wait_ge(s_evac, l * NSJ + S_JOBS.index(f"PT{i}b") + 1 + 2)
                    for u in range(2):
                        pt = PT[:, (i + 4 * u) * 3 * P:(i + 4 * u + 1) * 3 * P]
                        mm(b[:, u * SEQ:u * SEQ + SEQ], v_sb[:, 0, :], pt[:, 0:SEQ], start=(u == 0), stop=False,
                           skip_group_check=True)
                        last = mm(b[:, u * SEQ + P:u * SEQ + SEQ], v_sb[:, 1, :], pt[:, SEQ:3 * P], start=False,
                                  stop=True, skip_group_check=True)
                    last.then_inc(s_ready, 1)
                pe.wait_ge(dt_ready, l + 1)
                b = begin("v", "acs")
                da = dtA[:, 1, :, :].rearrange("p c h -> p (c h)")
                mm(b[:, 0:16], tri[:, :], da, start=True, stop=True)
                mm(b[:, 16:32], ones[:, :], da, start=True, stop=True).then_inc(v_ready, 1)
                def cumulative(ch):
                    pe.wait_ge(R_ready, l * 2 + ch + 1)
                    for hh in range(2):
                        b = begin("v", f"ab{ch}{hh}")
                        mm(b[:, :], ones[:, :], scratch[:, ch * 1024 + hh * W:ch * 1024 + hh * W + W],
                           start=True, stop=True).then_inc(v_ready, 1)

                def chunk_output(ch):
                    b = begin("v", f"y{ch}")
                    pe.wait_ge(M_ready, l * 2 + ch + 1)
                    for hd in range(MH):
                        last = mm(b[:, hd * MP:hd * MP + MP], M_sb[:, hd, :], xdt[:, ch, hd * MP:hd * MP + MP],
                                  start=True, stop=True)
                    last.then_inc(v_ready, 1)

                cumulative(0)
                b = begin("s", "scT")
                pe.wait_ge(CTd_ready, l + 1)
                for c2 in range(TT):
                    last = mm(b[:, c2 * 256:c2 * 256 + 256].rearrange("p (g s) -> p g s", g=2),
                              xbcT[:, 4, c2 * P:c2 * P + P], CTd[:, :, c2 * P:c2 * P + P], start=True, stop=True)
                last.then_inc(s_ready, 1)
                chan_job("scx")
                chunk_output(0)
                b = begin("s", "states")
                pe.wait_ge(ssd_in, l + 1)
                mm(b[:, :], Btok[:, :], xdtd[:, :], start=True, stop=True).then_inc(s_ready, 1)
                cumulative(1)
                chan_job("scb")
                b = begin("v", "yoff")
                pe.wait_ge(s_evac, l * NSJ + S_JOBS.index("states") + 1 + 2)
                mm(b[:, :], xbcT[:, 5, P:2 * P], prevd[:, :], start=True, stop=True).then_inc(v_ready, 1)
                chunk_output(1)
                pe.wait_ge(gv_ready, l + 1)
                for q in range(2):
                    b = begin("v", f"mix{q}")
                    for g in range(2):
                        for ch in range(TT):
                            last = mm(b[:, (g * TT + ch) * P:(g * TT + ch + 1) * P],
                                      gv[:, ch, (2 * q + g) * P:(2 * q + g + 1) * P], wsT[:, 2 * q + g, :],
                                      start=True, stop=True)
                    last.then_inc(v_ready, 1)

                for n, (i, j) in enumerate(GATE_STEPS):
                    if i == 3 and j == 0:
                        pe.wait_ge(od_ready, l + 1)
                        for q in range(2):
                            b = begin("s", f"odT{q}")
                            for m in range(2):
                                for t in range(TT):
                                    last = tr(b[:, (m * TT + t) * P:(m * TT + t + 1) * P],
                                              y_sb[:, t, (2 * q + m) * P:(2 * q + m + 1) * P], ident[:, :])
                            last.then_inc(s_ready, 1)
                    if n == 0:
                        pe.wait_ge(h_moved, l + 1)
                    tok_job(f"g{i}{j}", hs=h_late)
                    w = split_unit()
                    pe.wait_ge(o_split, l * NB + n // 2 + 1)
                    for t in range(TT):
                        b = begin("v", f"b{i}{j}{t}")
                        for k in range(CT):
                            ts = slice(t * P, t * P + P)
                            last = exact_mm(b[:, :], (o_high[:, k, ts], o_low[:, i, k, ts]),
                                            [part[:, k, :] for part in w], k == 0, k == CT - 1)
                        last.then_inc(units_read if t else v_ready, 1)
                    if n in SUM_OF_STEP:
                        name = SUM_OF_STEP[n]
                        (mod_row if name[0] == "g" else mod_columns)(name, BY_CHUNK[name] - (name[0] == "m"))
                pe.wait_ge(merged_ready, l + 1)
                for q in range(4):
                    b = begin("s", f"mT{q}")
                    for k in range(2):
                        for t in range(TT):
                            last = tr(b[:, (k * TT + t) * P:(k * TT + t + 1) * P],
                                      merged[:, t, (2 * q + k) * P:(2 * q + k + 1) * P], ident[:, :])
                    last.then_inc(s_ready, 1)
                pe.wait_ge(s_evac, l * NSJ + S_JOBS.index("mT3") + 1 + 2)
                for j in range(2):
                    b2 = [begin("v", f"o{j}{t}") for t in range(TT)]
                    for h in range(2):
                        tok_project([b[:, :] for b in b2], split_unit(), h, 0, W, h_late).then_inc(units_read, 1)

                pe.wait_ge(xn_ready, l * 4 + 4)
                modulate_transposes(2)

                pe.wait_ge(proj_evac, (l + 1) * NPJ + 2)
                pe.wait_ge(s_evac, (l + 1) * NSJ + 2)

                def h_moe(kk):
                    return h2_high[:, kk, :], h_low[:, kk, :]

                def gate_up(b0, slot, n):
                    for h in range(2):
                        w = parts(MOE0 + n + h, slot + h)
                        if isinstance(n, int) and n == 0:
                            pe.wait_ge(h2_split, l * 2 + h + 1)
                        chan_project(bank[:, b0:b0 + 2, :], w, h, 0, CT, h_moe).then_inc(units_read, 1)

                def down(slot, n, e1):
                    pe.wait_ge(hid_ready, l * NE + e1)
                    for j in range(2):
                        w = parts(MOE0 + n + j, slot + j)
                        for t in range(TT):
                            for k in range(CT):
                                last = exact_mm(bank[:, 4 + 2 * t + j, :],
                                                [part[:, k, t * P:t * P + P] for part in (hid_high, hid_low)],
                                                [part[:, k, :] for part in w], k == 0, k == CT - 1)
                        last.then_inc(units_read, 1)

                gate_up(0, 0, 0)
                b = begin("v", "router")
                pe.wait_ge(rw_split, 1)
                for t in range(TT):
                    for k in range(KD):
                        last = exact_mm(b[:, t * NE:t * NE + NE], [part[:, t * P:t * P + P] for part in h_moe(k)],
                                        (rw_high[:, k, :], rw_low[:, k, :]), k == 0, k == KD - 1)
                last.then_inc(v_ready, 1)
                if "pad" in V_JOBS:
                    begin("v", "pad")
                gate_up(2, 2, 2)
                with pe.Fori(1, NE) as e:
                    pe.wait_ge(silu_done, l * NE + e)
                    gate_up(0, 4, PER_E * e - 2)
                    pe.wait_ge(v_evac, (l + 1) * NVJ + 2)
                    pe.wait_ge(down_used, l * NE + e)
                    down(0, PER_E * e, e)
                    gate_up(2, 2, PER_E * e + 2)
                pe.wait_ge(sums_ready, l + 2)
                pe.wait_ge(silu_done, (l + 1) * NE)
                for j in range(2):
                    last = mm(bank[:, j, :], ones[:, :], ada_sums[:, j * W:j * W + W], start=True, stop=True)
                last.then_inc(gate2_ready, 1)
                pe.wait_ge(down_used, (l + 1) * NE)
                down(4, PER_E * NE - 2, NE)

        @block.scalar
        def _(act):
            A = nc.scalar.activation
            act.wait_ge(c_in, 16)
            A(cact[:, :], c_raw[:, :], ACT.Silu).then_inc(cact_ready, 1)
            act.wait_ge(rw_in, 32)
            A(rw_high[:, :, :], rw[:, :, :], ACT.Copy).then_inc(rw_rounded, 1)
            act.wait_ge(x_in, 16)
            act.wait_ge(angles_ready, 1)
            A(rope[:, :, :, :], ang[:, :, :, :], ACT.Sin).then_inc(rope_ready, 1)
            with act.Fori(0, DEPTH) as l:
                seen = {"s": 0, "proj": 0}

                def round_expert_unit(n, slot, uses):
                    act.wait_ge(slot_loaded[slot], l * (16 * SLOT_L[slot]) + 16 * (SLOT_MIX[slot] + uses))
                    act.wait_ge(units_read, l * UNITS_L + MOE0 + n - HIGHS + 1 + RING)
                    A(w_high[slot % HIGHS][:, :, :], ring[:, slot, :, :], ACT.Copy).then_inc(w_rounded, 1)

                def round_mixer(n):
                    cols = columns_of(n)
                    act.wait_ge(slot_loaded[n % RING], l * (16 * SLOT_L[n % RING]) + 16 * LANDED[n])
                    if LAST_IN[n] is not None:
                        act.wait_ge(units_read, l * UNITS_L + LAST_IN[n] + 1 + RING)
                    A(mixer_high[n][:, :, cols], ring[:, n % RING, :, cols], ACT.Copy).then_inc(w_rounded, 1)

                def round_after(name):
                    round_mixer(ROUND_AFTER[name])

                def round_branch(i):
                    A(o_high[:, :, :], oT[:, i, :, :], ACT.Copy).then_inc(o_rounded, 1)

                def job(kind, name):
                    if name in ROUND_BEFORE:
                        round_mixer(ROUND_BEFORE[name])
                    jobs = S_JOBS if kind == "s" else PROJ_JOBS
                    assert jobs[seen[kind]] == name, (name, jobs[seen[kind]])
                    seen[kind] += 1
                    if kind == "s":
                        act.wait_ge(s_ready, l * NSJ + seen[kind])
                    else:
                        act.wait_ge(units_read, l * UNITS_L + UNITS.index((name, 1)) + 1 + RING)
                    return ps(name) if kind == "s" else pj(name)

                def copy(dst, src):
                    return A(dst, src, ACT.Copy)

                def roots(norm):
                    act.wait_ge(mean_ready, l * 2 + norm)
                    A(st[:, 2, 0:TT], st[:, 1, 0:TT], ACT.Sqrt).then_inc(rs_ready, 1)
                    if norm == 1:
                        round_mixer(0)
                    act.wait_ge(rstd_ready, l * 2 + norm)
                    A(merged[:, 0, :], x_sb[:, 0, :], ACT.Copy, scale=st[:, 2, 2:3]).then_inc(xn_ready, 1)

                def modulate(norm):
                    act.wait_ge(modc_ready, l * 2 + norm)
                    for q in range(2):
                        b = job("s", f"h{norm}_{q}")
                        for k in range(2):
                            kk = 2 * q + k
                            last = A(hT[:, kk, :], b[:, k * SEQ:k * SEQ + SEQ], ACT.Identity,
                                     scale=modc[:, norm - 1, 0, kk:kk + 1], bias=modc[:, norm - 1, 1, kk:kk + 1])
                        last.then_inc(s_evac, 1)

                for t in range(TT):
                    act.wait_ge(x_tile, l * TT + t + 1)
                    last = A(merged[:, t, :], x_sb[:, t, :], ACT.Square, accum_out=st[:, 0, t:t + 1])
                last.then_inc(ss_ready, 1)
                roots(1)
                modulate(1)
                act.wait_ge(s_evac, l * NSJ + S_JOBS.index("h1_1") + 1 + 2)
                A(h_high[:, 0:HK, :], hT[:, 0:HK, :], ACT.Copy).then_inc(h_rounded, 1)
                act.wait_ge(v_evac, l * NVJ + V_JOBS.index("h1_3") + 1 + 2)
                A(h_high[:, HK:, :], hT[:, HK:, :], ACT.Copy).then_inc(h_rounded, 1)
                round_mixer(1)
                round_mixer(2)
                b = job("proj", "C")
                copy(qik[:, :, 0:IH, :], b[:, 0, :].rearrange("p (t h d) -> p t h d", t=TT, d=ID))
                copy(xbc[:, 4:6, M_K - 1:], b[:, 1, :].rearrange("p (m s) -> p m s", m=2)).then_inc(proj_evac, 1)
                round_after("C")
                b = job("proj", "B")
                o = 2 * AG * AD
                copy(qik[:, :, IH, :], b[:, :, o:o + ID])
                copy(wdt[:, :, :], b[:, :, o + ID:o + ID + IH + MH])
                copy(v_sb[:, :, :], b[:, :, AG * AD:o])
                copy(qk[:, :, AH:AH + 2, :], b[:, :, 0:AG * AD].rearrange("p t (g d) -> p t g d", g=AG)
                     ).then_inc(proj_evac, 1)
                round_after("B")
                b = job("proj", "A")
                for t in range(TT):
                    last = copy(qk[:, t, 0:AH, :].rearrange("p (i g) d -> p i g d", g=AG),
                                b[:, t, :].rearrange("p (g i d) -> p i g d", g=AG, i=4))
                last.then_inc(proj_evac, 1)
                round_after("A")
                act.wait_ge(dt_abs, l + 1)
                A(st[:, 4, 0:16], st[:, 3, 0:16], ACT.Exp, scale=-1.0).then_inc(dt_exp, 1)
                act.wait_ge(dt_exp, l + 1)
                A(st[:, 5, 0:16], st[:, 4, 0:16], ACT.Ln, bias=1.0)
                A(st[:, 7, 0:MH], mrow[:, 1, :], ACT.Exp).then_inc(dt_log, 1)
                act.wait_ge(qk_ss, l + 1)
                A(st[:, 9, 0:20], st[:, 8, 0:20], ACT.Sqrt).then_inc(qk_rs, 1)
                b = job("s", "qiT")
                copy(qiT[:, :, :], b[:, :].rearrange("p (g s) -> p g s", g=2)).then_inc(s_evac, 1)
                b = job("s", "kiT")
                for j in range(4):
                    last = copy(kiTd[32 * j:32 * j + 32, j, :], b[32 * j:32 * j + 32, 0:SEQ])
                last.then_inc(s_evac, 1)
                b = job("proj", "xbc")
                copy(xbc[:, 0:4, M_K - 1:], b[:, :, :].rearrange("p b (m s) -> p (b m) s", m=2)
                     ).then_inc(proj_evac, 1)
                round_after("xbc")
                act.wait_ge(qk_roped, l + 1)
                n = 0
                for t in range(TT):
                    ns = (t + 1) * P
                    for g in range(2):
                        for u in range(2):
                            b = job("s", f"dot{t}{g}{u}")
                            if n >= 2:
                                act.wait_ge(relu_used, l * 8 + n - 1)
                            A(scratch[:, (n % 2) * W:(n % 2) * W + 2 * ns], b[:, 0:2 * ns], ACT.Relu
                              ).then_inc(s_evac, 1)
                            n += 1
                for half in range(2):
                    b = job("s", f"qT{half}")
                    copy(qT[:, 2 * half:2 * half + 2, :], b[:, :].rearrange("p (i s) -> p i s", i=2)
                         ).then_inc(s_evac, 1)
                b = job("s", "kT")
                for g in range(AG):
                    last = copy(kTd[64 * g:64 * g + 64, g, :], b[64 * g:64 * g + 64, 0:SEQ])
                last.then_inc(s_evac, 1)
                b = job("proj", "gv")
                A(gv, b[:, :, :], ACT.Gelu).then_inc(proj_evac, 1)
                round_after("gv")
                act.wait_ge(proj_evac, l * NPJ + PROJ_JOBS.index("gv") + 1 + 2)
                act.wait_ge(relu_used, l * 8 + 8)
                for t in range(TT):
                    last = A(scratch[:, t * W:t * W + W], gv[:, t, :], ACT.Square, accum_out=st[:, 10, t:t + 1])
                last.then_inc(gv_ss, 1)
                b = job("proj", "z")
                A(z_sb, b[:, :, :], ACT.Silu).then_inc(proj_evac, 1)
                round_after("z")
                act.wait_ge(gv_mean, l + 1)
                A(st[:, 12, 0:TT], st[:, 11, 0:TT], ACT.Sqrt).then_inc(gv_rs, 1)
                b = job("proj", "gu")
                A(uT[:, :, :], b[:, :, :].rearrange("p b (m s) -> p (b m) s", m=2), ACT.Gelu).then_inc(proj_evac, 1)
                round_after("gu")
                act.wait_ge(conv_ready, l + 1)
                for m in range(6):
                    last = A(xbcT[:, m, :], xbcT[:, m, :], ACT.Silu, bias=pcol[:, PR["mcb"] + m:PR["mcb"] + m + 1])
                last.then_inc(silu_ready, 1)
                act.wait_ge(silu_ready, l + 1)
                for g in range(MG):
                    last = copy(CTd[64 * g:64 * g + 64, g, :], xbcT[64 * g:64 * g + 64, 5, :])
                last.then_inc(CTd_ready, 1)
                for t in range(TT):
                    act.wait_ge(max_ready, l * 2 + t + 1)
                    lo, hi = (0, P) if t == 0 else (P, 3 * P)
                    for hd in range(AH):
                        last = A(P_sb[:, hd, lo:hi], P_sb[:, hd, lo:hi], ACT.Exp, scale=AD ** -0.5,
                                 bias=st[:, 14 + t, hd:hd + 1], accum_out=st[:, 16 + t, hd:hd + 1])
                    last.then_inc(exp_ready, 1)
                round_mixer(SC0 + 2)
                round_mixer(SC0 + 3)
                for t in range(TT):
                    b = job("s", f"xs{t}")
                    copy(xs_tok[:, t, :], b[:, :]).then_inc(s_evac, 1)
                b = job("s", "Bt")
                copy(Btok[:, :], b[:, 0:P]).then_inc(s_evac, 1)
                for i in range(4):
                    for u in range(2):
                        hd = i + 4 * u
                        b = job("s", f"PT{i}{'ab'[u]}")
                        copy(PT[:, hd * 3 * P:(hd + 1) * 3 * P], b[:, 0:3 * P]).then_inc(s_evac, 1)
                    b = job("s", f"PV{i}")
                    for u in range(2):
                        last = copy(oT[64 * u:64 * u + 64, 0, i, :], b[64 * u:64 * u + 64, u * SEQ:u * SEQ + SEQ])
                    last.then_inc(s_evac, 1)
                b = job("proj", "scc")
                copy(scc, b[:, :, :].rearrange("p b (m s) -> p (b m) s", m=2)).then_inc(proj_evac, 1)
                act.wait_ge(acs_ready, l + 1)
                A(dtA[:, 2:4, :, :], dtA[:, 2:4, :, :], ACT.Exp).then_inc(decay_out, 1)
                b = job("s", "scT")
                copy(scT[:, :, :, :], b[:, :].rearrange("p (c g s) -> p c g s", c=2, g=2)).then_inc(s_evac, 1)
                act.wait_ge(diff_ready, l * 2 + 1)
                A(M_sb, M_sb, ACT.Exp).then_inc(dec_exp, 1)
                b = job("proj", "scx")
                copy(cx[:, :, 2:], b[:, :, :].rearrange("p b (m s) -> p (b m) s", m=2)).then_inc(proj_evac, 1)
                round_after("scx")
                b = job("s", "states")
                copy(prevd[0:64, 0:256], b[0:64, 0:256])
                copy(prevd[64:128, 256:512], b[64:128, 256:512]).then_inc(s_evac, 1)
                b = job("proj", "scb")
                copy(scb, b[:, :, :].rearrange("p b (m s) -> p (b m) s", m=2)).then_inc(proj_evac, 1)
                act.wait_ge(diff_ready, l * 2 + 2)
                A(M_sb, M_sb, ACT.Exp).then_inc(dec_exp, 1)

                act.wait_ge(M_ready, l * 2 + 1)
                round_mixer(GATE0)
                act.wait_ge(v_ready, l * NVR + V_PLAIN.index("y1") + 1)
                for h in range(2):
                    last = copy(h1_high[h][:, :, :], h_high[:, HK * h:HK * h + HK, :])
                last.then_inc(h_moved, 1)
                act.wait_ge(y_ss, l + 1)
                A(st[:, 20, 0:TT], st[:, 19, 0:TT], ACT.Sqrt).then_inc(y_rs, 1)
                round_mixer(GATE0 + 1)
                act.wait_ge(ob_ready, l + 1)
                round_branch(1)
                act.wait_ge(oc_ready, l + 1)
                round_mixer(GATE0 + 2)
                for n, (i, j) in enumerate(GATE_STEPS):
                    u = GATE0 + 3 * n
                    if i == 3 and j == 0:
                        for q in range(2):
                            b = job("s", f"odT{q}")
                            for m in range(2):
                                mt = 2 * q + m
                                last = A(oT[:, 3, mt, :], b[:, m * SEQ:m * SEQ + SEQ], ACT.Copy,
                                         scale=pcol[:, PR["mng"] + mt:PR["mng"] + mt + 1])
                            last.then_inc(s_evac, 1)
                        act.wait_ge(s_evac, l * NSJ + S_JOBS.index("odT1") + 1 + 2)
                    if j == 0 and n > 0:
                        act.wait_ge(units_read, l * UNITS_L + u + RING)
                        round_branch(i)
                    round_mixer(u + 3)
                    b = job("proj", f"g{i}{j}")
                    if n >= 2:
                        act.wait_ge(gsig_used, l * 8 + n - 1)
                    A(gsig[j], b[:, :, :], ACT.Sigmoid).then_inc(proj_evac, 1)
                    round_mixer(u + 4)
                    round_mixer(u + 5)
                for q in range(4):
                    b = job("s", f"mT{q}")
                    copy(h1_high[q // 2][:, 2 * (q % 2):2 * (q % 2) + 2, :],
                         b[:, :].rearrange("p (k s) -> p k s", k=2)).then_inc(mT_rounded, 1)
                round_mixer(MOE0 - 1)
                round_expert_unit(0, 0, 1)
                for j in range(2):
                    act.wait_ge(x_half, l * 2 + j + 1)
                    for t in range(TT):
                        last = A(y_sb[:, t, :], x_sb[:, t, j * W:j * W + W], ACT.Square,
                                 accum_out=st[:, 0, 2 * j + t:2 * j + t + 1])
                    if j == 0:
                        round_expert_unit(1, 1, 1)
                        round_expert_unit(2, 2, 1)
                last.then_inc(ss_ready, 1)
                roots(2)
                modulate(2)
                act.wait_ge(s_evac, l * NSJ + S_JOBS.index("h2_1") + 1 + 2)
                A(h2_high[:, 0:HK, :], hT[:, 0:HK, :], ACT.Copy).then_inc(h2_rounded, 1)
                act.wait_ge(v_evac, l * NVJ + V_JOBS.index("h2_3") + 1 + 2)
                A(h2_high[:, HK:, :], hT[:, HK:, :], ACT.Copy).then_inc(h2_rounded, 1)
                round_expert_unit(3, 3, 1)
                act.wait_ge(logit_ready, l + 1)
                A(rt1[:, 0, :, :], rt1[:, 0, :, :], ACT.Sigmoid).then_inc(sig_ready, 1)
                def silu_gate(read, e):
                    act.wait_ge(units_read, l * UNITS_L + MOE0 + read + RING)
                    act.wait_ge(hid_made, l * NE + e + 1)
                    A(sg.rearrange("p (b m) s -> p b (m s)", b=2), bank[:, 0:2, :], ACT.Silu).then_inc(silu_done, 1)

                def round_hidden(e):
                    act.wait_ge(hid_made, l * NE + e + 2)
                    A(hid_high[:, :, :], hid, ACT.Copy).then_inc(hid_rounded, 1)

                round_expert_unit(4, 4, 1)
                silu_gate(2, 0)
                round_expert_unit(5, 5, 1)
                with act.Fori(1, NE) as e:
                    u = PER_E * e

                    def round_expert(n):
                        round_expert_unit(u + n, n, e + 1)

                    round_expert(0)
                    round_hidden(e - 1)
                    round_expert(1)
                    round_expert(2)
                    silu_gate(u, e)
                    for n in range(3, PER_E):
                        round_expert(n)
                round_hidden(NE - 1)

        @block.vector
        def _(dve):
            V = nc.vector
            count = [0]

            def step(ins):
                count[0] += 1
                return ins.then_inc(dve_step, 1)

            def settle():
                dve.wait_ge(dve_step, count[0])

            def arrive():
                count[0] += 1
                dve.sem_inc(dve_step, 1)

            for started in (pcol_ready, layer_done, down_used, acc_ready, hid_made):
                dve.sem_inc(started, 1)
            dve.sem_inc(x_tile, TT)
            def ada_unit(acc, q, at, chain):
                dve.wait_ge(ada_loaded[q], (at + 1) * 16)
                for k in range(2):
                    w, ck = ada_place[q][:, k, :], cact[:, 2 * q + k:2 * q + k + 1]
                    if q == 0 and k == 0:
                        ins = V.tensor_scalar(acc, w, ck, None, ALU.mult)
                    else:
                        ins = V.scalar_tensor_tensor(out=acc, in0=w, scalar=ck, in1=acc, op0=ALU.mult, op1=ALU.add)
                    if k == 1:
                        ins.then_inc(ada_freed, 1)
                        dve.wait_ge(ada_freed, 4 * at + q + 1 + 4)
                    else:
                        chain(ins)

            def chain(ins):
                step(ins)
                settle()

            dve.wait_ge(cact_ready, 1)
            for n in range(ADA_0):
                c0 = (MOE_CHUNKS - ADA_0 + n) * W
                for q in range(4):
                    ada_unit(ada_sums[:, c0:c0 + W], q, n, chain)
            dve.sem_inc(sums_ready, 1)
            dve.wait_ge(rw_rounded, 1)
            V.tensor_tensor(rw_low[:, :, :], rw[:, :, :], rw_high[:, :, :], ALU.subtract).then_inc(rw_split, 1)
            dve.wait_ge(pos_in, 16)
            dve.wait_ge(consts, FILLS + 4)
            step(V.tensor_copy(pos_f[:, :], pos_i[:, :]))
            settle()
            for i in range(2):
                step(V.tensor_tensor(ang[:, i, :, :], bcast(pos_f[:, :], 2, AROT // 2),
                                     bcast(invf[:, :], 1, TT), ALU.mult))
            settle()
            round_up = 1.5 * 2.0 ** 23
            for i in range(2):
                step(V.tensor_scalar(turns[:, i, :, :], ang[:, i, :, :], 1.0 / (2 * math.pi), 0.25 * i,
                                     ALU.mult, ALU.add))
            settle()
            step(V.tensor_scalar(turns[:, :, :, :], turns[:, :, :, :], round_up, None, ALU.add))
            settle()
            step(V.tensor_scalar(turns[:, :, :, :], turns[:, :, :, :], round_up, None, ALU.subtract))
            settle()
            c1 = 6.28125
            c2 = float(np.float32(round((2 * math.pi - c1) * 2 ** 20) / 2 ** 20))
            c3 = 2 * math.pi - c1 - c2
            for part in (c1, c2, c3):
                step(V.scalar_tensor_tensor(out=ang[:, :, :, :].rearrange("p a t f -> p (a t f)"),
                                            in0=turns[:, :, :, :].rearrange("p a t f -> p (a t f)"), scalar=-part,
                                            in1=ang[:, :, :, :].rearrange("p a t f -> p (a t f)"),
                                            op0=ALU.mult, op1=ALU.add))
                settle()
            step(V.tensor_scalar(ang[:, 1, :, :], ang[:, 1, :, :], math.pi / 2, None, ALU.add))
            settle()
            V.tensor_scalar(ang[:, :, :, :], ang[:, :, :, :], 3.1415925, -3.1415925, ALU.min, ALU.max
                            ).then_inc(angles_ready, 1)

            dve.wait_ge(rope_ready, 1)
            dve.sem_clear(dve_step)
            count[0] = 0

            with dve.Fori(0, DEPTH) as l:
                seen = [0]

                def job(name):
                    assert V_JOBS[seen[0]] == name, (name, V_JOBS[seen[0]])
                    seen[0] += 1
                    if name in BY_UNIT:
                        dve.wait_ge(units_read, l * UNITS_L + BY_UNIT[name] + 1 + RING)
                    elif name in BY_CHUNK:
                        dve.wait_ge(acc_used, l * GATE_CHUNKS + BY_CHUNK[name] + 1 + 2)
                    else:
                        dve.wait_ge(v_ready, l * NVR + V_PLAIN.index(name) + 1)
                    return ps(name)

                def evacuated():
                    dve.wait_ge(v_evac, l * NVJ + seen[0] + 2)

                def split_unit(n, slot, high, cols=slice(0, W)):
                    dve.wait_ge(w_rounded, l * UNITS_L + n + 1)
                    V.tensor_tensor(w_low[:, slot, :, cols], ring[:, slot, :, cols], high[:, :, cols], ALU.subtract
                                    ).then_inc(w_split, 1)

                def split_mixer(n):
                    split_unit(n, n % RING, mixer_high[n], columns_of(n))

                def split_expert(n, slot):
                    split_unit(MOE0 + n, slot, w_high[slot % HIGHS])

                def col(name, i=0, n=1):
                    return pcol[:, PR[name] + i:PR[name] + i + n]

                def norm_scale(norm):
                    dve.wait_ge(ss_ready, l * 2 + norm)
                    if norm == 2:
                        step(V.tensor_tensor(st[:, 0, 0:TT], st[:, 0, 0:TT], st[:, 0, TT:2 * TT], ALU.add))
                        settle()
                    V.tensor_scalar(st[:, 1, 0:TT], st[:, 0, 0:TT], 1.0 / D_MODEL, EPS, ALU.mult, ALU.add
                                    ).then_inc(mean_ready, 1)
                    dve.wait_ge(rs_ready, l * 2 + norm)
                    V.reciprocal(st[:, 2, 2:2 + TT], st[:, 2, 0:TT]).then_inc(rstd_ready, 1)
                    dve.wait_ge(rstd_ready, l * 2 + norm)
                    V.tensor_scalar(merged[:, 1, :], x_sb[:, 1, :], st[:, 2, 3:4], None, ALU.mult).then_inc(xn_ready, 1)

                def mod_cols(norm):
                    a0 = (0 if norm == 1 else 3) * KD
                    step(V.tensor_tensor(modc[:, norm - 1, 1, :], mod_sum[:, norm - 1, 0:KD], col("adab", a0, KD),
                                         ALU.add))
                    step(V.tensor_tensor(modc[:, norm - 1, 0, :], mod_sum[:, norm - 1, KD:], col("adab", a0 + KD, KD),
                                         ALU.add))
                    settle()
                    V.scalar_tensor_tensor(out=modc[:, norm - 1, 0, :], in0=modc[:, norm - 1, 0, :], scalar=1.0,
                                           in1=col(f"norm{norm}", 0, KD), op0=ALU.add, op1=ALU.mult
                                           ).then_inc(modc_ready, 1)
                    dve.wait_ge(modc_ready, l * 2 + norm)

                def modulate(norm):
                    for q in range(2, 4):
                        b = job(f"h{norm}_{q}")
                        for k in range(2):
                            kk = 2 * q + k
                            last = V.tensor_scalar(hT[:, kk, :], b[:, k * SEQ:k * SEQ + SEQ],
                                                   modc[:, norm - 1, 0, kk:kk + 1], modc[:, norm - 1, 1, kk:kk + 1],
                                                   ALU.mult, ALU.add)
                        last.then_inc(v_evac, 1)

                b = job(PCOL)
                V.tensor_copy(mod_sum[:, 0, :], b[:, PROWS:PROWS + 2 * KD])
                V.tensor_copy(pcol[:, 0:PROWS], b[:, 0:PROWS]).then_inc(v_evac, 1)
                evacuated()
                dve.sem_inc(pcol_ready, 1)
                mod_cols(1)
                norm_scale(1)
                split_mixer(0)
                modulate(1)
                for h in range(2):
                    hs = slice(HK * h, HK * h + HK)
                    dve.wait_ge(h_rounded, l * 2 + h + 1)
                    V.tensor_tensor(h_low[:, hs, :], hT[:, hs, :], h_high[:, hs, :], ALU.subtract).then_inc(h_split, 1)
                split_mixer(1)
                split_mixer(2)

                def rotate(v, nh, half, freq_step, done):
                    x1, x2 = v[:, :, :, 0:half], v[:, :, :, half:2 * half]
                    sin = bcast(rope[:, 0, :, 0:AROT // 2:freq_step], 2, nh)
                    cos = bcast(rope[:, 1, :, 0:AROT // 2:freq_step], 2, nh)
                    tmp = [rt[:, i, 0:TT * nh, 0:half].rearrange("p (t h) f -> p t h f", t=TT) for i in range(4)]
                    step(V.tensor_tensor(tmp[0], x1, cos, ALU.mult))
                    step(V.tensor_tensor(tmp[1], x2, sin, ALU.mult))
                    step(V.tensor_tensor(tmp[2], x2, cos, ALU.mult))
                    step(V.tensor_tensor(tmp[3], x1, sin, ALU.mult))
                    settle()
                    step(V.tensor_tensor(x1, tmp[0], tmp[1], ALU.subtract))
                    last = V.tensor_tensor(x2, tmp[2], tmp[3], ALU.add)
                    if done is None:
                        step(last)
                        settle()
                    else:
                        last.then_inc(done, 1)

                dve.wait_ge(proj_evac, l * NPJ + 2 + 2)
                rotate(qik[:, :, :, :], IH + 1, IROT // 2, 2, None)
                V.tensor_copy(kirep[:, :, :, :], bcast(qik[:, :, IH, :], 2, 4)).then_inc(idx_rope, 1)
                dve.wait_ge(rows_in, (l + 1) * (6 * 16))
                r16 = lambda i: st[:, i, 0:16].rearrange("p (t h) -> p t h", t=TT)
                step(V.tensor_tensor(r16(6), wdt[:, :, IH:], bcast(mrow[:, 0, :], 1, TT), ALU.add))
                step(V.tensor_scalar(wdt[:, :, 0:IH], wdt[:, :, 0:IH], float(np.float32(IH ** -0.5 * ID ** -0.5)),
                                     None, ALU.mult))
                settle()
                step(V.tensor_scalar(st[:, 3, 0:16], st[:, 6, 0:16], -1.0, None, ALU.mult))
                settle()
                V.tensor_tensor(st[:, 3, 0:16], st[:, 3, 0:16], st[:, 6, 0:16], ALU.max).then_inc(dt_abs, 1)
                dve.wait_ge(proj_evac, l * NPJ + 3 + 2)
                NQ = TT * (AH + AG)
                qk2 = qk[:, :, :, :].rearrange("p t h d -> p (t h) d")
                sq = scratch[:, 0:NQ * AD].rearrange("p (h d) -> p h d", d=AD)
                step(V.tensor_tensor(sq, qk2, qk2, ALU.mult))
                settle()
                step(V.tensor_reduce(st[:, 8, 0:NQ], sq, AX_X, ALU.add))
                settle()
                V.tensor_scalar(st[:, 8, 0:NQ], st[:, 8, 0:NQ], 1.0 / AD, EPS, ALU.mult, ALU.add).then_inc(qk_ss, 1)
                dve.wait_ge(qk_rs, l + 1)
                step(V.reciprocal(st[:, 9, 0:NQ], st[:, 9, 0:NQ]))
                settle()
                step(V.tensor_tensor(qk2, qk2, bcast(st[:, 9, 0:NQ], 2, AD), ALU.mult))
                settle()
                for t in range(TT):
                    step(V.tensor_tensor(qk[:, t, 0:AH, :], qk[:, t, 0:AH, :], bcast(gain[:, 0, :], 1, AH), ALU.mult))
                    step(V.tensor_tensor(qk[:, t, AH:, :], qk[:, t, AH:, :], bcast(gain[:, 1, :], 1, AG), ALU.mult))
                settle()
                rotate(qk[:, :, :, :], AH + AG, AROT // 2, 1, qk_roped)

                spans = [score[:, 0:P], score[:, P:3 * P]]
                masks = [mask[:, 0:P], mask[:, P:3 * P]]
                causal = [future[:, P:2 * P], future[:, :]]
                n = 0
                for t in range(TT):
                    ns = (t + 1) * P
                    for g in range(2):
                        for u in range(2):
                            dve.wait_ge(s_evac, l * NSJ + S_JOBS.index(f"dot{t}{g}{u}") + 1 + 2)
                            for q in range(2):
                                hd = 4 * g + 2 * u + q
                                prev = causal[t] if hd == 0 else spans[t]
                                ins = V.scalar_tensor_tensor(
                                    out=spans[t], in0=scratch[:, (n % 2) * W + q * ns:(n % 2) * W + (q + 1) * ns],
                                    scalar=wdt[:, t, hd:hd + 1], in1=prev, op0=ALU.mult, op1=ALU.add)
                                if q == 1:
                                    ins.then_inc(relu_used, 1)
                                    dve.wait_ge(relu_used, l * 8 + n + 1)
                                else:
                                    step(ins)
                                    settle()
                            n += 1
                arrive()
                for r in range(TOPK // 8):
                    for t in range(TT):
                        step(V.max(top8[:, t, :], spans[t]))
                    settle()
                    for t in range(TT):
                        step(V.match_replace(spans[t], top8[:, t, :], spans[t], TAKEN))
                    settle()
                for t in range(TT):
                    step(V.tensor_scalar(masks[t], spans[t], TAKEN / 2, -BIG, ALU.is_gt, ALU.mult))
                settle()
                for t in range(TT):
                    step(V.tensor_tensor(masks[t], masks[t], causal[t], ALU.add))
                b = job("wsT")
                V.tensor_tensor(wsT[:, :, :], b[:, :].rearrange("p (g t) -> p g t", g=GG), bcast(tri[:, :], 1, GG),
                                ALU.mult).then_inc(v_evac, 1)
                dve.wait_ge(gv_ss, l + 1)
                V.tensor_scalar(st[:, 11, 0:TT], st[:, 10, 0:TT], 1.0 / W, EPS, ALU.mult, ALU.add).then_inc(gv_mean, 1)
                dve.wait_ge(proj_evac, l * NPJ + PROJ_JOBS.index("xbc") + 1 + 2)
                for k in range(M_K):
                    for m in range(6):
                        tap, wk = xbc[:, m, k:k + SEQ], col("mcw", k * 6 + m)
                        if k == 0:
                            step(V.tensor_scalar(xbcT[:, m, :], tap, wk, None, ALU.mult))
                        else:
                            ins = V.scalar_tensor_tensor(out=xbcT[:, m, :], in0=tap, scalar=wk, in1=xbcT[:, m, :],
                                                         op0=ALU.mult, op1=ALU.add)
                            if k == M_K - 1 and m == 5:
                                ins.then_inc(conv_ready, 1)
                            else:
                                step(ins)
                    if k < M_K - 1:
                        settle()
                dve.wait_ge(dt_log, l + 1)
                step(V.tensor_scalar(st[:, 3, 0:16], st[:, 4, 0:16], 1.0, None, ALU.add))
                settle()
                step(V.tensor_scalar(st[:, 3, 0:16], st[:, 3, 0:16], 1.0, 1e-30, ALU.subtract, ALU.max))
                settle()
                step(V.reciprocal(st[:, 3, 0:16], st[:, 3, 0:16]))
                step(V.tensor_tensor(st[:, 5, 0:16], st[:, 5, 0:16], st[:, 4, 0:16], ALU.mult))
                settle()
                step(V.tensor_tensor(st[:, 5, 0:16], st[:, 5, 0:16], st[:, 3, 0:16], ALU.mult))
                settle()
                step(V.scalar_tensor_tensor(out=dtA[:, 0, :, :].rearrange("p t h -> p (t h)"), in0=st[:, 6, 0:16],
                                            scalar=0.0, in1=st[:, 5, 0:16], op0=ALU.max, op1=ALU.add))
                step(V.tensor_scalar(st[:, 7, 0:MH], st[:, 7, 0:MH], -1.0, None, ALU.mult))
                settle()
                V.tensor_tensor(dtA[:, 1, :, :], dtA[:, 0, :, :], bcast(st[:, 7, 0:MH], 1, TT), ALU.mult
                                ).then_inc(dt_ready, 1)

                dve.wait_ge(gv_rs, l + 1)
                step(V.reciprocal(st[:, 12, 0:TT], st[:, 12, 0:TT]))
                settle()
                for t in range(TT):
                    last = V.tensor_scalar(gv[:, t, :], gv[:, t, :], st[:, 12, t:t + 1], None, ALU.mult)
                last.then_inc(gv_ready, 1)

                for t in range(TT):
                    lo, hi = (0, P) if t == 0 else (P, 3 * P)
                    for i in range(4):
                        b = job(f"lg{t}{i}")
                        settle()
                        arrive()
                        for u in range(2):
                            hd = i + 4 * u
                            ns = hi - lo
                            ins = V.tensor_tensor_reduce(P_sb[:, hd, lo:hi], b[:, u * ns:(u + 1) * ns], masks[t], 1.0,
                                                         -3e38, ALU.add, ALU.max, st[:, 13, t * 8 + hd:t * 8 + hd + 1])
                            if u == 1:
                                ins.then_inc(v_evac, 1)
                    evacuated()
                    V.tensor_scalar(st[:, 14 + t, 0:AH], st[:, 13, t * 8:t * 8 + 8], -AD ** -0.5, None, ALU.mult
                                    ).then_inc(max_ready, 1)
                for t in range(TT):
                    lo, hi = (0, P) if t == 0 else (P, 3 * P)
                    dve.wait_ge(exp_ready, l * 2 + t + 1)
                    step(V.reciprocal(st[:, 16 + t, 8:16], st[:, 16 + t, 0:8]))
                    settle()
                    for hd in range(AH):
                        last = V.tensor_scalar(P_sb[:, hd, lo:hi], P_sb[:, hd, lo:hi], st[:, 16 + t, 8 + hd:9 + hd],
                                               None, ALU.mult)
                        if t < TT - 1 or hd < AH - 1:
                            step(last)
                last.then_inc(p_ready, 1)

                b = job("acs")
                V.tensor_copy(acs[:, :, :, :].rearrange("p a c h -> p (a c h)"), b[:, 0:32]).then_inc(v_evac, 1)
                evacuated()
                step(V.tensor_tensor(dtA[:, 2, :, :], acs[:, 1, :, :], acs[:, 0, :, :], ALU.subtract))
                V.tensor_copy(dtA[:, 3, :, :], acs[:, 0, :, :]).then_inc(acs_ready, 1)
                for ch in range(TT):
                    V.tensor_tensor(scratch[:, ch * 1024:ch * 1024 + 1024].rearrange("p (h l) -> p h l", h=MH),
                                    bcast(dtA[:, 1, ch, :], 2, P), bcast(tri[:, :], 1, MH), ALU.mult
                                    ).then_inc(R_ready, 1)
                dve.wait_ge(s_evac, l * NSJ + S_JOBS.index("PV3") + 1 + 2)
                for ch in range(TT):
                    step(V.tensor_tensor(xdt[:, ch, :].rearrange("p (h q) -> p h q", h=MH),
                                         xs_tok[:, ch, :].rearrange("p (h q) -> p h q", h=MH),
                                         bcast(dtA[:, 0, ch, :], 2, MP), ALU.mult))
                settle()
                dve.wait_ge(decay_out, l + 1)
                V.tensor_tensor(xdtd[:, :].rearrange("p (h q) -> p h q", h=MH),
                                xdt[:, 0, :].rearrange("p (h q) -> p h q", h=MH),
                                bcast(dtA[:, 2, 0, :], 2, MP), ALU.mult).then_inc(ssd_in, 1)

                def decay(ch):
                    if ch:
                        dve.wait_ge(v_ready, l * NVR + V_PLAIN.index("y0") + 1)
                    for hh in range(2):
                        b = job(f"ab{ch}{hh}")
                        V.tensor_tensor(M_sb[:, 4 * hh:4 * hh + 4, :], b[:, :].rearrange("p (h l) -> p h l", h=4),
                                        bcast(acs[:, 0, ch, 4 * hh:4 * hh + 4], 2, P), ALU.subtract
                                        ).then_inc(v_evac, 1)
                    evacuated()
                    V.tensor_tensor(M_sb, M_sb, bcast(late[:, :], 1, MH), ALU.add).then_inc(diff_ready, 1)

                def weigh(ch):
                    dve.wait_ge(dec_exp, l * 2 + ch + 1)
                    dve.wait_ge(s_evac, l * NSJ + S_JOBS.index("scT") + 1 + 2)
                    for g in range(MG):
                        last = V.tensor_tensor(M_sb[:, 4 * g:4 * g + 4, :], M_sb[:, 4 * g:4 * g + 4, :],
                                               bcast(scT[:, ch, g, :], 1, 4), ALU.mult)
                        if g == 0:
                            step(last)
                    last.then_inc(M_ready, 1)

                def skip_y(ch):
                    b = job(f"y{ch}")
                    V.tensor_tensor(y_sb[:, ch, :], y_sb[:, ch, :], b[:, :], ALU.add).then_inc(v_evac, 1)
                    evacuated()

                decay(0)
                for ch in range(TT):
                    step(V.tensor_tensor(y_sb[:, ch, :].rearrange("p (h q) -> p h q", h=MH),
                                         xs_tok[:, ch, :].rearrange("p (h q) -> p h q", h=MH),
                                         bcast(mrow[:, 2, :], 2, MP), ALU.mult))
                weigh(0)
                settle()
                skip_y(0)
                decay(1)
                dve.wait_ge(proj_evac, l * NPJ + PROJ_JOBS.index("scx") + 1 + 2)
                step(V.memset(cx[:, :, 0:2], 0.0))
                step(V.tensor_tensor(cx[:, :, 2:], cx[:, :, 2:], scc, ALU.mult))
                settle()
                for k in range(SC_K):
                    for m in range(CT):
                        tap, wk = cx[:, m, k:k + SEQ], col("scw", k * CT + m)
                        if k == 0:
                            step(V.tensor_scalar(oT[:, 1, m, :], tap, wk, None, ALU.mult))
                        else:
                            step(V.scalar_tensor_tensor(out=oT[:, 1, m, :], in0=tap, scalar=wk, in1=oT[:, 1, m, :],
                                                        op0=ALU.mult, op1=ALU.add))
                    settle()
                weigh(1)
                split_mixer(GATE0)
                b = job("yoff")
                yo = scratch[:, 0:W]
                V.tensor_tensor(yo.rearrange("p (h q) -> p h q", h=MH), b[:, :].rearrange("p (h q) -> p h q", h=MH),
                                bcast(dtA[:, 3, 1, :], 2, MP), ALU.mult).then_inc(v_evac, 1)
                evacuated()
                step(V.tensor_tensor(y_sb[:, 1, :], y_sb[:, 1, :], yo, ALU.add))
                settle()
                def split_branch(n, i):
                    dve.wait_ge(o_rounded, l * NB + n + 1)
                    V.tensor_tensor(o_low[:, i, :, :], oT[:, i, :, :], o_high[:, :, :], ALU.subtract
                                    ).then_inc(o_split, 1)

                skip_y(1)
                dve.wait_ge(proj_evac, l * NPJ + PROJ_JOBS.index("z") + 1 + 2)
                step(V.tensor_tensor(y_sb, y_sb, z_sb, ALU.mult))
                settle()
                for t in range(TT):
                    step(V.tensor_tensor_reduce(scratch[:, t * W:t * W + W], y_sb[:, t, :], y_sb[:, t, :], 1.0, 0.0,
                                                ALU.mult, ALU.add, st[:, 19, 8 + t:9 + t]))
                settle()
                V.tensor_scalar(st[:, 19, 0:TT], st[:, 19, 8:8 + TT], 1.0 / W, EPS, ALU.mult, ALU.add
                                ).then_inc(y_ss, 1)
                dve.wait_ge(proj_evac, l * NPJ + PROJ_JOBS.index("scb") + 1 + 2)
                V.tensor_tensor(oT[:, 1, :, :], oT[:, 1, :, :], scb, ALU.mult).then_inc(ob_ready, 1)
                split_mixer(GATE0 + 1)
                split_branch(0, 1)
                dve.wait_ge(proj_evac, l * NPJ + PROJ_JOBS.index("gu") + 1 + 2)
                for q in range(2):
                    b = job(f"mix{q}")
                    for g in range(2):
                        m = 2 * q + g
                        last = V.scalar_tensor_tensor(
                            out=oT[:, 2, m, :].rearrange("p (c t) -> p c t", c=TT),
                            in0=b[:, g * SEQ:g * SEQ + SEQ].rearrange("p (c t) -> p c t", c=TT),
                            scalar=col("gvg", m), in1=bcast(gsb[:, m, :], 1, TT), op0=ALU.mult, op1=ALU.add)
                    last.then_inc(v_evac, 1)
                evacuated()
                V.tensor_tensor(oT[:, 2, :, :], oT[:, 2, :, :], uT[:, :, :], ALU.mult).then_inc(oc_ready, 1)
                split_mixer(GATE0 + 2)
                dve.wait_ge(y_rs, l + 1)
                step(V.reciprocal(st[:, 20, 0:TT], st[:, 20, 0:TT]))
                settle()
                for t in range(TT):
                    last = V.tensor_scalar(y_sb[:, t, :], y_sb[:, t, :], st[:, 20, t:t + 1], None, ALU.mult)
                last.then_inc(od_ready, 1)

                dve.wait_ge(gateb_in, (l + 1) * 32)

                def take_sums(name):
                    b = job(name)
                    if name[0] == "g":
                        j = int(name[5])
                        V.tensor_tensor(gate_bc[:, 0, j * W:j * W + W], gate_bc[:, 0, j * W:j * W + W], b[:, :],
                                        ALU.add).then_inc(v_evac, 1)
                    else:
                        part = {"mod67": 0, "mod89": 1}[name]
                        V.tensor_copy(mod_sum[:, 1, part * KD:part * KD + KD], b[:, 0:KD]).then_inc(v_evac, 1)

                for n, (i, j) in enumerate(GATE_STEPS):
                    if j == 0 and n > 0:
                        split_branch(n // 2, i)
                    split_mixer(GATE0 + 3 * n + 3)
                    dve.wait_ge(proj_evac, l * NPJ + PROJ_JOBS.index(f"g{i}{j}") + 1 + 2)
                    split_mixer(GATE0 + 3 * n + 4)
                    for t in range(TT):
                        b = job(f"b{i}{j}{t}")
                        part = merged[:, t, j * W:j * W + W]
                        dst = part if n < 2 else gsig[j][:, t, :]
                        V.tensor_tensor(dst, gsig[j][:, t, :], b[:, :], ALU.mult).then_inc(v_evac, 1)
                    evacuated()
                    if n < 2:
                        dve.sem_inc(gsig_used, 1)
                    else:
                        for t in range(TT):
                            part = merged[:, t, j * W:j * W + W]
                            last = V.tensor_tensor(part, part, gsig[j][:, t, :], ALU.add)
                            if t == 0:
                                step(last)
                        last.then_inc(gsig_used, 1)
                        dve.wait_ge(gsig_used, l * 8 + n + 1)
                    if n == len(GATE_STEPS) - 1:
                        dve.sem_inc(merged_ready, 1)
                    split_mixer(GATE0 + 3 * n + 5)
                    if n in SUM_OF_STEP:
                        take_sums(SUM_OF_STEP[n])
                    if n < GATE_CHUNKS:
                        dve.wait_ge(acc_used, l * GATE_CHUNKS + n + 1)
                        for q in range(4):
                            ada_unit(ada_acc[:, n % 2, :], q, ADA_0 + l * MOD_CHUNKS + n, chain)
                        dve.sem_inc(acc_ready, 1)
                evacuated()
                mod_cols(2)

                for q in range(4):
                    dve.wait_ge(mT_rounded, l * 4 + q + 1)
                    b = ps(f"mT{q}")
                    V.tensor_tensor(h_low[:, 2 * q:2 * q + 2, :], b[:, :].rearrange("p (k s) -> p k s", k=2),
                                    h1_high[q // 2][:, 2 * (q % 2):2 * (q % 2) + 2, :], ALU.subtract
                                    ).then_inc(s_evac, 1)
                split_mixer(MOE0 - 1)
                for j in range(2):
                    for t in range(TT):
                        b = job(f"o{j}{t}")
                        V.tensor_tensor(merged[:, t, j * W:j * W + W], b[:, :], gate_bc[:, 0, j * W:j * W + W],
                                        ALU.mult).then_inc(v_evac, 1)
                    evacuated()
                    half = slice(j * W, j * W + W)
                    V.tensor_tensor(x_sb[:, :, half], x_sb[:, :, half], merged[:, :, half], ALU.add
                                    ).then_inc(x_half, 1)
                    if j == 0:
                        split_expert(0, 0)
                        split_expert(1, 1)
                norm_scale(2)
                split_expert(2, 2)
                modulate(2)
                for h in range(2):
                    hs = slice(HK * h, HK * h + HK)
                    dve.wait_ge(h2_rounded, l * 2 + h + 1)
                    V.tensor_tensor(h_low[:, hs, :], hT[:, hs, :], h2_high[:, hs, :], ALU.subtract
                                    ).then_inc(h2_split, 1)
                split_expert(3, 3)

                R = lambda i: rt1[:, i, :, :]
                G = lambda i: rt1[:, i, :, :].rearrange("p t (g k) -> p t g k", g=EG)
                LG = lambda i: rt1[:, i, :, 0:EG]

                def op(out_, a, b_, o):
                    step(V.tensor_tensor(out_, a, b_, o))

                b = job("router")
                V.tensor_copy(R(0), b[:, 0:TT * NE].rearrange("p (t e) -> p t e", t=TT)).then_inc(v_evac, 1)
                if "pad" in V_JOBS:
                    seen[0] += 1
                    dve.wait_ge(v_evac, l * NVJ + NVJ - 1 + 2)
                    dve.sem_inc(v_evac, 1)
                evacuated()
                dve.sem_inc(logit_ready, 1)
                dve.wait_ge(sig_ready, l + 1)
                op(R(1), R(0), bcast(rbias[:, :], 1, TT), ALU.add)
                settle()
                op(rt1[:, 2, :, 0:2 * EG].rearrange("p t (g k) -> p t g k", g=EG), G(1)[:, :, :, 0:2], G(1)[:, :, :, 2:4],
                   ALU.max)
                op(rt1[:, 3, :, 0:2 * EG].rearrange("p t (g k) -> p t g k", g=EG), G(1)[:, :, :, 0:2], G(1)[:, :, :, 2:4],
                   ALU.min)
                settle()
                hi = rt1[:, 2, :, 0:2 * EG].rearrange("p t (g k) -> p t g k", g=EG)
                lo = rt1[:, 3, :, 0:2 * EG].rearrange("p t (g k) -> p t g k", g=EG)
                op(LG(4), hi[:, :, :, 0], hi[:, :, :, 1], ALU.max)
                op(LG(5), hi[:, :, :, 0], hi[:, :, :, 1], ALU.min)
                op(LG(6), lo[:, :, :, 0], lo[:, :, :, 1], ALU.max)
                settle()
                op(LG(5), LG(5), LG(6), ALU.max)
                settle()
                op(LG(4), LG(4), LG(5), ALU.add)
                settle()

                def first_of(val, n_, rank, tmp, dst):
                    step(V.tensor_reduce(rt1[:, tmp, :, 0], val, AX_X, ALU.max))
                    settle()
                    op(dst, val, bcast(rt1[:, tmp, :, 0], 2, n_), ALU.is_equal)
                    settle()
                    op(dst, dst, bcast(rank[:, 0:n_], 1, TT), ALU.mult)
                    settle()
                    step(V.tensor_reduce(rt1[:, tmp, :, 1], dst, AX_X, ALU.max))
                    settle()
                    op(dst, dst, bcast(rt1[:, tmp, :, 1], 2, n_), ALU.is_equal)
                    settle()

                first_of(LG(4), EG, rank, 6, LG(5))
                step(V.tensor_scalar(LG(5), LG(5), 1.0, BIG, ALU.subtract, ALU.mult))
                settle()
                op(G(2), G(1), bcast(LG(5), 3, EPG), ALU.add)
                settle()
                first_of(R(2), NE, rank, 6, R(3))
                step(V.scalar_tensor_tensor(out=R(4), in0=R(3), scalar=-2 * BIG, in1=R(2), op0=ALU.mult, op1=ALU.add))
                settle()
                first_of(R(4), NE, rank, 6, R(5))
                op(R(3), R(3), R(5), ALU.add)
                settle()
                op(R(3), R(3), R(0), ALU.mult)
                settle()
                step(V.tensor_reduce(rt1[:, 6, :, 0], R(3), AX_X, ALU.add))
                settle()
                step(V.reciprocal(rt1[:, 6, :, 1], rt1[:, 6, :, 0]))
                settle()
                op(comb[:, :, :], R(3), bcast(rt1[:, 6, :, 1], 2, NE), ALU.mult)
                settle()
                dve.sem_clear(dve_step)
                count[0] = 0

                def hidden(read, e):
                    dve.wait_ge(silu_done, l * NE + e + 1)
                    dve.wait_ge(units_read, l * UNITS_L + MOE0 + read + RING)
                    V.tensor_tensor(hid.rearrange("p (b m) s -> p b (m s)", b=2),
                                    sg.rearrange("p (b m) s -> p b (m s)", b=2), bank[:, 2:4, :], ALU.mult
                                    ).then_inc(hid_made, 1)

                def split_hidden(e):
                    dve.wait_ge(hid_rounded, l * NE + e + 1)
                    V.tensor_tensor(hid_low[:, :, :], hid, hid_high[:, :, :],
                                    ALU.subtract).then_inc(hid_ready, 1)

                moe_count = [0]

                def moe_chain(ins):
                    moe_count[0] += 1
                    ins.then_inc(moe_step, 1)
                    dve.wait_ge(moe_step, moe_count[0])

                def end_step():
                    dve.sem_inc(moe_step, 1)
                    dve.sem_clear(moe_step)
                    moe_count[0] = 0

                def add_expert(read, e):
                    moe_chain(V.tensor_copy(cw[:, :], comb[:, :, bass.ds(e, 1)].rearrange("p t o -> p (t o)")))
                    dve.wait_ge(units_read, l * UNITS_L + MOE0 + read + RING)
                    for t in range(TT):
                        o = merged[:, t, :].rearrange("p (b n) -> p b n", b=2)
                        last = V.scalar_tensor_tensor(out=o, in0=bank[:, 4 + 2 * t:6 + 2 * t, :],
                                                      scalar=cw[:, t:t + 1], in1=o, op0=ALU.mult, op1=ALU.add)
                    last.then_inc(down_used, 1)
                    dve.wait_ge(down_used, l * NE + e + 2)
                    end_step()

                def expert_step(e, ada):
                    u = PER_E * e
                    for n in range(4):
                        split_expert(u + n, n)
                        if n == 0:
                            split_hidden(e - 1)
                        if ada:
                            ada_unit(ada_sums[:, bass.ds((e - 1) * W, W)], n,
                                     ADA_0 + l * MOD_CHUNKS + GATE_CHUNKS + e - 1, moe_chain)
                    add_expert(u + 2, e - 1)
                    split_expert(u + 4, 4)
                    split_expert(u + 5, 5)
                    hidden(u + 4, e)

                moe_chain(V.memset(scratch[:, :], 0.0))
                end_step()
                split_expert(4, 4)
                split_expert(5, 5)
                hidden(4, 0)
                with dve.Fori(1, 1 + MOE_CHUNKS) as e:
                    expert_step(e, True)
                dve.sem_inc(sums_ready, 1)
                with dve.Fori(1 + MOE_CHUNKS, NE) as e:
                    expert_step(e, False)
                split_hidden(NE - 1)
                dve.wait_ge(gate2_ready, l + 1)
                step(V.tensor_tensor(gate_bc[:, 1, :], gate_bc[:, 1, :],
                                     bank[:, 0:2, :].rearrange("p b n -> p (b n)"), ALU.add))
                settle()
                for t in range(TT):
                    step(V.tensor_tensor(merged[:, t, :], merged[:, t, :], gate_bc[:, 1, :], ALU.mult))
                settle()
                step(V.tensor_tensor(x_sb[:, :, :], x_sb[:, :, :], merged, ALU.add))
                step(V.tensor_copy(cw[:, :], comb[:, :, NE - 1]))
                settle()
                dve.wait_ge(units_read, (l + 1) * UNITS_L + RING)
                for t in range(TT):
                    ins = V.scalar_tensor_tensor(
                        out=merged[:, t, :].rearrange("p (b n) -> p b n", b=2), in0=bank[:, 4 + 2 * t:6 + 2 * t, :],
                        scalar=cw[:, t:t + 1], in1=gate_bc[:, 1, :].rearrange("p (b n) -> p b n", b=2),
                        op0=ALU.mult, op1=ALU.mult)
                    if t < TT - 1:
                        step(ins)
                        settle()
                    else:
                        ins.then_inc(down_used, 1)
                        dve.wait_ge(down_used, (l + 1) * NE + 1)
                    V.tensor_tensor(x_sb[:, t, :], x_sb[:, t, :], merged[:, t, :], ALU.add).then_inc(x_tile, 1)
                dve.wait_ge(x_tile, (l + 2) * TT)
                dve.sem_inc(layer_done, 1)
                dve.wait_ge(layer_done, l + 2)
                arrive()
                dve.sem_clear(dve_step)
                count[0] = 0


_INS = ["x", "c", "positions", "ada_w", "ada_b", "norm1_g", "w_in", "q_norm_g", "k_norm_g", "sc_conv_w",
        "g_v_norm_g", "g_spatial_w", "g_spatial_b", "m_conv_w", "m_conv_b", "m_dt_bias", "m_a_log", "m_d",
        "m_norm_g", "w_branch", "w_out", "norm2_g", "router_w", "router_bias", "exp_w_gate", "exp_w_up",
        "exp_w_down"]


def kernel(**inputs):
    import concourse.bacc as bacc
    from concourse.bass_utils import run_bass_kernel_spmd

    nc = bacc.Bacc("TRN2", target_bir_lowering=False, num_devices=1)
    arrays, args = {}, []
    for name in _INS:
        a = np.ascontiguousarray(inputs[name])
        arrays[f"in_{name}"] = a
        args.append(nc.dram_tensor(f"in_{name}", a.shape, mybir.dt.from_np(a.dtype), kind="ExternalInput").ap())
    out = nc.dram_tensor("out", (1, SEQ, D_MODEL), F32, kind="ExternalOutput").ap()
    hybrid_trunk(nc, *args, out)
    r = run_bass_kernel_spmd(nc, [arrays], core_ids=[0])
    return r.results[0]["out"]
```
